# Optimizing a Trainium2 kernel written in Bass

```python
import math
import jax, jax.numpy as jnp
from jax import lax
import numpy as np

D_MODEL = 1024
BATCH = 1
SEQ = 512
DEPTH = 1
DEC_BATCH = 8
DEC_SEQ = 1
PAST_LEN = 4096
PAGE_SIZE = 128

PLE_DIM = 256
A_WIDTH = D_MODEL
A_GROUPS = 8
A_GROUP_DIM = A_WIDTH // A_GROUPS
A_CHUNK = 128
GLA_HEADS = 4
GLA_DK = D_MODEL // 2 // GLA_HEADS
GLA_DV = D_MODEL // GLA_HEADS
GLA_RANK = 16
GLA_TAU = 16.0
GLA_CHUNK = 16
PEER_HEADS = 8
PEER_NKEYS = 128
PEER_N = PEER_NKEYS * PEER_NKEYS
PEER_DKEY = 256
PEER_TOPK = 16
PEER_BLOCK = 128
DEEPNORM_ALPHA = (2.0 * DEPTH) ** 0.25
DEEPNORM_BETA = (8.0 * DEPTH) ** -0.25
LN_EPS = 1e-5
IN_SIZES = (A_WIDTH, A_WIDTH, GLA_HEADS * GLA_DK, GLA_HEADS * GLA_DK, GLA_HEADS * GLA_DV, GLA_HEADS * GLA_DV, GLA_RANK, D_MODEL, D_MODEL)
IN_COLS = sum(IN_SIZES)

kernel_name = 'hybrid_gmlp_gla_peer_decoder_step'

def _layernorm(x, g, b):
    xf = x.astype(jnp.float32)
    mu = jnp.mean(xf, axis=-1, keepdims=True)
    var = jnp.mean(jnp.square(xf - mu), axis=-1, keepdims=True)
    return ((xf - mu) * lax.rsqrt(var + LN_EPS) * g + b).astype(x.dtype)

def _chunk_spatial_gate(u, v, w_s, b_s):
    bsz, L, _ = v.shape
    c = min(L, A_CHUNK)
    n = L // c
    mask = jnp.tril(jnp.ones((c, c), dtype=bool))
    w = jnp.where(mask, w_s[:, :c, :c], 0)
    vc = v.reshape(bsz, n, c, A_GROUPS, A_GROUP_DIM)
    z = jnp.einsum('gts,bnsgd->bntgd', w, vc) + b_s[:, :c].T[:, :, None]
    return u * z.reshape(bsz, L, A_WIDTH)

def _gla_chunk(S, qkvg):
    q, k, v, g = qkvg
    c = q.shape[1]
    b = jnp.cumsum(g, axis=1)
    o_inter = jnp.einsum('bthk,bhkv->bthv', q * jnp.exp(b), S)
    mask = jnp.tril(jnp.ones((c, c), dtype=bool))[None, :, :, None, None]
    diff = b[:, :, None] - b[:, None, :]
    decay = jnp.where(mask, jnp.exp(jnp.minimum(diff, 0.0)), 0.0)
    att = jnp.einsum('bthk,bshk,btshk->bhts', q, k, decay)
    o = o_inter + jnp.einsum('bhts,bshv->bthv', att, v)
    b_last = b[:, -1]
    S_new = jnp.exp(b_last)[..., None] * S + jnp.einsum('bshk,bshv->bhkv', k * jnp.exp(b_last[:, None] - b), v)
    return S_new, o

def _gla(q, k, v, g, S0):
    bsz, L = q.shape[:2]
    c = math.gcd(L, GLA_CHUNK)
    n = L // c

    def to_chunks(t):
        return jnp.moveaxis(t.reshape(bsz, n, c, *t.shape[2:]), 1, 0)

    S_fin, o = lax.scan(_gla_chunk, S0, (to_chunks(q), to_chunks(k), to_chunks(v), to_chunks(g)))
    o = jnp.moveaxis(o, 0, 1).reshape(bsz, L, GLA_HEADS, GLA_DV)
    return o, S_fin

def _peer(x, w_q, keys, u_tab, v_tab):
    bsz, L, d = x.shape
    T = bsz * L
    blk = math.gcd(T, PEER_BLOCK)
    half = PEER_DKEY // 2
    keys_f = keys.astype(jnp.float32)

    def block(xb):
        q = (xb @ w_q).reshape(blk, PEER_HEADS, 2, half).astype(jnp.float32)
        mu = jnp.mean(q, axis=-1, keepdims=True)
        q = (q - mu) * lax.rsqrt(jnp.mean(jnp.square(q - mu), axis=-1, keepdims=True) + LN_EPS)
        s = jnp.einsum('thpd,hpnd->thpn', q, keys_f)
        s1, i1 = lax.top_k(s[:, :, 0], PEER_TOPK)
        s2, i2 = lax.top_k(s[:, :, 1], PEER_TOPK)
        cand = (s1[..., :, None] + s2[..., None, :]).reshape(blk, PEER_HEADS, PEER_TOPK * PEER_TOPK)
        sc, ci = lax.top_k(cand, PEER_TOPK)
        e1 = jnp.take_along_axis(i1, ci // PEER_TOPK, axis=-1)
        e2 = jnp.take_along_axis(i2, ci % PEER_TOPK, axis=-1)
        idx = e1 * PEER_NKEYS + e2
        gate = jax.nn.softmax(sc, axis=-1)
        h = jax.nn.gelu(jnp.einsum('thkd,td->thk', u_tab[idx], xb).astype(jnp.float32))
        w = (gate * h).astype(xb.dtype)
        return jnp.einsum('thk,thkd->td', w, v_tab[idx])

    y = lax.map(block, x.reshape(T // blk, blk, d))
    return y.reshape(bsz, L, d)

def _layer(x, p, S0, w_in, w_s, b_s, ln_v_g, ln_v_b, w_gk, b_gk, gla_norm_g, w_br_a, w_br_b, w_o,
           ln1_g, ln1_b, peer_wq, peer_keys, peer_u, peer_v, ln2_g, ln2_b, w_pe, w_pg):
    bsz, L, _ = x.shape
    proj = x @ w_in
    splits = np.cumsum(IN_SIZES)[:-1].tolist()
    ua, va, q, k, v, r, gk_low, g_a, g_b = jnp.split(proj, splits, axis=-1)
    va_n = _layernorm(jax.nn.gelu(va), ln_v_g, ln_v_b)
    y_a = _chunk_spatial_gate(jax.nn.gelu(ua), va_n, w_s, b_s)
    qf = q.reshape(bsz, L, GLA_HEADS, GLA_DK).astype(jnp.float32) * (GLA_DK ** -0.5)
    kf = k.reshape(bsz, L, GLA_HEADS, GLA_DK).astype(jnp.float32)
    vf = v.reshape(bsz, L, GLA_HEADS, GLA_DV).astype(jnp.float32)
    log_a = jax.nn.log_sigmoid((gk_low @ w_gk + b_gk).astype(jnp.float32)).reshape(bsz, L, GLA_HEADS, GLA_DK) / GLA_TAU
    o, S_new = _gla(qf, kf, vf, log_a, S0.astype(jnp.float32))
    o = o * lax.rsqrt(jnp.mean(jnp.square(o), axis=-1, keepdims=True) + LN_EPS) * gla_norm_g.astype(jnp.float32)
    y_b = jax.nn.silu(r) * o.reshape(bsz, L, GLA_HEADS * GLA_DV).astype(x.dtype)
    m = jax.nn.sigmoid(g_a) * (y_a @ w_br_a) + jax.nn.sigmoid(g_b) * (y_b @ w_br_b)
    x1 = _layernorm(DEEPNORM_ALPHA * x + m @ w_o, ln1_g, ln1_b)
    x2 = _layernorm(DEEPNORM_ALPHA * x1 + _peer(x1, peer_wq, peer_keys, peer_u, peer_v), ln2_g, ln2_b)
    x3 = x2 + (p @ w_pe) * jax.nn.sigmoid(x2 @ w_pg)
    c = min(L, A_CHUNK)
    return x3, S_new, va_n[:, L - c:]

def setup_inputs(seed: int = 0) -> dict:
    key = jax.random.key(seed)
    ks = jax.random.split(key, 32)

    def nrm(k, shape, scale):
        return jax.random.normal(k, shape, jnp.float32) * scale

    return {
        'x_prompt': nrm(ks[0], (BATCH, SEQ, D_MODEL), 1.0),
        'x_sample': nrm(ks[1], (DEC_BATCH, DEC_SEQ, D_MODEL), 1.0),
        'state_gla': nrm(ks[2], (DEPTH, DEC_BATCH, GLA_HEADS, GLA_DK, GLA_DV), 0.5),
        'p_prompt': nrm(ks[3], (DEPTH, BATCH, SEQ, PLE_DIM), 1.0),
        'p_sample': nrm(ks[4], (DEPTH, DEC_BATCH, DEC_SEQ, PLE_DIM), 1.0),
        'w_in': nrm(ks[5], (DEPTH, D_MODEL, IN_COLS), D_MODEL ** -0.5),
        'w_s': nrm(ks[6], (DEPTH, A_GROUPS, A_CHUNK, A_CHUNK), A_CHUNK ** -0.5),
        'b_s': 1.0 + nrm(ks[7], (DEPTH, A_GROUPS, A_CHUNK), 0.1),
        'ln_v_g': 1.0 + nrm(ks[8], (DEPTH, A_WIDTH), 0.05),
        'ln_v_b': nrm(ks[9], (DEPTH, A_WIDTH), 0.02),
        'w_gk': nrm(ks[10], (DEPTH, GLA_RANK, GLA_HEADS * GLA_DK), GLA_RANK ** -0.5),
        'b_gk': nrm(ks[11], (DEPTH, GLA_HEADS * GLA_DK), 0.1),
        'gla_norm_g': 1.0 + nrm(ks[12], (DEPTH, GLA_DV), 0.05),
        'w_br_a': nrm(ks[13], (DEPTH, A_WIDTH, D_MODEL), A_WIDTH ** -0.5),
        'w_br_b': nrm(ks[14], (DEPTH, GLA_HEADS * GLA_DV, D_MODEL), (GLA_HEADS * GLA_DV) ** -0.5),
        'w_o': nrm(ks[15], (DEPTH, D_MODEL, D_MODEL), DEEPNORM_BETA * D_MODEL ** -0.5),
        'ln1_g': 1.0 + nrm(ks[16], (DEPTH, D_MODEL), 0.05),
        'ln1_b': nrm(ks[17], (DEPTH, D_MODEL), 0.02),
        'peer_wq': nrm(ks[18], (DEPTH, D_MODEL, PEER_HEADS * PEER_DKEY), D_MODEL ** -0.5),
        'peer_keys': nrm(ks[19], (DEPTH, PEER_HEADS, 2, PEER_NKEYS, PEER_DKEY // 2), (PEER_DKEY // 2) ** -0.5),
        'peer_u': nrm(ks[20], (DEPTH, PEER_N, D_MODEL), D_MODEL ** -0.5),
        'peer_v': nrm(ks[21], (DEPTH, PEER_N, D_MODEL), DEEPNORM_BETA),
        'ln2_g': 1.0 + nrm(ks[22], (DEPTH, D_MODEL), 0.05),
        'ln2_b': nrm(ks[23], (DEPTH, D_MODEL), 0.02),
        'w_pe': nrm(ks[24], (DEPTH, PLE_DIM, D_MODEL), PLE_DIM ** -0.5),
        'w_pg': nrm(ks[25], (DEPTH, D_MODEL, D_MODEL), D_MODEL ** -0.5),
    }

def reference(x_prompt, x_sample, state_gla, p_prompt, p_sample, w_in, w_s, b_s, ln_v_g, ln_v_b, w_gk, b_gk,
              gla_norm_g, w_br_a, w_br_b, w_o, ln1_g, ln1_b, peer_wq, peer_keys, peer_u, peer_v, ln2_g, ln2_b,
              w_pe, w_pg):
    yp, ys = x_prompt, x_sample
    gla_p, gla_s, cv_p, cv_s = [], [], [], []
    for i in range(DEPTH):
        params = (w_in[i], w_s[i], b_s[i], ln_v_g[i], ln_v_b[i], w_gk[i], b_gk[i], gla_norm_g[i], w_br_a[i],
                  w_br_b[i], w_o[i], ln1_g[i], ln1_b[i], peer_wq[i], peer_keys[i], peer_u[i], peer_v[i],
                  ln2_g[i], ln2_b[i], w_pe[i], w_pg[i])
        s0_prompt = jnp.zeros((x_prompt.shape[0], GLA_HEADS, GLA_DK, GLA_DV), jnp.float32)
        yp, sp, vp = _layer(yp, p_prompt[i], s0_prompt, *params)
        ys, ss, vs = _layer(ys, p_sample[i], state_gla[i], *params)
        gla_p.append(sp)
        gla_s.append(ss)
        cv_p.append(vp)
        cv_s.append(vs)
    return (yp, ys, jnp.stack(gla_p), jnp.stack(gla_s), jnp.stack(cv_p), jnp.stack(cv_s))


_drawn_inputs = setup_inputs


def setup_inputs(seed=0):
    import zlib

    import numpy as np

    out = dict(_drawn_inputs(seed))
    spreads = {}
    factors = {'ln_v_b': 2.857, 'ln2_b': 3.224}
    for name, (base, spread) in spreads.items():
        noise = np.random.default_rng([zlib.crc32(name.encode()), seed]).standard_normal(out[name].shape)
        drawn = base * np.exp(spread * noise) if base else spread * noise
        out[name] = __import__('jax').numpy.asarray(drawn.astype(out[name].dtype))
    for name, factor in factors.items():
        out[name] = (out[name] * factor).astype(out[name].dtype)
    return out
```

```python
import math
from contextlib import ExitStack

import concourse.bass as bass
from concourse import mybir

F32 = mybir.dt.float32
U32 = mybir.dt.uint32
ALU = mybir.AluOpType
ACT = mybir.ActivationFunctionType
AX = mybir.AxisListType

D = 1024
T, S = 512, 8
N = T + S
NT = T // 128
HALF = N // 2
KC = D // 128
G = 8
H, DK, DV, RANK = 4, 128, 256, 16
PH, NK, TOPK = 8, 128, 16
SLOTS = PH * TOPK
EPS = 1e-5
ALPHA = 2.0 ** 0.25
TAU = 16.0
NEG = -3.0e38

BLOCKS = ["q0", "k0", "v0", "v1", "va0", "va1", "ua0", "ua1", "r0", "r1",
          "ga0", "ga1", "gb0", "gb1", "bra0", "bra1", "brb0", "brb1"]
RING = 3
UB, VB, DB = 4, 6, 4
ITERS = NT * PH


def rows(j):
    return 128 if j < NT else S


def cols(j):
    return slice(128 * j, 128 * j + rows(j))


def jobs():
    out = [(None, "low", 0)]
    for i, b in enumerate(BLOCKS):
        if b[:-1] in ("v", "va"):
            out += [(i, "natural", j) for j in range(NT + 1)]
        else:
            out += [(i, "columns", c) for c in range(4)]
        if b == "q0":
            out += [(None, "decay", h) for h in range(H)]
    return out


JOBS = jobs()


def done_with(name):
    return max(n for n, (b, _, _) in enumerate(JOBS) if b == BLOCKS.index(name)) + 1


BEFORE_GATES = done_with("r1")
BEFORE_BRANCH = done_with("gb1")


def decoder_step(nc, x_all, x_t, state, p_t, w_blk, w_gkl, w_gk, b_gk, ws_t, ws0, b_s, lnv_g, lnv_b, gn_g,
                 w_o, ln1_g, ln1_b, w_q, keys_t, u_tab, v_tab, ln2_g, ln2_b, w_pe, w_pg,
                 y_all, st_p, st_s, cv_p, cv_s):
    with ExitStack() as ctx:
        def sem(name):
            return ctx.enter_context(nc.semaphore(name))

        def tensor(name, shape, dt=F32):
            return ctx.enter_context(nc.sbuf_tensor(name, shape, dt))

        WORDS = 51968
        arena = tensor("arena", [128, WORDS])

        def at(off, *shape):
            n = math.prod(shape)
            assert off + n <= WORDS, (off, n)
            v = arena[:, off:off + n]
            if len(shape) == 2:
                v = v.rearrange("p (a b) -> p a b", a=shape[0])
            if len(shape) == 3:
                v = v.rearrange("p (a b c) -> p a b c", a=shape[0], b=shape[1])
            return v

        BW, TW = KC * 512, KC * N
        O_ACT = RING * BW
        O_V = O_ACT + 4 * TW
        O_TMP = O_V + 2 * (NT + 1) * D
        ring = [at(BW * i, KC, 512) for i in range(RING)]
        xT, uaT, qkT, rT = (at(O_ACT + TW * i, KC, N) for i in range(4))
        vN = at(O_V, NT + 1, D)
        vaN = at(O_V + (NT + 1) * D, NT + 1, D)
        gaT, gbT = at(O_V, KC, N), at(O_V + TW, KC, N)

        place = [O_TMP]

        def take(*shape):
            v = at(place[0], *shape)
            place[0] += math.prod(shape)
            return v

        logT = take(H, N)
        wsT = take(G, 128)
        S0 = [take(S, DV), take(S, DV)]
        lnvg, lnvb = S0[1][:, 0:4, :].rearrange("p a b -> p (a b)"), S0[1][:, 4:8, :].rearrange("p a b -> p (a b)")
        Sst = take(H, DV)
        attS, knat = take(H, 128), take(H, 128)
        Ep, Em = take(H, 128), take(H, 128)
        oN = at(place[0] - 2 * H * 128, H, DV)
        mask, ones = take(128), take(128)
        thin = take(N + H * DK)
        gkl, wgk = thin[0:RANK, 0:N], thin[0:RANK, N:N + H * DK]
        bsrow = thin[0:1, 0:G * 128]
        kpad = take(S, 128)
        dg = kpad[0:S, 0, 0:G * S].rearrange("p (a b) -> p a b", a=G)
        bs0 = kpad[0:1, 1, 0:G * S].rearrange("p (a b) -> p a b", a=G)
        qpad = take(S, S)
        wgkl = take(KC, RANK)
        wq = [at(O_ACT + TW * i, KC, 512) for i in range(4)]
        x1T = [at(2 * BW + D * i, KC, 128) for i in range(2)]
        keysT = at(2 * BW + 2 * D, 2 * PH, NK)
        ln2g, ln2b, wpe = at(O_V, D), at(O_V + D, D), at(O_V + 2 * D, 2, D)
        x1 = at(O_V + TW, NT + 1, D)
        o = O_V + TW + (NT + 1) * D
        qN, qT, pT = at(o, 2, NK), at(o + 256, 2, 128), at(o + 512, 2, 128)
        assert o + 768 <= O_TMP
        ubuf = [at(O_TMP + D * i, D) for i in range(UB)]
        vbuf = [at(O_TMP + D * (UB + i), D) for i in range(VB)]
        ln1g, ln1b = vbuf[VB - 2], vbuf[VB - 1]
        place[0] = O_TMP + D * (UB + VB)
        sg = take(D)
        scores, scoresR = take(2, NK), take(2, NK)
        onehot = at(place[0] - 512, 2, TOPK, TOPK)
        cand, candR = take(TOPK * TOPK), take(TOPK * TOPK)
        idxf = cand[0:S, 0:SLOTS]
        diag = [take(128) for _ in range(DB)]

        ident = tensor("ident", [128, 128])
        idx = [tensor(f"idx{i}", [128, SLOTS], U32) for i in range(2)]
        gates = [tensor(f"gates{i}", [128, SLOTS]) for i in range(2)]
        vals, e12 = (tensor(n, [128, 2, TOPK]) for n in ("vals", "e12"))
        abf = vals
        inds, abu = (tensor(n, [128, 2, TOPK], U32) for n in ("inds", "abu"))
        indf = tensor("indf", [128, 2, TOPK])
        top, ex, iota16 = (tensor(n, [128, TOPK]) for n in ("top", "ex", "iota16"))
        topi = tensor("topi", [128, TOPK], U32)
        iotau = tensor("iotau", [128, TOPK], U32)
        hraw, hact, wgt = (tensor(n, [128, 2, TOPK]) for n in ("hraw", "hact", "wgt"))
        bn, mv = tensor("bn", [128, 2, 6]), tensor("mv", [128, 2, 2])
        sd, rstd = tensor("sd", [128, 4]), tensor("rstd", [128, 4])
        soft = tensor("soft", [128, 3])
        ss = tensor("ss", [128, H])
        bgk, gng = tensor("bgk", [128, H]), tensor("gng", [128, 2])
        mid = tensor("mid", [128, NT, 2, H])
        fac = tensor("fac", [128, NT, H])
        egT = tensor("egT", [128, H, S])
        w00 = tensor("w00", [S, G])
        idxT = tensor("idxT", [SLOTS, S], U32)
        gateT, hS, aS = (tensor(n, [SLOTS, S]) for n in ("gateT", "hS", "aS"))
        wpad = tensor("wpad", [SLOTS, S, S])

        PJ = ctx.enter_context(nc.psum_tensor("PJ", [128, 2, 2, 512], F32))
        X = [ctx.enter_context(nc.psum_tensor(f"X{i}", [128, 1024], F32)) for i in range(2)]
        Y = PJ[:, 0, :, :]
        W = PJ[:, 1, :, :]
        RQ, RT = X[1][:, 0:512], X[1][:, 512:1024]

        xt_in, small_in, row_in, cvx, x_in = (sem(n) for n in ("xt_in", "small_in", "row_in", "cvx", "x_in"))
        blk_in = [sem(f"blk_in{i}") for i in range(RING)]
        const_ok, cst_v = sem("const_ok"), sem("cst_v")
        pj_done, pj_act, pj_dve = sem("pj_done"), sem("pj_act"), sem("pj_dve")
        act_chain, dve_chain, pool_chain = sem("act_chain"), sem("dve_chain"), sem("pool_chain")
        soft_part, log_ok, mid_ok, e_ok, qk_ok = (sem(n) for n in ("soft_part", "log_ok", "mid_ok", "e_ok", "qk_ok"))
        var_ok, sd_ok, vn_ok = sem("var_ok"), sem("sd_ok"), sem("vn_ok")
        z_done, ya_ok = sem("z_done"), sem("ya_ok")
        att_done, att_ok, knat_ok, o_done, kv_done, s_ok = (sem(n) for n in (
            "att_done", "att_ok", "knat_ok", "o_done", "kv_done", "s_ok"))
        ss_ok, orms_ok, on_ok, ot_done, yb_ok = (sem(n) for n in ("ss_ok", "orms_ok", "on_ok", "ot_done", "yb_ok"))
        s0_in = [sem("s0_in0"), sem("s0_in1")]
        kpad_ok, outer_done, s0_new, os_done = (sem(n) for n in ("kpad_ok", "outer_done", "s0_new", "os_done"))
        cv_out, stp_out = sem("cv_out"), sem("stp_out")
        s0_out = [sem("s0_out0"), sem("s0_out1")]
        wo_in, ln1_in, keys_in, wpg_in, wpe_in, ln2_in = (sem(n) for n in (
            "wo_in", "ln1_in", "keys_in", "wpg_in", "wpe_in", "ln2_in"))
        xr_in = [sem(f"xr_in{j}") for j in range(NT + 1)]
        wq_in = [sem(f"wq_in{i}") for i in range(4)]
        pt_in = sem("pt_in")
        w_done, x1_ok, tr_done, x1t_ok = (sem(n) for n in ("w_done", "x1_ok", "tr_done", "x1t_ok"))
        q_done, qn_ok, qt_done, qt_ok, s_done, route_ok, exp_in, exp_ok = (sem(n) for n in (
            "q_done", "qn_ok", "qt_done", "qt_ok", "s_done", "route_ok", "exp_in", "exp_ok"))
        u_in = [sem(f"u_in{i}") for i in range(UB)]
        v_in = [sem(f"v_in{i}") for i in range(VB)]
        u_used, h_ok, w_ok, diag_ok, v_used, y_done = (sem(n) for n in (
            "u_used", "h_ok", "w_ok", "diag_ok", "v_used", "y_done"))
        y_read, x2_ok, x2t_ok, g_done, g_ok, pe_done, x3_ok = (sem(n) for n in (
            "y_read", "x2_ok", "x2t_ok", "g_done", "g_ok", "pe_done", "x3_ok"))
        it_done, it_ok = sem("it_done"), sem("it_ok")
        xb_done, hs_ok, wpad_ok = sem("xb_done"), sem("hs_ok"), sem("wpad_ok")
        y_out = sem("y_out")

        block = ctx.enter_context(nc.Block())

        def expert_steps():
            return range(ITERS)

        WIDE = {}
        for j in range(NT + 1):
            WIDE["wo", j] = len(WIDE)
        for j in range(NT + 1):
            WIDE["pg", j] = len(WIDE)
            WIDE["pe", j] = len(WIDE)
        order = [("x1", 0), ("x1", 1)]
        for j in range(1, NT):
            order += [("x1", j + 1), ("x2", j - 1)]
        order += [("x2", NT - 1), ("x2", NT)]
        TURN = {k: n for n, k in enumerate(order)}

        def sdn(what, j, h=0):
            return SD_ORDER.index((what, j, h))

        SD_ORDER = [("va", j, 0) for j in range(NT + 1)] + [("o", j, 0) for j in range(NT + 1)]
        SD_ORDER += [("x1", j, 0) for j in range(NT + 1)] + [("q", 0, h) for h in range(PH)]
        for j in range(NT):
            for h in range(PH):
                if h == 1 and j > 0:
                    SD_ORDER.append(("x2", j - 1, 0))
                SD_ORDER.append(("q", j + 1, h))
        SD_ORDER += [("x2", NT - 1, 0), ("x2", NT, 0)]

        @block.sync
        def _(sp):
            sp.dma_start(wgkl, w_gkl).then_inc(small_in, 16)
            sp.dma_start(xT, x_t).then_inc(xt_in, 16)
            sp.dma_start(wgk, w_gk).then_inc(small_in, 16)
            sp.dma_start(bgk[:, :], b_gk).then_inc(small_in, 16)

            def load_block(i):
                if i >= RING:
                    sp.wait_ge(pj_done, done_with(BLOCKS[i - RING]))
                sp.dma_start(ring[i % RING], w_blk[i]).then_inc(blk_in[i % RING], 16)

            for i in range(RING):
                load_block(i)
            sp.dma_start(wsT, ws_t).then_inc(row_in, 16)
            sp.dma_start(lnvg, lnv_g.partition_broadcast(128)).then_inc(row_in, 16)
            sp.dma_start(lnvb, lnv_b.partition_broadcast(128)).then_inc(row_in, 16)
            sp.dma_start(w00[:, :], ws0.partition_broadcast(S)).then_inc(row_in, 16)
            sp.dma_start(gng[:, :], gn_g).then_inc(row_in, 16)
            for i in range(RING, BLOCKS.index("ga0") + RING):
                load_block(i)
                if i == RING + 1:
                    sp.dma_start(bsrow, b_s).then_inc(row_in, 16)
                if i == RING:
                    sp.dma_start(S0[0], state[0]).then_inc(s0_in[0], 16)
            sp.wait_ge(vn_ok, NT + 1)
            sp.dma_start(cv_p, vaN[:, NT - 1, :]).then_inc(cv_out, 16)
            sp.dma_start(cv_s, vaN[0:S, NT, :]).then_inc(cv_out, 16)
            sp.dma_start(S0[1], state[1]).then_inc(s0_in[1], 16)
            sp.wait_ge(s_ok, NT)
            sp.dma_start(st_p, Sst).then_inc(stp_out, 16)
            for h in range(H):
                sp.wait_ge(s0_new, 8 * (h + 1))
                sp.wait_ge(os_done, h + 1)
                sp.dma_start(st_s[h], S0[h % 2]).then_inc(s0_out[h % 2], 16)
                if h + 2 < H:
                    sp.wait_ge(s0_out[h % 2], 16)
                    sp.dma_start(S0[h % 2], state[h + 2]).then_inc(s0_in[h % 2], 16)
            for i in range(BLOCKS.index("ga0") + RING, len(BLOCKS)):
                load_block(i)
            sp.wait_ge(pj_done, BEFORE_BRANCH)
            sp.wait_ge(yb_ok, NT + 1)
            sp.dma_start(wq[0], w_q[0]).then_inc(wq_in[0], 16)
            sp.dma_start(wq[2], w_q[2]).then_inc(wq_in[2], 16)
            sp.wait_ge(stp_out, 16)
            for i in range(2):
                sp.wait_ge(s0_out[i], 32)
            sp.dma_start(ln1g, ln1_g.partition_broadcast(128)).then_inc(ln1_in, 16)
            sp.dma_start(ln1b, ln1_b.partition_broadcast(128)).then_inc(ln1_in, 16)
            for i in range(2):
                sp.wait_ge(pj_done, done_with(BLOCKS[len(BLOCKS) - RING + i]))
                sp.dma_start(ring[i], w_o[i]).then_inc(wo_in, 16)
                if i == 0:
                    sp.dma_start(wq[1], w_q[1]).then_inc(wq_in[1], 16)
            sp.wait_ge(pj_dve, len(JOBS) - BEFORE_BRANCH)
            for j in range(NT + 1):
                sp.dma_start(x1[0:rows(j), j, :], x_all[cols(j), :]).then_inc(xr_in[j], 16)
            sp.dma_start(keysT, keys_t).then_inc(keys_in, 16)
            sp.dma_start(wq[3], w_q[3]).then_inc(wq_in[3], 16)
            sp.wait_ge(w_done, NT + 1)
            for i in range(2):
                sp.dma_start(ring[i], w_pg[i]).then_inc(wpg_in, 16)
            sp.dma_start(wpe, w_pe).then_inc(wpe_in, 16)
            sp.dma_start(ln2g, ln2_g.partition_broadcast(128)).then_inc(ln2_in, 16)
            sp.dma_start(ln2b, ln2_b.partition_broadcast(128)).then_inc(ln2_in, 16)
            for j in range(NT + 1):
                if j:
                    sp.wait_ge(w_done, WIDE["pe", j - 1] + 1)
                sp.dma_start(pT[:, :, 0:rows(j)], p_t[:, :, cols(j)]).then_inc(pt_in, 16)
                sp.wait_ge(x3_ok, j + 1)
                sp.dma_start(y_all[cols(j), :], x1[0:rows(j), j, :]).then_inc(y_out, 16)
            sp.wait_ge(cv_out, 32)
            sp.wait_ge(y_out, 16 * (NT + 1))

        @block.gpsimd
        def _(pool):
            pool.memset(ident[:, :], 0.0).then_inc(pool_chain, 1)
            pool.memset(mask, 1.0).then_inc(pool_chain, 1)
            pool.memset(ones, 1.0).then_inc(const_ok, 1)
            pool.memset(qpad, 0.0).then_inc(const_ok, 1)
            pool.memset(wpad[:, :, :], 0.0).then_inc(const_ok, 1)
            pool.iota(iotau[:, :], pattern=[[1, TOPK]], base=0, channel_multiplier=0).then_inc(pool_chain, 1)
            pool.wait_ge(pool_chain, 3)
            pool.tensor_copy(iota16[:, :], iotau[:, :]).then_inc(const_ok, 1)
            pool.affine_select(out=ident[:, :], in_=ident[:, :], compare_op=ALU.not_equal, fill=1.0, base=0,
                               pattern=[[-1, 128]], channel_multiplier=1).then_inc(const_ok, 1)
            pool.affine_select(out=mask, in_=mask, compare_op=ALU.is_ge, fill=0.0, base=0,
                               pattern=[[1, 128]], channel_multiplier=-1).then_inc(const_ok, 1)

            def gather_u(n, k):
                m = n * TOPK + k
                if m >= UB:
                    pool.wait_ge(u_used, m - UB + 1)
                pool.indirect_dma_start(ubuf[m % UB], None, u_tab, bass.IndirectOffsetOnAxis(
                    idx[(n // PH) % 2][:, m % SLOTS:m % SLOTS + 1], 0)).then_inc(u_in[m % UB], 16)

            def gather_v(n, k):
                m = n * TOPK + k
                if m >= VB:
                    pool.wait_ge(v_used, m - VB + 1)
                pool.indirect_dma_start(vbuf[m % VB], None, v_tab, bass.IndirectOffsetOnAxis(
                    idx[(n // PH) % 2][:, m % SLOTS:m % SLOTS + 1], 0)).then_inc(v_in[m % VB], 16)

            pool.wait_ge(x1_ok, NT + 1)
            pool.wait_ge(route_ok, 1)
            for k in range(TOPK):
                gather_u(0, k)
            for n in expert_steps():
                if n + 1 < ITERS:
                    pool.wait_ge(route_ok, n + 2)
                for k in range(TOPK):
                    if n + 1 < ITERS:
                        gather_u(n + 1, k)
                    gather_v(n, k)
            pool.wait_ge(it_ok, 2)
            for b in range(S):
                m = ITERS * TOPK + b
                pool.wait_ge(u_used, m - UB + 1)
                pool.indirect_dma_start(ubuf[m % UB], None, u_tab, bass.IndirectOffsetOnAxis(
                    idxT[:, b:b + 1], 0)).then_inc(u_in[m % UB], 16)
            for b in range(S):
                m = ITERS * TOPK + b
                pool.wait_ge(v_used, m - VB + 1)
                pool.indirect_dma_start(vbuf[m % VB], None, v_tab, bass.IndirectOffsetOnAxis(
                    idxT[:, b:b + 1], 0)).then_inc(v_in[m % VB], 16)

        @block.scalar
        def _(act):
            chain = [0]

            def link(ins):
                chain[0] += 1
                ins.then_inc(act_chain, 1)
                act.wait_ge(act_chain, chain[0])

            def deviation(what, j, p, n, src, scale, h=0):
                i = sdn(what, j, h)
                act.wait_ge(var_ok, i + 1)
                act.activation(sd[0:p, 0:n], src, ACT.Sqrt, scale=scale).then_inc(sd_ok, 1)

            evac = [0]
            dest = {"q": (qkT, 0), "k": (qkT, 4), "ua": (uaT, 0), "r": (rT, 0), "ga": (gaT, 0), "gb": (gbT, 0)}
            func = {"q": ACT.Copy, "k": ACT.Copy, "ua": ACT.Gelu_apprx_tanh, "r": ACT.Silu,
                    "ga": ACT.Sigmoid, "gb": ACT.Sigmoid, "v": ACT.Copy, "va": ACT.Gelu_apprx_tanh}

            def evacuate(n):
                blk, kind, part = JOBS[n]
                act.wait_ge(pj_done, n + 1)
                half = PJ[:, n % 2, :, 0:HALF]
                if kind == "low":
                    act.activation(gkl.rearrange("p (a b) -> p a b", a=2), half[0:RANK], ACT.Copy).then_inc(pj_act, 1)
                elif kind == "decay":
                    act.activation(logT[:, part, :].rearrange("p (a b) -> p a b", a=2), half, ACT.Identity,
                                   bias=bgk[:, part:part + 1]).then_inc(pj_act, 1)
                elif kind == "columns":
                    name = BLOCKS[blk]
                    t, c0 = dest[name[:-1]]
                    c = c0 + 4 * int(name[-1]) + part
                    act.activation(t[:, c, :].rearrange("p (a b) -> p a b", a=2), half, func[name[:-1]],
                                   scale=DK ** -0.5 if name[:-1] == "q" else 1.0).then_inc(pj_act, 1)
                else:
                    name = BLOCKS[blk]
                    t = vN if name[:-1] == "v" else vaN
                    c = 512 * int(name[-1])
                    p = rows(part)
                    act.activation(t[0:p, part, c:c + 512], PJ[0:p, n % 2, 0, :], func[name[:-1]]).then_inc(pj_act, 1)

            def soft_logs():
                act.wait_ge(pj_act, n_log)
                tmp = rT[:, 0:H, :]
                link(act.activation(tmp, logT, ACT.Abs))
                link(act.activation(tmp, tmp, ACT.Exp, scale=-1.0))
                act.activation(tmp, tmp, ACT.Ln, bias=1.0).then_inc(soft_part, 1)

            def decays():
                for j in range(NT):
                    act.wait_ge(mid_ok, j + 1)
                    if j:
                        act.wait_ge(qk_ok, j)
                    for h in range(H):
                        act.activation(Ep[:, h, :], logT[:, h, cols(j)], ACT.Exp, scale=1.0 / TAU,
                                       bias=mid[:, j, 0, h:h + 1])
                        last = act.activation(Em[:, h, :], logT[:, h, cols(j)], ACT.Exp, scale=-1.0 / TAU,
                                              bias=mid[:, j, 1, h:h + 1])
                    last.then_inc(e_ok, 1)
                act.wait_ge(mid_ok, NT + 1)
                link(act.activation(fac[:, :, :], fac[:, :, :], ACT.Exp, scale=1.0 / TAU))
                act.activation(egT[:, :, :], logT[:, :, T:N], ACT.Exp, scale=1.0 / TAU).then_inc(e_ok, 1)

            n_log = max(n for n, (_, kind, _) in enumerate(JOBS) if kind == "decay") + 1
            n_va = done_with("va1")
            n_ua = done_with("ua1")
            for n in range(n_log):
                evacuate(n)
            soft_logs()
            for n in range(n_log, done_with("v0")):
                evacuate(n)
            decays()
            for n in range(done_with("v0"), n_va):
                evacuate(n)
            for n in range(n_va, n_ua):
                evacuate(n)
            for j in range(NT + 1):
                deviation("va", j, rows(j), 1, mv[0:rows(j), 0, 1:2], 1.0)
            for n in range(n_ua, BEFORE_GATES):
                evacuate(n)

            def gla_norm(j):
                p = rows(j)
                act.wait_ge(o_done, j + 1)
                if j:
                    act.wait_ge(ot_done, j)
                for h in range(H):
                    last = act.activation(oN[0:p, h, :], X[1][0:p, h * DV:(h + 1) * DV], ACT.Square,
                                          accum_out=ss[0:p, h:h + 1])
                last.then_inc(ss_ok, 1)
                deviation("o", j, p, H, rstd[0:p, 0:H], 1.0)
                act.wait_ge(orms_ok, j + 1)
                for h in range(H):
                    last = act.activation(oN[0:p, h, :], X[1][0:p, h * DV:(h + 1) * DV], ACT.Copy,
                                          scale=rstd[0:p, h:h + 1])
                last.then_inc(on_ok, 1)

            act.wait_ge(qk_ok, NT)
            for j in range(NT):
                act.wait_ge(att_done, j + 1)
                act.activation(knat, X[0][:, 512:1024].rearrange("p (a b) -> p a b", a=H), ACT.Copy).then_inc(knat_ok, 1)
                gla_norm(j)
            act.wait_ge(att_done, NT + 1)
            act.wait_ge(kv_done, NT)
            act.activation(knat[0:S], X[0][0:S, 0:512].rearrange("p (a b) -> p a b", a=H), ACT.Copy).then_inc(knat_ok, 1)
            gla_norm(NT)
            act.wait_ge(cv_out, 32)
            for n in range(BEFORE_GATES, BEFORE_BRANCH):
                evacuate(n)

            def copy_turned(what, j):
                n = TURN[what, j]
                p = rows(j)
                act.wait_ge(tr_done, n + 1)
                dst = x1T[(j if what == "x1" else j + 1) % 2][:, :, 0:p]
                act.activation(dst, X[0][:, :].rearrange("p (a b) -> p a b", a=KC)[:, :, 0:p], ACT.Copy).then_inc(
                    x1t_ok, 1)

            def route(j, h, part):
                p, r = rows(j), j * PH + h
                if part == 0:
                    deviation("q", j, p, 2, mv[0:p, :, 1:2].rearrange("p a b -> p (a b)"), 1.0, h)
                elif part == 1:
                    act.wait_ge(qt_done, r + 1)
                    act.activation(qT[:, :, 0:p], RT[:, 0:256].rearrange("p (a b) -> p a b", a=2)[:, :, 0:p],
                                   ACT.Copy).then_inc(qt_ok, 1)
                else:
                    act.wait_ge(exp_in, r + 1)
                    act.activation(ex[0:p, :], top[0:p, :], ACT.Exp, bias=soft[0:p, 0:1],
                                   accum_out=soft[0:p, 1:2]).then_inc(exp_ok, 1)

            def diagonals(n, ks):
                for k in ks:
                    m = n * TOPK + k
                    if k == 0:
                        act.wait_ge(w_ok, n + 1)
                    if m >= DB:
                        act.wait_ge(v_used, m - DB + 1)
                    act.activation(diag[m % DB], ident[:, :], ACT.Copy, scale=wgt[:, n % 2, k:k + 1]).then_inc(diag_ok, 1)

            def gelu(n):
                act.wait_ge(h_ok, n + 1)
                act.activation(hact[:, n % 2, :], hraw[:, n % 2, :], ACT.Gelu_apprx_tanh).then_inc(g_ok, 1)

            def finish(j, part):
                p = rows(j)
                if part == 0:
                    deviation("x2", j, p, 1, mv[0:p, 0, 1:2], 1.0)
                elif part == 1:
                    copy_turned("x2", j)
                else:
                    act.wait_ge(w_done, WIDE["pg", j] + 1)
                    if j:
                        act.wait_ge(x3_ok, j)
                    act.activation(sg[0:p, :].rearrange("p (a b) -> p a b", a=2), W[0:p], ACT.Sigmoid).then_inc(g_done, 1)

            for j in range(NT + 1):
                if j == 1:
                    copy_turned("x1", 0)
                deviation("x1", j, rows(j), 1, mv[0:rows(j), 0, 1:2], 1.0)
            copy_turned("x1", 1)
            for h in range(PH):
                for part in range(3):
                    route(0, h, part)
            gelu(0)
            for n in expert_steps():
                j, h = n // PH, n % PH
                if h == 0 and j > 0:
                    copy_turned("x1", j + 1)
                diagonals(n, range(0, 3))
                if h == 1 and j > 0:
                    finish(j - 1, 0)
                route(j + 1, h, 0)
                diagonals(n, range(3, 6))
                route(j + 1, h, 1)
                diagonals(n, range(6, 10))
                route(j + 1, h, 2)
                diagonals(n, range(10, 16))
                if h == 1 and j > 0:
                    finish(j - 1, 1)
                if h == 2 and j > 0:
                    finish(j - 1, 2)
                if n + 1 < ITERS:
                    gelu(n + 1)
            act.wait_ge(it_done, 2)
            act.activation(gateT[:, :], RT[:, 0:8], ACT.Copy).then_inc(it_ok, 1)
            for part in range(3):
                finish(NT - 1, part)
            act.wait_ge(hs_ok, 1)
            act.activation(aS[:, :], hS[:, :], ACT.Gelu_apprx_tanh).then_inc(g_ok, 1)
            for part in range(3):
                finish(NT, part)

        @block.vector
        def _(v):
            chain = [0]

            def link(ins):
                chain[0] += 1
                ins.then_inc(dve_chain, 1)
                v.wait_ge(dve_chain, chain[0])

            def row_stats(src, p):
                v.bn_stats(bn[0:p, 0, :], src[:, 0:512])
                link(v.bn_stats(bn[0:p, 1, :], src[:, 512:1024]))
                link(v.bn_aggr(mv[0:p, 0, :], bn[0:p].rearrange("p a b -> p (a b)")))
                v.tensor_scalar(mv[0:p, 0, 1:2], mv[0:p, 0, 1:2], EPS, None, ALU.add).then_inc(var_ok, 1)

            def inverse(what, j, p, n, h=0):
                i = sdn(what, j, h)
                v.wait_ge(sd_ok, i + 1)
                return v.reciprocal(rstd[0:p, 0:n], sd[0:p, 0:n])

            def layernorm(t, what, j, g, b, done):
                p = rows(j)
                row_stats(t, p)
                link(inverse(what, j, p, 1))
                link(v.tensor_scalar(t, t, mv[0:p, 0, 0:1], rstd[0:p, 0:1], ALU.subtract, ALU.mult))
                link(v.tensor_tensor(t, t, g[0:p], ALU.mult))
                v.tensor_tensor(t, t, b[0:p], ALU.add).then_inc(done, 1)

            v.wait_ge(const_ok, 6)
            v.wait_ge(soft_part, 1)
            link(v.scalar_tensor_tensor(out=logT, in0=logT, scalar=0.0, in1=rT[:, 0:H, :], op0=ALU.min,
                                        op1=ALU.subtract))
            for j in range(NT):
                for h in range(H):
                    c = logT[:, h, cols(j)]
                    last = v.tensor_tensor_scan(c, ones, c, 0.0, ALU.mult, ALU.add)
                    chain[0] += 1
                    last.then_inc(dve_chain, 1)
            v.wait_ge(dve_chain, chain[0])
            for j in range(NT):
                m = logT[:, :, 128 * j + 63:128 * j + 64].rearrange("p a b -> p (a b)")
                link(v.tensor_scalar(mid[:, j, 0, :], m, -1.0 / TAU, None, ALU.mult))
                v.tensor_scalar(mid[:, j, 1, :], m, 1.0 / TAU, None, ALU.mult).then_inc(mid_ok, 1)
            for j in range(NT):
                m = logT[:, :, 128 * j + 63:128 * j + 64].rearrange("p a b -> p (a b)")
                e = logT[:, :, 128 * j + 127:128 * j + 128].rearrange("p a b -> p (a b)")
                ins = v.tensor_tensor(fac[:, j, :], e, m, ALU.subtract)
                if j + 1 < NT:
                    link(ins)
                    m2 = logT[:, :, 128 * j + 191:128 * j + 192].rearrange("p a b -> p (a b)")
                    link(v.tensor_tensor(fac[:, j, :], fac[:, j, :], m2, ALU.add))
            ins.then_inc(mid_ok, 1)
            v.wait_ge(pj_act, done_with("k0"))
            for j in range(NT):
                v.wait_ge(e_ok, j + 1)
                v.tensor_tensor(qkT[:, 0:H, cols(j)], qkT[:, 0:H, cols(j)], Ep, ALU.mult)
                link(v.tensor_tensor(qkT[:, H:2 * H, cols(j)], qkT[:, H:2 * H, cols(j)], Em, ALU.mult))
                v.sem_inc(qk_ok, 1)
            v.wait_ge(row_in, 16 * 6)
            link(v.tensor_tensor(wsT, wsT, mask.unsqueeze(1).broadcast_to([128, G, 128]), ALU.mult))
            v.tensor_copy(bs0, bsrow.rearrange("p (a b) -> p a b", a=G)[:, :, 0:1].broadcast_to([1, G, S]))
            link(v.tensor_tensor(dg, ident[0:S, 0:S].unsqueeze(1).broadcast_to([S, G, S]),
                                 w00[:, :].unsqueeze(2).broadcast_to([S, G, S]), ALU.mult))
            for j in range(NT + 1):
                n = [i for i, (b, _, part) in enumerate(JOBS)
                     if b is not None and BLOCKS[b] == "va1" and part == j][0]
                v.wait_ge(pj_act, n + 1)
                layernorm(vaN[0:rows(j), j, :], "va", j, lnvg, lnvb, vn_ok)

            def gate_values(j):
                v.wait_ge(z_done, j + 1)
                if j == 0:
                    v.wait_ge(pj_act, done_with("ua1"))
                p = rows(j)
                z = X[j % 2][:, 0:G * p].rearrange("p (a b) -> p a b", a=G)
                v.tensor_tensor(uaT[:, :, cols(j)], uaT[:, :, cols(j)], z, ALU.mult).then_inc(ya_ok, 1)

            for j in range(NT + 1):
                gate_values(j)

            def output_stats(j):
                p = rows(j)
                v.wait_ge(ss_ok, j + 1)
                v.tensor_scalar(rstd[0:p, 0:H], ss[0:p, 0:H], 1.0 / DV, EPS, ALU.mult, ALU.add).then_inc(var_ok, 1)
                inverse("o", j, p, H).then_inc(orms_ok, 1)

            def branch_b(j):
                p = rows(j)
                v.wait_ge(ot_done, j + 1)
                v.wait_ge(pj_act, BEFORE_GATES)
                t = PJ[:, j % 2, :, :].rearrange("p a (b c) -> p (a b) c", b=4)
                for q in range(2):
                    dst = rT[:, q::2, cols(j)]
                    last = v.scalar_tensor_tensor(out=dst, in0=t[:, q::2, 0:p], scalar=gng[:, q:q + 1], in1=dst,
                                                  op0=ALU.mult, op1=ALU.mult)
                    chain[0] += 1
                    last.then_inc(dve_chain, 1)
                v.wait_ge(dve_chain, chain[0])
                v.sem_inc(yb_ok, 1)

            for j in range(NT):
                v.wait_ge(att_done, j + 1)
                if j:
                    v.wait_ge(o_done, j)
                v.tensor_tensor(attS, X[0][:, 0:512].rearrange("p (a b) -> p a b", a=H),
                                mask.unsqueeze(1).broadcast_to([128, H, 128]), ALU.mult).then_inc(att_ok, 1)
                v.wait_ge(kv_done, j + 1)
                kv = X[0][:, :].rearrange("p (a b) -> p a b", a=H)
                v.wait_ge(e_ok, NT + 1)
                src = kv
                if j:
                    v.wait_ge(o_done, j + 1)
                    link(v.tensor_tensor(Sst, kv, Sst, ALU.add))
                    src = Sst
                for h in range(H):
                    last = v.tensor_scalar(Sst[:, h, :], src[:, h, :], fac[:, j, h:h + 1], None, ALU.mult)
                    chain[0] += 1
                    last.then_inc(dve_chain, 1)
                v.wait_ge(dve_chain, chain[0])
                v.sem_inc(s_ok, 1)
                output_stats(j)
                if j:
                    branch_b(j - 1)
            v.wait_ge(knat_ok, NT + 1)
            for h in range(H):
                if h:
                    v.wait_ge(outer_done, 2 * h)
                v.tensor_tensor(kpad[0:S], knat[0:S, h, :].unsqueeze(1).broadcast_to([S, S, 128]),
                                ident[0:S, 0:S].unsqueeze(2).broadcast_to([S, S, 128]), ALU.mult).then_inc(kpad_ok, 1)
                if h:
                    v.wait_ge(os_done, h)
                v.tensor_copy(qpad.rearrange("p a b -> p (a b)")[:, 0:S * S:S + 1], qkT[:, h, T:N]).then_inc(kpad_ok, 1)
                v.wait_ge(s0_in[h % 2], 16 * (h // 2 + 1))
                for b in range(S):
                    if b % 4 == 0:
                        v.wait_ge(outer_done, 2 * h + b // 4 + 1)
                    v.scalar_tensor_tensor(out=S0[h % 2][:, b, :], in0=S0[h % 2][:, b, :], scalar=egT[:, h, b:b + 1],
                                           in1=X[0][:, (b % 4) * DV:(b % 4 + 1) * DV], op0=ALU.mult,
                                           op1=ALU.add).then_inc(s0_new, 1)
                if h == 0:
                    branch_b(NT - 1)
            output_stats(NT)
            branch_b(NT)
            v.wait_ge(pj_act, BEFORE_BRANCH)
            for n in range(BEFORE_BRANCH, len(JOBS)):
                blk, _, part = JOBS[n]
                name = BLOCKS[blk]
                c = 4 * int(name[-1]) + part
                ga, gb = (t[:, c, :].rearrange("p (a b) -> p a b", a=2) for t in (gaT, gbT))
                v.wait_ge(pj_done, n + 1)
                half = PJ[:, n % 2, :, 0:HALF]
                if name[:-1] == "bra":
                    v.tensor_tensor(ga, ga, half, ALU.mult).then_inc(pj_dve, 1)
                else:
                    v.wait_ge(pj_dve, n - BEFORE_BRANCH)
                    link(v.tensor_tensor(gb, gb, half, ALU.mult))
                    v.tensor_tensor(ga, ga, gb, ALU.add).then_inc(pj_dve, 1)

            def scaled_add(dst, src, n_done, done):
                p = dst.shape[0]
                chain[0] += 1
                v.scalar_tensor_tensor(out=dst.rearrange("p (a b) -> p a b", a=2),
                                       in0=dst.rearrange("p (a b) -> p a b", a=2), scalar=ALPHA, in1=src[0:p],
                                       op0=ALU.mult, op1=ALU.add).then_inc(dve_chain, 1)
                v.wait_ge(dve_chain, chain[0])
                v.sem_inc(done, 1)

            v.wait_ge(ln1_in, 32)
            for j in range(NT + 1):
                t = x1[0:rows(j), j, :]
                v.wait_ge(xr_in[j], 16)
                v.wait_ge(w_done, WIDE["wo", j] + 1)
                scaled_add(t, W, 0, y_read)
                layernorm(t, "x1", j, ln1g, ln1b, x1_ok)

            def top16(vals16, inds16, src, spare):
                link(v.max(vals16[:, 0:8], src))
                v.max_index(inds16[:, 0:8], vals16[:, 0:8], src)
                link(v.match_replace(spare, vals16[:, 0:8], src, NEG))
                link(v.max(vals16[:, 8:16], spare))
                link(v.max_index(inds16[:, 8:16], vals16[:, 8:16], spare))

            def route(j, h, part):
                p, r = rows(j), j * PH + h
                if part == 0:
                    v.wait_ge(q_done, r + 1)
                    v.bn_stats(bn[0:p, 0, :], RQ[0:p, 0:128])
                    link(v.bn_stats(bn[0:p, 1, :], RQ[0:p, 128:256]))
                    v.bn_aggr(mv[0:p, 0, :], bn[0:p, 0, :])
                    link(v.bn_aggr(mv[0:p, 1, :], bn[0:p, 1, :]))
                    v.tensor_scalar(mv[0:p, :, 1:2], mv[0:p, :, 1:2], EPS, None, ALU.add).then_inc(var_ok, 1)
                elif part == 1:
                    link(inverse("q", j, p, 2, h))
                    for i in range(2):
                        last = v.tensor_scalar(qN[0:p, i, :], RQ[0:p, 128 * i:128 * i + 128], mv[0:p, i, 0:1],
                                               rstd[0:p, i:i + 1], ALU.subtract, ALU.mult)
                        last.then_inc(qn_ok, 1)
                elif part == 2:
                    v.wait_ge(s_done, r + 1)
                    link(v.tensor_copy(scores[0:p], RQ[0:p, 256:512].rearrange("p (a b) -> p a b", a=2)))
                    for i in range(2):
                        top16(vals[0:p, i, :], inds[0:p, i, :], scores[0:p, i, :], scoresR[0:p, i, :])
                    v.tensor_copy(indf[0:p], inds[0:p])
                    link(v.tensor_tensor(cand[0:p].rearrange("p (a b) -> p a b", a=TOPK),
                                         vals[0:p, 0, :].unsqueeze(2).broadcast_to([p, TOPK, TOPK]),
                                         vals[0:p, 1, :].unsqueeze(1).broadcast_to([p, TOPK, TOPK]), ALU.add))
                    top16(top[0:p], topi[0:p], cand[0:p], candR[0:p])
                    link(v.tensor_scalar(soft[0:p, 0:1], top[0:p, 0:1], -1.0, None, ALU.mult))
                    v.sem_inc(exp_in, 1)
                    v.tensor_scalar(abu[0:p, 0, :], topi[0:p], 4, None, ALU.logical_shift_right)
                    link(v.tensor_scalar(abu[0:p, 1, :], topi[0:p], 15, None, ALU.bitwise_and))
                    link(v.tensor_copy(abf[0:p], abu[0:p]))
                    link(v.tensor_tensor(onehot[0:p], abf[0:p].unsqueeze(3).broadcast_to([p, 2, TOPK, TOPK]),
                                         iota16[0:p].unsqueeze(1).unsqueeze(1).broadcast_to([p, 2, TOPK, TOPK]),
                                         ALU.is_equal))
                    link(v.tensor_tensor(onehot[0:p], onehot[0:p],
                                         indf[0:p].unsqueeze(2).broadcast_to([p, 2, TOPK, TOPK]), ALU.mult))
                    link(v.tensor_reduce(e12[0:p], onehot[0:p], AX.X, ALU.add))
                else:
                    s = slice(h * TOPK, (h + 1) * TOPK)
                    v.wait_ge(exp_ok, r + 1)
                    link(v.reciprocal(soft[0:p, 2:3], soft[0:p, 1:2]))
                    v.tensor_scalar(gates[j % 2][0:p, s], ex[0:p, :], soft[0:p, 2:3], None, ALU.mult)
                    link(v.scalar_tensor_tensor(out=idx[j % 2][0:p, s], in0=e12[0:p, 0, :], scalar=float(NK),
                                                in1=e12[0:p, 1, :], op0=ALU.mult, op1=ALU.add))
                    v.sem_inc(route_ok, 1)

            def dots(n, ks):
                for k in ks:
                    m = n * TOPK + k
                    v.wait_ge(u_in[m % UB], 16 * (m // UB + 1))
                    t = ubuf[m % UB]
                    last = v.tensor_tensor_reduce(out=t, in0=t, in1=x1[:, n // PH, :], scale=1.0, scalar=0.0,
                                                  op0=ALU.mult, op1=ALU.add, accum_out=hraw[:, n % 2, k:k + 1])
                    last.then_inc(u_used, 1)
                if ks[-1] == TOPK - 1:
                    v.wait_ge(u_used, (n + 1) * TOPK)
                    v.sem_inc(h_ok, 1)

            def weights(n):
                v.wait_ge(g_ok, n + 1)
                s = slice((n % PH) * TOPK, (n % PH + 1) * TOPK)
                v.tensor_tensor(wgt[:, n % 2, :], hact[:, n % 2, :], gates[(n // PH) % 2][:, s], ALU.mult).then_inc(
                    w_ok, 1)

            def finish(j, part):
                p = rows(j)
                t = x1[0:p, j, :]
                if part == 0:
                    v.wait_ge(y_done, j + 1)
                    if j == 0:
                        v.wait_ge(ln2_in, 32)
                    scaled_add(t, Y, 0, y_read)
                elif part == 1:
                    layernorm(t, "x2", j, ln2g, ln2b, x2_ok)
                else:
                    v.wait_ge(g_done, j + 1)
                    v.wait_ge(w_done, WIDE["pe", j] + 1)
                    s2 = sg[0:p, :].rearrange("p (a b) -> p a b", a=2)
                    link(v.tensor_tensor(s2, s2, W[0:p], ALU.mult))
                    v.tensor_tensor(t, t, sg[0:p, :], ALU.add).then_inc(x3_ok, 1)

            for h in range(PH):
                for part in range(4):
                    route(0, h, part)
            dots(0, range(TOPK))
            weights(0)
            for n in expert_steps():
                j, h = n // PH, n % PH
                nxt = n + 1 < ITERS
                if h == 0 and j > 0:
                    finish(j - 1, 0)
                if h == 1 and j > 0:
                    finish(j - 1, 1)
                route(j + 1, h, 0)
                if nxt:
                    dots(n + 1, range(0, 2))
                route(j + 1, h, 1)
                if nxt:
                    dots(n + 1, range(2, 8))
                route(j + 1, h, 2)
                if nxt:
                    dots(n + 1, range(8, 12))
                route(j + 1, h, 3)
                if nxt:
                    dots(n + 1, range(12, 16))
                    if n >= 1:
                        v.wait_ge(diag_ok, n * TOPK)
                    weights(n + 1)
                if h == 3 and j > 0:
                    finish(j - 1, 2)
            link(v.tensor_copy(idxf, idx[NT % 2][0:S, :]))
            v.sem_inc(it_done, 1)
            v.wait_ge(it_done, 2)
            v.tensor_copy(idxT[:, :], RQ[:, 0:8]).then_inc(it_ok, 1)
            finish(NT - 1, 0)
            finish(NT - 1, 1)
            finish(NT - 1, 2)
            for b in range(S):
                m = ITERS * TOPK + b
                v.wait_ge(u_in[m % UB], 16 * (m // UB + 1))
                v.wait_ge(xb_done, b + 1)
                t = ubuf[m % UB].rearrange("p (a b) -> p a b", a=2)
                v.tensor_tensor_reduce(out=t, in0=t, in1=X[0][:, :].rearrange("p (a b) -> p a b", a=2), scale=1.0,
                                       scalar=0.0, op0=ALU.mult, op1=ALU.add,
                                       accum_out=hS[:, b:b + 1]).then_inc(u_used, 1)
            v.wait_ge(u_used, ITERS * TOPK + S)
            v.sem_inc(hs_ok, 1)
            v.wait_ge(g_ok, ITERS + 1)
            v.wait_ge(it_ok, 2)
            v.tensor_tensor(wpad[:, :, :].rearrange("p a b -> p (a b)")[:, 0:S * S:S + 1], aS[:, :], gateT[:, :],
                            ALU.mult).then_inc(wpad_ok, 1)
            for part in range(3):
                finish(NT, part)

        @block.tensor
        def _(pe):
            mm = nc.tensor.matmul
            pe.wait_ge(const_ok, 6)
            pe.wait_ge(small_in, 48)
            pe.wait_ge(xt_in, 16)

            def project(n):
                blk, kind, part = JOBS[n]
                if n >= 2:
                    if n - 2 < BEFORE_BRANCH:
                        pe.wait_ge(pj_act, n - 1)
                    else:
                        pe.wait_ge(pj_dve, n - 1 - BEFORE_BRANCH)
                if blk is not None:
                    pe.wait_ge(blk_in[blk % RING], 16 * (blk // RING + 1))
                out = PJ[:, n % 2, :, :]
                if kind == "natural":
                    p = rows(part)
                    for c in range(KC):
                        last = mm(out[0:p, 0, :], xT[:, c, cols(part)], ring[blk % RING][:, c, :],
                                  start=c == 0, stop=c == KC - 1)
                elif kind == "decay":
                    pe.wait_ge(pj_act, 1)
                    for s in range(2):
                        last = mm(out[:, s, 0:HALF], wgk[:, part * DK:(part + 1) * DK], gkl[:, s * HALF:(s + 1) * HALF],
                                  start=True, stop=True)
                else:
                    src = {"bra": uaT, "brb": rT}.get(BLOCKS[blk][:-1] if blk is not None else "", xT)
                    for c in range(KC):
                        w = wgkl[:, c, :] if kind == "low" else ring[blk % RING][:, c, part * 128:(part + 1) * 128]
                        for s in range(2):
                            last = mm(out[0:RANK if kind == "low" else 128, s, 0:HALF], w,
                                      src[:, c, s * HALF:(s + 1) * HALF], start=c == 0, stop=c == KC - 1)
                last.then_inc(pj_done, 1)

            for n in range(BEFORE_GATES):
                project(n)

            for j in range(NT + 1):
                p = rows(j)
                pe.wait_ge(vn_ok, j + 1)
                if j >= 2:
                    pe.wait_ge(ya_ok, j - 1)
                z = X[j % 2][:, 0:G * p].rearrange("p (a b) -> p a b", a=G)
                for g in range(G):
                    w = wsT[:, g, :] if j < NT else dg[:, g, :]
                    b = bsrow[:, g * 128:(g + 1) * 128] if j < NT else bs0[:, g, :]
                    mm(z[:, g, :], vaN[0:p, j, g * 128:(g + 1) * 128], w, start=True, stop=False)
                    last = mm(z[:, g, :], ones[0:1, :], b, start=False, stop=True)
                last.then_inc(z_done, 1)

            def turn_output(j):
                p = rows(j)
                pe.wait_ge(on_ok, j + 1)
                pe.wait_ge(pj_act, BEFORE_GATES)
                if j >= 2:
                    pe.wait_ge(yb_ok, j - 1)
                for c in range(KC):
                    last = nc.tensor.transpose(PJ[:, j % 2, c // 4, (c % 4) * 128:(c % 4) * 128 + p],
                                               oN[0:p, c // 2, (c % 2) * 128:(c % 2 + 1) * 128], ident[0:p, 0:p])
                last.then_inc(ot_done, 1)

            pe.wait_ge(ya_ok, NT + 1)
            for j in range(NT):
                pe.wait_ge(qk_ok, j + 1)
                if j:
                    pe.wait_ge(s_ok, j)
                for h in range(H):
                    mm(X[0][:, h * 128:(h + 1) * 128], qkT[:, H + h, cols(j)], qkT[:, h, cols(j)], start=True, stop=True)
                for h in range(H):
                    last = nc.tensor.transpose(X[0][:, 512 + h * 128:640 + h * 128], qkT[:, H + h, cols(j)], ident[:, :])
                last.then_inc(att_done, 1)
                if j:
                    turn_output(j - 1)
                pe.wait_ge(att_ok, j + 1)
                for h in range(H):
                    o_h = X[1][:, h * DV:(h + 1) * DV]
                    last = mm(o_h, attS[:, h, :], vN[:, j, h * DV:(h + 1) * DV], start=True, stop=j == 0)
                    if j:
                        last = mm(o_h, qkT[:, h, cols(j)], Sst[:, h, :], start=False, stop=True)
                last.then_inc(o_done, 1)
                pe.wait_ge(knat_ok, j + 1)
                for h in range(H):
                    last = mm(X[0][:, h * DV:(h + 1) * DV], knat[:, h, :], vN[:, j, h * DV:(h + 1) * DV],
                              start=True, stop=True)
                last.then_inc(kv_done, 1)
            pe.wait_ge(s_ok, NT)
            for h in range(H):
                last = nc.tensor.transpose(X[0][0:S, h * 128:(h + 1) * 128], qkT[:, H + h, T:N], ident[:, :])
            last.then_inc(att_done, 1)
            turn_output(NT - 1)
            pe.wait_ge(knat_ok, NT + 1)
            for h in range(H):
                pe.wait_ge(kpad_ok, 2 * h + 2)
                for b in range(S):
                    if b % 4 == 0 and 8 * h + b:
                        pe.wait_ge(s0_new, 8 * h + b)
                    last = mm(X[0][:, (b % 4) * DV:(b % 4 + 1) * DV], kpad[0:S, b, :], vN[0:S, NT, h * DV:(h + 1) * DV],
                              start=True, stop=True)
                    if b % 4 == 3:
                        last.then_inc(outer_done, 1)
                pe.wait_ge(s0_new, 8 * h + 8)
                for b in range(S):
                    last = mm(X[1][0:S, h * DV:(h + 1) * DV], qpad[:, b, :], S0[h % 2][:, b, :],
                              start=b == 0, stop=b == S - 1)
                last.then_inc(os_done, 1)
            pe.wait_ge(os_done, H)
            pe.sem_inc(o_done, 1)
            turn_output(NT)
            pe.wait_ge(yb_ok, NT + 1)
            for n in range(BEFORE_GATES, len(JOBS)):
                project(n)

            def wide(what, j):
                p = rows(j)
                n = WIDE[what, j]
                if what == "wo":
                    if j:
                        pe.wait_ge(y_read, j)
                    lhs = [gaT[:, c, cols(j)] for c in range(KC)]
                    rhs = [[ring[s][:, c, :] for c in range(KC)] for s in range(2)]
                elif what == "pg":
                    if j:
                        pe.wait_ge(x3_ok, j)
                    pe.wait_ge(x1t_ok, TURN["x2", j] + 1)
                    pe.wait_ge(wpg_in, 32)
                    lhs = [x1T[(j + 1) % 2][:, c, 0:p] for c in range(KC)]
                    rhs = [[ring[s][:, c, :] for c in range(KC)] for s in range(2)]
                else:
                    pe.wait_ge(g_done, j + 1)
                    pe.wait_ge(wpe_in, 16)
                    pe.wait_ge(pt_in, 16 * (j + 1))
                    lhs = [pT[:, c, 0:p] for c in range(2)]
                    rhs = [[wpe[:, c, 512 * s:512 * s + 512] for c in range(2)] for s in range(2)]
                for c in range(len(lhs)):
                    for s in range(2):
                        last = mm(W[0:p, s, :], lhs[c], rhs[s][c], start=c == 0, stop=c == len(lhs) - 1)
                last.then_inc(w_done, 1)

            def turn(what, j):
                p = rows(j)
                n = TURN[what, j]
                pe.wait_ge(x1_ok if what == "x1" else x2_ok, j + 1)
                if n:
                    pe.wait_ge(x1t_ok, n)
                for c in range(KC):
                    last = nc.tensor.transpose(X[0][:, c * 128:c * 128 + p], x1[0:p, j, c * 128:(c + 1) * 128],
                                               ident[0:p, 0:p])
                last.then_inc(tr_done, 1)

            def route(j, h, part):
                p, r = rows(j), j * PH + h
                if part == 0:
                    if h == 0:
                        pe.wait_ge(x1t_ok, TURN["x1", j] + 1)
                    if r:
                        pe.wait_ge(route_ok, r)
                    pe.wait_ge(wq_in[h // 2], 16)
                    for c in range(KC):
                        last = mm(RQ[0:p, 0:256], x1T[j % 2][:, c, 0:p], wq[h // 2][:, c, (h % 2) * 256:(h % 2 + 1) * 256],
                                  start=c == 0, stop=c == KC - 1)
                    last.then_inc(q_done, 1)
                elif part == 1:
                    pe.wait_ge(qn_ok, 2 * r + 2)
                    for i in range(2):
                        last = nc.tensor.transpose(RT[:, i * 128:i * 128 + p], qN[0:p, i, :], ident[0:p, 0:p])
                    last.then_inc(qt_done, 1)
                else:
                    pe.wait_ge(qt_ok, r + 1)
                    pe.wait_ge(keys_in, 16)
                    for i in range(2):
                        last = mm(RQ[0:p, 256 + i * 128:384 + i * 128], qT[:, i, 0:p], keysT[:, 2 * h + i, :],
                                  start=True, stop=True)
                    last.then_inc(s_done, 1)

            def sums(n, ks):
                for k in ks:
                    m = n * TOPK + k
                    first, final = m % SLOTS == 0, m % SLOTS == SLOTS - 1
                    if first and n:
                        pe.wait_ge(y_read, NT + 1 + n // PH)
                    pe.wait_ge(v_in[m % VB], 16 * (m // VB + 1))
                    pe.wait_ge(diag_ok, m + 1)
                    for s in range(2):
                        last = mm(Y[:, s, :], diag[m % DB], vbuf[m % VB][:, 512 * s:512 * s + 512], start=first, stop=final)
                    last.then_inc(v_used, 1)
                    if final:
                        pe.wait_ge(v_used, m + 1)
                        pe.sem_inc(y_done, 1)

            pe.wait_ge(pj_dve, len(JOBS) - BEFORE_BRANCH)
            pe.wait_ge(wo_in, 32)
            for j in range(NT + 1):
                wide("wo", j)
                if j == 1:
                    turn("x1", 0)
            turn("x1", 1)
            for h in range(PH):
                for part in range(3):
                    route(0, h, part)
            for n in expert_steps():
                j, h = n // PH, n % PH
                if h == 0 and j > 0:
                    turn("x1", j + 1)
                route(j + 1, h, 0)
                sums(n, range(0, 3))
                route(j + 1, h, 1)
                sums(n, range(3, 6))
                route(j + 1, h, 2)
                sums(n, range(6, 16))
                if h == 1 and j > 0:
                    turn("x2", j - 1)
                if h == 2 and j > 0:
                    wide("pg", j - 1)
                if h == 3 and j > 0:
                    wide("pe", j - 1)
            pe.wait_ge(it_done, 1)
            pe.wait_ge(route_ok, (NT + 1) * PH)
            nc.tensor.transpose(RQ[:, 0:8], idxf, ident[0:S, 0:S])
            last = nc.tensor.transpose(RT[:, 0:8], gates[NT % 2][0:S, :], ident[0:S, 0:S])
            last.then_inc(it_done, 1)
            turn("x2", NT - 1)
            wide("pg", NT - 1)
            wide("pe", NT - 1)
            pe.wait_ge(x1t_ok, TURN["x2", NT - 1] + 1)
            for b in range(S):
                if b:
                    pe.wait_ge(u_used, ITERS * TOPK + b)
                for s in range(2):
                    last = mm(X[0][:, 512 * s:512 * s + 512], ident[0:S, b:b + 1].broadcast_to([S, 128]),
                              x1[0:S, NT, 512 * s:512 * s + 512], start=True, stop=True)
                last.then_inc(xb_done, 1)
            pe.wait_ge(wpad_ok, 1)
            pe.wait_ge(y_read, NT + 1 + NT)
            for b in range(S):
                m = ITERS * TOPK + b
                pe.wait_ge(v_in[m % VB], 16 * (m // VB + 1))
                for s in range(2):
                    last = mm(Y[0:S, s, :], wpad[:, b, :], vbuf[m % VB][:, 512 * s:512 * s + 512],
                              start=b == 0, stop=b == S - 1)
                last.then_inc(v_used, 1)
            pe.wait_ge(v_used, ITERS * TOPK + S)
            pe.sem_inc(y_done, 1)
            turn("x2", NT)
            wide("pg", NT)
            wide("pe", NT)


def kernel(**inputs):
    import numpy as np
    import concourse.bacc as bacc
    from concourse.bass_utils import run_bass_kernel_spmd

    a = {k: np.asarray(t) for k, t in inputs.items()}

    def chunked(w, width):
        r, c = w.shape
        return w.reshape(r // 128, 128, c // width, width).transpose(2, 1, 0, 3)

    w_in = a["w_in"][0]
    starts = {"ua": 0, "va": D, "q": 2 * D, "k": 2 * D + 512, "v": 3 * D, "r": 4 * D,
              "ga": 5 * D + RANK, "gb": 6 * D + RANK}
    blocks = []
    for name in BLOCKS:
        kind, i = name[:-1], int(name[-1])
        if kind == "bra":
            src, c = a["w_br_a"][0], 512 * i
        elif kind == "brb":
            src, c = a["w_br_b"][0], 512 * i
        else:
            src, c = w_in, starts[kind] + 512 * i
        blocks.append(chunked(src[:, c:c + 512], 512)[0])
    x_all = np.concatenate([a["x_prompt"][0], a["x_sample"][:, 0]])
    p_all = np.concatenate([a["p_prompt"][0, 0], a["p_sample"][0, :, 0]])
    ins = {
        "x_all": x_all,
        "x_t": x_all.T.reshape(KC, 128, N).transpose(1, 0, 2),
        "state": a["state_gla"][0].transpose(1, 2, 0, 3),
        "p_t": p_all.T.reshape(2, 128, N).transpose(1, 0, 2),
        "w_blk": np.stack(blocks),
        "w_gkl": chunked(w_in[:, 5 * D:5 * D + RANK], RANK)[0],
        "w_gk": a["w_gk"][0],
        "b_gk": a["b_gk"][0].reshape(H, DK).T,
        "ws_t": a["w_s"][0].transpose(2, 0, 1),
        "ws0": a["w_s"][0][:, 0, 0],
        "b_s": a["b_s"][0].reshape(1, G * 128),
        "lnv_g": a["ln_v_g"][0], "lnv_b": a["ln_v_b"][0],
        "gn_g": a["gla_norm_g"][0].reshape(2, 128).T,
        "w_o": chunked(a["w_o"][0], 512),
        "ln1_g": a["ln1_g"][0], "ln1_b": a["ln1_b"][0],
        "w_q": chunked(a["peer_wq"][0], 512),
        "keys_t": a["peer_keys"][0].reshape(2 * PH, NK, 128).transpose(2, 0, 1),
        "u_tab": a["peer_u"][0], "v_tab": a["peer_v"][0],
        "ln2_g": a["ln2_g"][0], "ln2_b": a["ln2_b"][0],
        "w_pe": a["w_pe"][0].reshape(2, 128, D).transpose(1, 0, 2),
        "w_pg": chunked(a["w_pg"][0], 512),
    }
    outs = {"y_all": (N, D), "st_p": (DK, H, DV), "st_s": (H, DK, S, DV), "cv_p": (128, D), "cv_s": (S, D)}
    nc = bacc.Bacc("TRN2", target_bir_lowering=False, num_devices=1)
    arrays, aps = {}, []
    for name, t in ins.items():
        arrays[f"in_{name}"] = np.ascontiguousarray(t)
        aps.append(nc.dram_tensor(f"in_{name}", t.shape, F32, kind="ExternalInput").ap())
    for name, shape in outs.items():
        aps.append(nc.dram_tensor(f"out_{name}", shape, F32, kind="ExternalOutput").ap())
    decoder_step(nc, *aps)
    r = run_bass_kernel_spmd(nc, [arrays], core_ids=[0]).results[0]
    y = r["out_y_all"]
    return (y[:T].reshape(1, T, D), y[T:].reshape(S, 1, D),
            r["out_st_p"].transpose(1, 0, 2).reshape(1, 1, H, DK, DV),
            r["out_st_s"].transpose(2, 0, 1, 3).reshape(1, S, H, DK, DV),
            r["out_cv_p"].reshape(1, 1, 128, D), r["out_cv_s"].reshape(1, S, 1, D))
```

```python
import math
from contextlib import ExitStack

import concourse.bass as bass
from concourse import mybir

F32 = mybir.dt.float32
U32 = mybir.dt.uint32
ALU = mybir.AluOpType
ACT = mybir.ActivationFunctionType
AX = mybir.AxisListType

D = 1024
T, S = 512, 8
N = T + S
NT = T // 128
HALF = N // 2
KC = D // 128
G = 8
H, DK, DV, RANK = 4, 128, 256, 16
PH, NK, TOPK = 8, 128, 16
SLOTS = PH * TOPK
EPS = 1e-5
ALPHA = 2.0 ** 0.25
TAU = 16.0
NEG = -3.0e38

BLOCKS = ["q0", "k0", "v0", "v1", "va0", "va1", "ua0", "ua1", "r0", "r1",
          "ga0", "ga1", "gb0", "gb1", "bra0", "bra1", "brb0", "brb1"]
RING = 3
ROUTE_PARTS = 7
LEAD = 2
AHEAD = 4
UB, VB, DB = 4, 6, 6
ITERS = NT * PH
WO_AT = {1: 0, NT: 2, 2: 3, 3: 6}
FIRST_SAMPLE = 5
SAMPLE_DOTS_AT, SAMPLE_SUMS_AT = ITERS - 4, ITERS - 3


def rows(j):
    return 128 if j < NT else S


def cols(j):
    return slice(128 * j, 128 * j + rows(j))


def jobs():
    out = [(None, "low", 0)]
    for i, b in enumerate(BLOCKS):
        if b[:-1] in ("v", "va"):
            out += [(i, "natural", j) for j in range(NT + 1)]
        else:
            out += [(i, "columns", c) for c in range(4)]
        if b == "q0":
            out += [(None, "decay", h) for h in range(H)]
    return out


JOBS = jobs()


def done_with(name):
    return max(n for n, (b, _, _) in enumerate(JOBS) if b == BLOCKS.index(name)) + 1


BEFORE_GATES = done_with("r1")
BEFORE_BRANCH = done_with("gb1")


def decoder_step(nc, x_all, x_t, state, p_t, w_blk, w_gkl, w_gk, b_gk, ws_t, ws0, b_s, lnv_g, lnv_b, gn_g,
                 w_o, ln1_g, ln1_b, w_q, keys_t, u_tab, v_tab, ln2_g, ln2_b, w_pe, w_pg,
                 y_all, st_p, st_s, cv_p, cv_s):
    with ExitStack() as ctx:
        def sem(name):
            return ctx.enter_context(nc.semaphore(name))

        def tensor(name, shape, dt=F32):
            return ctx.enter_context(nc.sbuf_tensor(name, shape, dt))

        WORDS = 52288
        arena = tensor("arena", [128, WORDS])

        def at(off, *shape):
            n = math.prod(shape)
            assert off + n <= WORDS, (off, n)
            v = arena[:, off:off + n]
            if len(shape) == 2:
                v = v.rearrange("p (a b) -> p a b", a=shape[0])
            if len(shape) == 3:
                v = v.rearrange("p (a b c) -> p a b c", a=shape[0], b=shape[1])
            return v

        BW, TW = KC * 512, KC * N
        O_ACT = RING * BW
        O_V = O_ACT + 4 * TW
        O_TMP = O_V + 2 * (NT + 1) * D
        ring = [at(BW * i, KC, 512) for i in range(RING)]
        xT, uaT, qkT, rT = (at(O_ACT + TW * i, KC, N) for i in range(4))
        vN = at(O_V, NT + 1, D)
        vaN = at(O_V + (NT + 1) * D, NT + 1, D)
        gaT, gbT = at(O_V, KC, N), at(O_V + TW, KC, N)

        place = [O_TMP]

        def take(*shape):
            v = at(place[0], *shape)
            place[0] += math.prod(shape)
            return v

        logT = take(H, N)
        wsT = take(G, 128)
        S0 = [take(S, DV), take(S, DV)]
        lnvg, lnvb = S0[1][:, 0:4, :].rearrange("p a b -> p (a b)"), S0[1][:, 4:8, :].rearrange("p a b -> p (a b)")
        Sst = take(H, DV)
        attS, knat = take(H, 128), take(H, 128)
        Ep, Em = take(H, 128), take(H, 128)
        oN = at(place[0] - 2 * H * 128, H, DV)
        mask, ones = take(128), take(128)
        thin = take(N + H * DK)
        gkl, wgk = thin[0:RANK, 0:N], thin[0:RANK, N:N + H * DK]
        bsrow = thin[0:1, 0:G * 128]
        kpad = take(S, 128)
        dg = kpad[0:S, 0, 0:G * S].rearrange("p (a b) -> p a b", a=G)
        bs0 = kpad[0:1, 1, 0:G * S].rearrange("p (a b) -> p a b", a=G)
        qpad = take(S, S)
        wgkl = take(KC, RANK)
        wq = [at(O_ACT + TW * i, KC, 512) for i in range(4)]
        x1T, x2T = (at(2 * BW + D * i, KC, 128) for i in range(2))
        keysT = at(2 * BW + 2 * D, 2 * PH, NK)
        ln2g, ln2b, wpe = at(O_V, D), at(O_V + D, D), at(O_V + 2 * D, 2, D)
        x1 = at(O_V + TW, NT + 1, D)
        o = O_V + TW + (NT + 1) * D
        qN, qT, pT = at(o, 2, NK), at(o + 256, 2, 128), at(o + 512, 2, 128)
        assert o + 768 <= O_TMP
        ubuf = [at(O_TMP + D * i, D) for i in range(UB)]
        vbuf = [at(O_TMP + D * (UB + i), D) for i in range(VB)]
        place[0] = O_TMP + D * (UB + VB)
        sg = take(D)
        ln1g, ln1b = sg, x2T.rearrange("p a b -> p (a b)")
        x1Ts = at(o + 768, KC, S)
        onehot = take(2, TOPK, TOPK)
        scores = onehot.rearrange("p a b c -> p (a b c)")[:, 0:2 * NK].rearrange("p (a b) -> p a b", a=2)
        cand = take(TOPK * TOPK)
        idxf, gatesS = take(SLOTS)[0:S], take(SLOTS)[0:S]
        diag = [take(128) for _ in range(DB)]

        ident = tensor("ident", [128, 128])
        idx = tensor("idx", [128, AHEAD, TOPK], U32)
        gates = tensor("gates", [128, AHEAD, TOPK])
        vals, e12 = (tensor(n, [128, 2, TOPK]) for n in ("vals", "e12"))
        abf = vals
        inds, abu = (tensor(n, [128, 2, TOPK], U32) for n in ("inds", "abu"))
        indf = tensor("indf", [128, 2, TOPK])
        top, ex, iota16 = (tensor(n, [128, TOPK]) for n in ("top", "ex", "iota16"))
        topi = tensor("topi", [128, TOPK], U32)
        iotau = tensor("iotau", [128, TOPK], U32)
        hraw, hact = (tensor(n, [128, 2, TOPK]) for n in ("hraw", "hact"))
        wgt = tensor("wgt", [128, 3, TOPK])
        bn, mv = tensor("bn", [128, 2, 6]), tensor("mv", [128, 2, 2])
        sd, rstd = tensor("sd", [128, 4]), tensor("rstd", [128, 4])
        soft = tensor("soft", [128, 3])
        ss = tensor("ss", [128, H])
        bgk, gng = tensor("bgk", [128, H]), tensor("gng", [128, 2])
        mid = tensor("mid", [128, NT, 2, H])
        fac = tensor("fac", [128, NT, H])
        egT = tensor("egT", [128, H, S])
        w00 = tensor("w00", [S, G])
        idxT = tensor("idxT", [SLOTS, S], U32)
        gateT, hS, aS = (tensor(n, [SLOTS, S]) for n in ("gateT", "hS", "aS"))
        wpad = tensor("wpad", [SLOTS, S, S])

        PJ = ctx.enter_context(nc.psum_tensor("PJ", [128, 2, 2, 512], F32))
        X = [ctx.enter_context(nc.psum_tensor(f"X{i}", [128, 1024], F32)) for i in range(2)]
        Y = PJ[:, 0, :, :]
        W = PJ[:, 1, :, :]
        RQ, RT = X[1][:, 0:512], X[1][:, 512:1024]

        xt_in, small_in, row_in, cvx, x_in = (sem(n) for n in ("xt_in", "small_in", "row_in", "cvx", "x_in"))
        blk_in = [sem(f"blk_in{i}") for i in range(RING)]
        const_ok, cst_v = sem("const_ok"), sem("cst_v")
        pj_done, pj_act, pj_dve = sem("pj_done"), sem("pj_act"), sem("pj_dve")
        act_chain, dve_chain, pool_chain = sem("act_chain"), sem("dve_chain"), sem("pool_chain")
        soft_part, log_ok, mid_ok, e_ok, qk_ok = (sem(n) for n in ("soft_part", "log_ok", "mid_ok", "e_ok", "qk_ok"))
        var_ok, sd_ok, vn_ok = sem("var_ok"), sem("sd_ok"), sem("vn_ok")
        z_done, ya_ok = sem("z_done"), sem("ya_ok")
        att_done, att_ok, knat_ok, o_done, kv_done, s_ok = (sem(n) for n in (
            "att_done", "att_ok", "knat_ok", "o_done", "kv_done", "s_ok"))
        ss_ok, orms_ok, on_ok, ot_done, yb_ok = (sem(n) for n in ("ss_ok", "orms_ok", "on_ok", "ot_done", "yb_ok"))
        s0_in = [sem("s0_in0"), sem("s0_in1")]
        kpad_ok, outer_done, s0_new, os_done = (sem(n) for n in ("kpad_ok", "outer_done", "s0_new", "os_done"))
        cv_out, stp_out = sem("cv_out"), sem("stp_out")
        s0_out = [sem("s0_out0"), sem("s0_out1")]
        wo_in, ln1_in, keys_in, wpg_in, wpe_in, ln2_in = (sem(n) for n in (
            "wo_in", "ln1_in", "keys_in", "wpg_in", "wpe_in", "ln2_in"))
        xr_in = [sem(f"xr_in{j}") for j in range(NT + 1)]
        wq_in = [sem(f"wq_in{i}") for i in range(4)]
        pt_in = sem("pt_in")
        w_done, x1_ok, tr_done, x1t_ok = (sem(n) for n in ("w_done", "x1_ok", "tr_done", "x1t_ok"))
        q_done, rq_read, qn_ok, qt_done, qt_ok, s_done, route_ok, exp_in, exp_ok = (sem(n) for n in (
            "q_done", "rq_read", "qn_ok", "qt_done", "qt_ok", "s_done", "route_ok", "exp_in", "exp_ok"))
        u_in = [sem(f"u_in{i}") for i in range(UB)]
        v_in = [sem(f"v_in{i}") for i in range(VB)]
        u_used, h_ok, w_ok, diag_ok, v_used, y_done = (sem(n) for n in (
            "u_used", "h_ok", "w_ok", "diag_ok", "v_used", "y_done"))
        y_read, x2_ok, x2t_ok, g_done, g_ok, pe_done, x3_ok = (sem(n) for n in (
            "y_read", "x2_ok", "x2t_ok", "g_done", "g_ok", "pe_done", "x3_ok"))
        it_done, it_ok = sem("it_done"), sem("it_ok")
        xb_done, hs_ok, gs_ok, wpad_ok, ys_done = (sem(n) for n in ("xb_done", "hs_ok", "gs_ok", "wpad_ok", "ys_done"))
        y_out = sem("y_out")

        block = ctx.enter_context(nc.Block())

        def head_at(n):
            return n // PH, n % PH

        def step(n):
            j, h = head_at(max(n, 0))
            ahead = head_at(n + LEAD) if n + LEAD < ITERS else None
            following = head_at(n + LEAD + 1) if n + LEAD + 1 < ITERS else None
            samples = (NT, (n - FIRST_SAMPLE) // 3) if n in range(FIRST_SAMPLE, FIRST_SAMPLE + 3 * PH, 3) else None
            out = []
            at_k = {"dots": 0, "sums": 0}

            def upto(what, k):
                m = n + (what == "dots")
                if at_k[what] < k:
                    if m in range(ITERS):
                        out.append((what, m, at_k[what], k))
                    at_k[what] = k

            parts = []
            if ahead:
                parts += [("route", *ahead, part) for part in range(ROUTE_PARTS)]
            if samples:
                parts.insert(4, ("q", *samples))
                parts += [("route", *samples, part) for part in range(ROUTE_PARTS)]
            if following:
                parts.insert(12 if samples else 5, ("q", *following))
            wide = [("wo", j1) for j1, n1 in WO_AT.items() if n1 == n]
            if h == 2 and j:
                wide = [("pg", j - 1)]
            if n == ITERS - 2:
                wide = [("pg", NT)]
            x1_parts = [("x1", j1, part) for j1, n1 in WO_AT.items() if n1 == n - 1 for part in range(4)]
            for w in wide:
                for part in range(4):
                    parts.insert(min(len(parts), 2 + 3 * part), (*w, part))
            parts = x1_parts + parts
            if h == 3 and j or n == ITERS - 1:
                parts.append(("pe", j - 1 if h == 3 else NT, 3))
            turn = [("x2", j - 1)] if h == 1 and j else []
            turn += [("x1", NT)] if n == FIRST_SAMPLE - 1 else []
            turn += [("x1", j + 1)] if h == 5 and j + 1 < NT else []
            turn += [("x2", NT)] if n == ITERS - 2 else []
            for t in turn:
                parts.insert(4 if t[0] == "x1" else 1, ("turn", *t)) if parts else parts.append(("turn", *t))
            if n == ITERS - 2:
                parts = [("turn", "x2", NT)] + [p for p in parts if p[0] != "turn"]

            if n == SAMPLE_DOTS_AT - 1:
                out.append(("samples",))
            if n == SAMPLE_DOTS_AT:
                out += [("sample dot", b) for b in range(S)]
            if h == 0 and j:
                upto("dots", 3)
                for part in range(4):
                    out.append(("x2", j - 1, part))
                    upto("dots", 4 + part)
                    upto("sums", part)
            if n == SAMPLE_SUMS_AT:
                out.append(("sample sums",))
                upto("dots", 3)
                for part in range(4):
                    out.append(("x2", NT, part))
                    upto("dots", 4 + part)
                    upto("sums", 1 + part)
            d0, s0 = at_k["dots"], at_k["sums"]
            for i, part in enumerate(parts):
                out.append(part)
                f = (i + 1) / (len(parts) + 1)
                upto("sums", s0 + int((TOPK - s0) * f))
                upto("dots", min(TOPK, d0 + int((TOPK - d0) * f) + 1))
            upto("sums", TOPK - 1)
            upto("dots", TOPK)
            upto("sums", TOPK)
            if n + 1 < ITERS:
                out.append(("weights", n + 1))
            return out

        def whole(what, j):
            return [(what, j, part) for part in range(4)]

        PLAN = whole("wo", 0) + whole("x1", 0) + [("turn", "x1", 0), ("q", 0, 0)]
        PLAN += [("route", 0, 0, part) for part in range(ROUTE_PARTS)] + [("q", 0, 1)]
        for n in range(-1, ITERS):
            PLAN += step(n)
        PLAN += whole("x2", NT - 1) + [("turn", "x2", NT - 1)] + whole("pg", NT - 1) + [("pe", NT - 1, 3)]

        def numbers(keys):
            return {k: n for n, k in enumerate(keys)}

        WIDE = numbers(e[:2] for e in PLAN if e[0] in ("wo", "pg", "pe") and e[2] == 3)
        TURN = numbers(e[1:] for e in PLAN if e[0] == "turn")
        ROUTE = numbers(e[1:3] for e in PLAN if e[0] == "q")
        X1 = numbers(e[1] for e in PLAN if e[0] == "x1" and e[2] == 0)
        X2 = numbers(e[1] for e in PLAN if e[0] == "x2" and e[2] == 0)
        SD = numbers([("va", j) for j in range(NT + 1)] + [("o", j) for j in range(NT + 1)]
                     + [e[:2] if e[0] != "route" else e[:3] for e in PLAN
                        if (e[0] in ("x1", "x2") and e[2] == 0) or (e[0] == "route" and e[3] == 0)])
        READ = numbers(e[:2] for e in PLAN if e[0] in ("x1", "x2") and e[2] == 0)
        LAST_X1 = list(X1)[-1]

        def u_number(n, k):
            return n * TOPK + k + (S if n > SAMPLE_DOTS_AT else 0)

        def v_number(n, k):
            return n * TOPK + k + (S if n >= SAMPLE_SUMS_AT else 0)

        U_SAMPLE, V_SAMPLE = (SAMPLE_DOTS_AT + 1) * TOPK, SAMPLE_SUMS_AT * TOPK

        @block.sync
        def _(sp):
            sp.dma_start(wgkl, w_gkl).then_inc(small_in, 16)
            sp.dma_start(xT, x_t).then_inc(xt_in, 16)
            sp.dma_start(wgk, w_gk).then_inc(small_in, 16)
            sp.dma_start(bgk[:, :], b_gk).then_inc(small_in, 16)

            def load_block(i):
                if i >= RING:
                    sp.wait_ge(pj_done, done_with(BLOCKS[i - RING]))
                sp.dma_start(ring[i % RING], w_blk[i]).then_inc(blk_in[i % RING], 16)

            for i in range(RING):
                load_block(i)
            sp.dma_start(wsT, ws_t).then_inc(row_in, 16)
            sp.dma_start(lnvg, lnv_g.partition_broadcast(128)).then_inc(row_in, 16)
            sp.dma_start(lnvb, lnv_b.partition_broadcast(128)).then_inc(row_in, 16)
            sp.dma_start(w00[:, :], ws0.partition_broadcast(S)).then_inc(row_in, 16)
            sp.dma_start(gng[:, :], gn_g).then_inc(row_in, 16)
            for i in range(RING, BLOCKS.index("ga0") + RING):
                load_block(i)
                if i == RING + 1:
                    sp.dma_start(bsrow, b_s).then_inc(row_in, 16)
                if i == RING:
                    sp.dma_start(S0[0], state[0]).then_inc(s0_in[0], 16)
            sp.wait_ge(vn_ok, NT + 1)
            sp.dma_start(cv_p, vaN[:, NT - 1, :]).then_inc(cv_out, 16)
            sp.dma_start(cv_s, vaN[0:S, NT, :]).then_inc(cv_out, 16)
            sp.dma_start(S0[1], state[1]).then_inc(s0_in[1], 16)
            sp.wait_ge(s_ok, NT)
            sp.dma_start(st_p, Sst).then_inc(stp_out, 16)
            for h in range(H):
                sp.wait_ge(s0_new, 8 * (h + 1))
                sp.wait_ge(os_done, h + 1)
                sp.dma_start(st_s[h], S0[h % 2]).then_inc(s0_out[h % 2], 16)
                if h + 2 < H:
                    sp.wait_ge(s0_out[h % 2], 16)
                    sp.dma_start(S0[h % 2], state[h + 2]).then_inc(s0_in[h % 2], 16)
            for i in range(BLOCKS.index("ga0") + RING, len(BLOCKS)):
                load_block(i)
            sp.wait_ge(pj_done, BEFORE_BRANCH)
            sp.wait_ge(yb_ok, NT + 1)
            sp.dma_start(wq[0], w_q[0]).then_inc(wq_in[0], 16)
            sp.dma_start(wq[2], w_q[2]).then_inc(wq_in[2], 16)
            sp.wait_ge(stp_out, 16)
            for i in range(2):
                sp.wait_ge(s0_out[i], 32)
            sp.dma_start(ln1g, ln1_g.partition_broadcast(128)).then_inc(ln1_in, 16)
            for i in range(2):
                sp.wait_ge(pj_done, done_with(BLOCKS[len(BLOCKS) - RING + i]))
                sp.dma_start(ring[i], w_o[i]).then_inc(wo_in, 16)
                if i == 0:
                    sp.dma_start(wq[1], w_q[1]).then_inc(wq_in[1], 16)
            sp.wait_ge(pj_dve, len(JOBS) - BEFORE_BRANCH)
            sp.dma_start(ln1b, ln1_b.partition_broadcast(128)).then_inc(ln1_in, 16)
            for j in range(NT + 1):
                sp.dma_start(x1[0:rows(j), j, :], x_all[cols(j), :]).then_inc(xr_in[j], 16)
            sp.dma_start(keysT, keys_t).then_inc(keys_in, 16)
            sp.dma_start(wq[3], w_q[3]).then_inc(wq_in[3], 16)
            sp.wait_ge(w_done, WIDE["wo", LAST_X1] + 1)
            sp.dma_start(ln2g, ln2_g.partition_broadcast(128)).then_inc(ln2_in, 16)
            sp.dma_start(ln2b, ln2_b.partition_broadcast(128)).then_inc(ln2_in, 16)
            for i in range(2):
                sp.dma_start(ring[i], w_pg[i]).then_inc(wpg_in, 16)
            sp.dma_start(wpe, w_pe).then_inc(wpe_in, 16)
            order = list(X2)
            for i, j in enumerate(order):
                if i:
                    sp.wait_ge(w_done, WIDE["pe", order[i - 1]] + 1)
                sp.dma_start(pT[:, :, 0:rows(j)], p_t[:, :, cols(j)]).then_inc(pt_in, 16)
                sp.wait_ge(x3_ok, i + 1)
                sp.dma_start(y_all[cols(j), :], x1[0:rows(j), j, :]).then_inc(y_out, 16)
            sp.wait_ge(cv_out, 32)
            sp.wait_ge(y_out, 16 * (NT + 1))

        @block.gpsimd
        def _(pool):
            pool.memset(ident[:, :], 0.0).then_inc(pool_chain, 1)
            pool.memset(mask, 1.0).then_inc(pool_chain, 1)
            pool.memset(ones, 1.0).then_inc(const_ok, 1)
            pool.memset(qpad, 0.0).then_inc(const_ok, 1)
            pool.memset(wpad[:, :, :], 0.0).then_inc(const_ok, 1)
            pool.iota(iotau[:, :], pattern=[[1, TOPK]], base=0, channel_multiplier=0).then_inc(pool_chain, 1)
            pool.wait_ge(pool_chain, 3)
            pool.tensor_copy(iota16[:, :], iotau[:, :]).then_inc(const_ok, 1)
            pool.affine_select(out=ident[:, :], in_=ident[:, :], compare_op=ALU.not_equal, fill=1.0, base=0,
                               pattern=[[-1, 128]], channel_multiplier=1).then_inc(const_ok, 1)
            pool.affine_select(out=mask, in_=mask, compare_op=ALU.is_ge, fill=0.0, base=0,
                               pattern=[[1, 128]], channel_multiplier=-1).then_inc(const_ok, 1)

            def gather_u(m, rows_of):
                if m >= UB:
                    pool.wait_ge(u_used, m - UB + 1)
                pool.indirect_dma_start(ubuf[m % UB], None, u_tab, bass.IndirectOffsetOnAxis(rows_of, 0)).then_inc(
                    u_in[m % UB], 16)

            def gather_v(m, rows_of):
                if m >= VB:
                    pool.wait_ge(v_used, m - VB + 1)
                pool.indirect_dma_start(vbuf[m % VB], None, v_tab, bass.IndirectOffsetOnAxis(rows_of, 0)).then_inc(
                    v_in[m % VB], 16)

            pool.wait_ge(route_ok, 1)
            for k in range(TOPK):
                gather_u(u_number(0, k), idx[:, 0, k:k + 1])
            for n in range(ITERS):
                if n + 1 < ITERS:
                    pool.wait_ge(route_ok, ROUTE[(n + 1) // PH, (n + 1) % PH] + 1)
                if n == SAMPLE_DOTS_AT:
                    pool.wait_ge(it_ok, 2)
                    for b in range(S):
                        gather_u(U_SAMPLE + b, idxT[:, b:b + 1])
                if n == SAMPLE_SUMS_AT:
                    for b in range(S):
                        gather_v(V_SAMPLE + b, idxT[:, b:b + 1])
                for k in range(TOPK):
                    if n + 1 < ITERS:
                        gather_u(u_number(n + 1, k), idx[:, (n + 1) % AHEAD, k:k + 1])
                    gather_v(v_number(n, k), idx[:, n % AHEAD, k:k + 1])

        @block.scalar
        def _(act):
            chain = [0]

            def link(ins):
                chain[0] += 1
                ins.then_inc(act_chain, 1)
                act.wait_ge(act_chain, chain[0])

            def deviation(key, p, n, src):
                act.wait_ge(var_ok, SD[key] + 1)
                act.activation(sd[0:p, 0:n], src, ACT.Sqrt).then_inc(sd_ok, 1)

            evac = [0]
            dest = {"q": (qkT, 0), "k": (qkT, 4), "ua": (uaT, 0), "r": (rT, 0), "ga": (gaT, 0), "gb": (gbT, 0)}
            func = {"q": ACT.Copy, "k": ACT.Copy, "ua": ACT.Gelu_apprx_tanh, "r": ACT.Silu,
                    "ga": ACT.Sigmoid, "gb": ACT.Sigmoid, "v": ACT.Copy, "va": ACT.Gelu_apprx_tanh}

            def evacuate(n):
                blk, kind, part = JOBS[n]
                act.wait_ge(pj_done, n + 1)
                half = PJ[:, n % 2, :, 0:HALF]
                if kind == "low":
                    act.activation(gkl.rearrange("p (a b) -> p a b", a=2), half[0:RANK], ACT.Copy).then_inc(pj_act, 1)
                elif kind == "decay":
                    act.activation(logT[:, part, :].rearrange("p (a b) -> p a b", a=2), half, ACT.Identity,
                                   bias=bgk[:, part:part + 1]).then_inc(pj_act, 1)
                elif kind == "columns":
                    name = BLOCKS[blk]
                    t, c0 = dest[name[:-1]]
                    c = c0 + 4 * int(name[-1]) + part
                    act.activation(t[:, c, :].rearrange("p (a b) -> p a b", a=2), half, func[name[:-1]],
                                   scale=DK ** -0.5 if name[:-1] == "q" else 1.0).then_inc(pj_act, 1)
                else:
                    name = BLOCKS[blk]
                    t = vN if name[:-1] == "v" else vaN
                    c = 512 * int(name[-1])
                    p = rows(part)
                    act.activation(t[0:p, part, c:c + 512], PJ[0:p, n % 2, 0, :], func[name[:-1]]).then_inc(pj_act, 1)

            def soft_logs():
                act.wait_ge(pj_act, n_log)
                tmp = rT[:, 0:H, :]
                link(act.activation(tmp, logT, ACT.Abs))
                link(act.activation(tmp, tmp, ACT.Exp, scale=-1.0))
                act.activation(tmp, tmp, ACT.Ln, bias=1.0).then_inc(soft_part, 1)

            def decays():
                for j in range(NT):
                    act.wait_ge(mid_ok, j + 1)
                    if j:
                        act.wait_ge(qk_ok, j)
                    for h in range(H):
                        act.activation(Ep[:, h, :], logT[:, h, cols(j)], ACT.Exp, scale=1.0 / TAU,
                                       bias=mid[:, j, 0, h:h + 1])
                        last = act.activation(Em[:, h, :], logT[:, h, cols(j)], ACT.Exp, scale=-1.0 / TAU,
                                              bias=mid[:, j, 1, h:h + 1])
                    last.then_inc(e_ok, 1)
                act.wait_ge(mid_ok, NT + 1)
                link(act.activation(fac[:, :, :], fac[:, :, :], ACT.Exp, scale=1.0 / TAU))
                act.activation(egT[:, :, :], logT[:, :, T:N], ACT.Exp, scale=1.0 / TAU).then_inc(e_ok, 1)

            n_log = max(n for n, (_, kind, _) in enumerate(JOBS) if kind == "decay") + 1
            n_va = done_with("va1")
            n_ua = done_with("ua1")
            for n in range(n_log):
                evacuate(n)
            soft_logs()
            for n in range(n_log, done_with("v0")):
                evacuate(n)
            decays()
            for n in range(done_with("v0"), n_va):
                evacuate(n)
            for n in range(n_va, n_ua):
                evacuate(n)
            for j in range(NT + 1):
                deviation(("va", j), rows(j), 1, mv[0:rows(j), 0, 1:2])
            for n in range(n_ua, BEFORE_GATES):
                evacuate(n)

            def gla_norm(j):
                p = rows(j)
                act.wait_ge(o_done, j + 1)
                if j:
                    act.wait_ge(ot_done, j)
                for h in range(H):
                    last = act.activation(oN[0:p, h, :], X[1][0:p, h * DV:(h + 1) * DV], ACT.Square,
                                          accum_out=ss[0:p, h:h + 1])
                last.then_inc(ss_ok, 1)
                deviation(("o", j), p, H, rstd[0:p, 0:H])
                act.wait_ge(orms_ok, j + 1)
                for h in range(H):
                    last = act.activation(oN[0:p, h, :], X[1][0:p, h * DV:(h + 1) * DV], ACT.Copy,
                                          scale=rstd[0:p, h:h + 1])
                last.then_inc(on_ok, 1)

            act.wait_ge(qk_ok, NT)
            for j in range(NT):
                act.wait_ge(att_done, j + 1)
                act.activation(knat, X[0][:, 512:1024].rearrange("p (a b) -> p a b", a=H), ACT.Copy).then_inc(knat_ok, 1)
                gla_norm(j)
            act.wait_ge(att_done, NT + 1)
            act.wait_ge(kv_done, NT)
            act.activation(knat[0:S], X[0][0:S, 0:512].rearrange("p (a b) -> p a b", a=H), ACT.Copy).then_inc(knat_ok, 1)
            gla_norm(NT)
            act.wait_ge(cv_out, 32)
            for n in range(BEFORE_GATES, BEFORE_BRANCH):
                evacuate(n)

            def route(j, h, part):
                p, r = rows(j), ROUTE[j, h]
                if part == 0:
                    deviation(("route", j, h), p, 2, mv[0:p, :, 1:2].rearrange("p a b -> p (a b)"))
                elif part == 1:
                    act.wait_ge(qt_done, r + 1)
                    act.activation(qT[:, :, 0:p], RT[:, 0:256].rearrange("p (a b) -> p a b", a=2)[:, :, 0:p],
                                   ACT.Copy).then_inc(qt_ok, 1)
                elif part == 4:
                    act.wait_ge(exp_in, r + 1)
                    act.activation(ex[0:p, :], top[0:p, :], ACT.Exp, bias=soft[0:p, 0:1],
                                   accum_out=soft[0:p, 1:2]).then_inc(exp_ok, 1)

            def diagonals(n, ks):
                for k in ks:
                    m = n * TOPK + k
                    if k == 0:
                        act.wait_ge(w_ok, n + 1)
                    if m >= DB:
                        act.wait_ge(v_used, v_number(*divmod(m - DB, TOPK)) + 1)
                    act.activation(diag[m % DB], ident[:, :], ACT.Copy, scale=wgt[:, n % 3, k:k + 1]).then_inc(diag_ok, 1)

            for e in PLAN:
                what, args = e[0], e[1:]
                if what in ("x1", "x2"):
                    if args[1] == 0:
                        deviation(e[:2], rows(args[0]), 1, mv[0:rows(args[0]), 0, 1:2])
                elif what == "turn":
                    name, j = args
                    p = rows(j)
                    act.wait_ge(tr_done, TURN[args] + 1)
                    dst = x1Ts if args == ("x1", NT) else (x1T if name == "x1" else x2T)[:, :, 0:p]
                    act.activation(dst, X[0][:, :].rearrange("p (a b) -> p a b", a=KC)[:, :, 0:p], ACT.Copy).then_inc(
                        x1t_ok, 1)
                elif what == "route":
                    route(*args)
                elif what == "sums":
                    diagonals(args[0], range(args[1], args[2]))
                elif what == "weights":
                    n = args[0]
                    act.wait_ge(h_ok, n + 1)
                    act.activation(hact[:, n % 2, :], hraw[:, n % 2, :], ACT.Gelu_apprx_tanh).then_inc(g_ok, 1)
                elif what == "pg" and args[1] == 3:
                    j = args[0]
                    p = rows(j)
                    act.wait_ge(w_done, WIDE[e[:2]] + 1)
                    if X2[j]:
                        act.wait_ge(x3_ok, X2[j])
                    act.activation(sg[0:p, :].rearrange("p (a b) -> p a b", a=2), W[0:p], ACT.Sigmoid).then_inc(g_done, 1)
                elif what == "samples":
                    act.wait_ge(it_done, 2)
                    act.activation(gateT[:, :], X[0][:, 512:512 + S], ACT.Copy).then_inc(it_ok, 1)
                elif what == "sample dot" and args[0] == S - 1:
                    act.wait_ge(hs_ok, 1)
                    act.activation(aS[:, :], hS[:, :], ACT.Gelu_apprx_tanh).then_inc(gs_ok, 1)

        @block.vector
        def _(v):
            chain = [0]

            def link(ins):
                chain[0] += 1
                ins.then_inc(dve_chain, 1)
                v.wait_ge(dve_chain, chain[0])

            def row_stats(src, p):
                v.bn_stats(bn[0:p, 0, :], src[:, 0:512])
                link(v.bn_stats(bn[0:p, 1, :], src[:, 512:1024]))
                link(v.bn_aggr(mv[0:p, 0, :], bn[0:p].rearrange("p a b -> p (a b)")))
                v.tensor_scalar(mv[0:p, 0, 1:2], mv[0:p, 0, 1:2], EPS, None, ALU.add).then_inc(var_ok, 1)

            def inverse(key, p, n):
                v.wait_ge(sd_ok, SD[key] + 1)
                return v.reciprocal(rstd[0:p, 0:n], sd[0:p, 0:n])

            def layernorm(t, key, g, b, done):
                p = rows(key[1])
                row_stats(t, p)
                link(inverse(key, p, 1))
                link(v.tensor_scalar(t, t, mv[0:p, 0, 0:1], rstd[0:p, 0:1], ALU.subtract, ALU.mult))
                link(v.tensor_tensor(t, t, g[0:p], ALU.mult))
                v.tensor_tensor(t, t, b[0:p], ALU.add).then_inc(done, 1)

            v.wait_ge(const_ok, 6)
            v.wait_ge(soft_part, 1)
            link(v.scalar_tensor_tensor(out=logT, in0=logT, scalar=0.0, in1=rT[:, 0:H, :], op0=ALU.min,
                                        op1=ALU.subtract))
            for j in range(NT):
                for h in range(H):
                    c = logT[:, h, cols(j)]
                    last = v.tensor_tensor_scan(c, ones, c, 0.0, ALU.mult, ALU.add)
                    chain[0] += 1
                    last.then_inc(dve_chain, 1)
            v.wait_ge(dve_chain, chain[0])
            for j in range(NT):
                m = logT[:, :, 128 * j + 63:128 * j + 64].rearrange("p a b -> p (a b)")
                link(v.tensor_scalar(mid[:, j, 0, :], m, -1.0 / TAU, None, ALU.mult))
                v.tensor_scalar(mid[:, j, 1, :], m, 1.0 / TAU, None, ALU.mult).then_inc(mid_ok, 1)
            for j in range(NT):
                m = logT[:, :, 128 * j + 63:128 * j + 64].rearrange("p a b -> p (a b)")
                e = logT[:, :, 128 * j + 127:128 * j + 128].rearrange("p a b -> p (a b)")
                ins = v.tensor_tensor(fac[:, j, :], e, m, ALU.subtract)
                if j + 1 < NT:
                    link(ins)
                    m2 = logT[:, :, 128 * j + 191:128 * j + 192].rearrange("p a b -> p (a b)")
                    link(v.tensor_tensor(fac[:, j, :], fac[:, j, :], m2, ALU.add))
            ins.then_inc(mid_ok, 1)
            v.wait_ge(pj_act, done_with("k0"))
            for j in range(NT):
                v.wait_ge(e_ok, j + 1)
                v.tensor_tensor(qkT[:, 0:H, cols(j)], qkT[:, 0:H, cols(j)], Ep, ALU.mult)
                link(v.tensor_tensor(qkT[:, H:2 * H, cols(j)], qkT[:, H:2 * H, cols(j)], Em, ALU.mult))
                v.sem_inc(qk_ok, 1)
            v.wait_ge(row_in, 16 * 6)
            link(v.tensor_tensor(wsT, wsT, mask.unsqueeze(1).broadcast_to([128, G, 128]), ALU.mult))
            v.tensor_copy(bs0, bsrow.rearrange("p (a b) -> p a b", a=G)[:, :, 0:1].broadcast_to([1, G, S]))
            link(v.tensor_tensor(dg, ident[0:S, 0:S].unsqueeze(1).broadcast_to([S, G, S]),
                                 w00[:, :].unsqueeze(2).broadcast_to([S, G, S]), ALU.mult))
            for j in range(NT + 1):
                n = [i for i, (b, _, part) in enumerate(JOBS)
                     if b is not None and BLOCKS[b] == "va1" and part == j][0]
                v.wait_ge(pj_act, n + 1)
                layernorm(vaN[0:rows(j), j, :], ("va", j), lnvg, lnvb, vn_ok)

            def gate_values(j):
                v.wait_ge(z_done, j + 1)
                if j == 0:
                    v.wait_ge(pj_act, done_with("ua1"))
                p = rows(j)
                z = X[j % 2][:, 0:G * p].rearrange("p (a b) -> p a b", a=G)
                v.tensor_tensor(uaT[:, :, cols(j)], uaT[:, :, cols(j)], z, ALU.mult).then_inc(ya_ok, 1)

            for j in range(NT + 1):
                gate_values(j)

            def output_stats(j):
                p = rows(j)
                v.wait_ge(ss_ok, j + 1)
                v.tensor_scalar(rstd[0:p, 0:H], ss[0:p, 0:H], 1.0 / DV, EPS, ALU.mult, ALU.add).then_inc(var_ok, 1)
                inverse(("o", j), p, H).then_inc(orms_ok, 1)

            def branch_b(j):
                p = rows(j)
                v.wait_ge(ot_done, j + 1)
                v.wait_ge(pj_act, BEFORE_GATES)
                t = PJ[:, j % 2, :, :].rearrange("p a (b c) -> p (a b) c", b=4)
                for q in range(2):
                    dst = rT[:, q::2, cols(j)]
                    last = v.scalar_tensor_tensor(out=dst, in0=t[:, q::2, 0:p], scalar=gng[:, q:q + 1], in1=dst,
                                                  op0=ALU.mult, op1=ALU.mult)
                    chain[0] += 1
                    last.then_inc(dve_chain, 1)
                v.wait_ge(dve_chain, chain[0])
                v.sem_inc(yb_ok, 1)

            for j in range(NT):
                v.wait_ge(att_done, j + 1)
                if j:
                    v.wait_ge(o_done, j)
                v.tensor_tensor(attS, X[0][:, 0:512].rearrange("p (a b) -> p a b", a=H),
                                mask.unsqueeze(1).broadcast_to([128, H, 128]), ALU.mult).then_inc(att_ok, 1)
                v.wait_ge(kv_done, j + 1)
                kv = X[0][:, :].rearrange("p (a b) -> p a b", a=H)
                v.wait_ge(e_ok, NT + 1)
                src = kv
                if j:
                    v.wait_ge(o_done, j + 1)
                    link(v.tensor_tensor(Sst, kv, Sst, ALU.add))
                    src = Sst
                for h in range(H):
                    last = v.tensor_scalar(Sst[:, h, :], src[:, h, :], fac[:, j, h:h + 1], None, ALU.mult)
                    chain[0] += 1
                    last.then_inc(dve_chain, 1)
                v.wait_ge(dve_chain, chain[0])
                v.sem_inc(s_ok, 1)
                output_stats(j)
                if j:
                    branch_b(j - 1)
            v.wait_ge(knat_ok, NT + 1)
            for h in range(H):
                if h:
                    v.wait_ge(outer_done, 2 * h)
                v.tensor_tensor(kpad[0:S], knat[0:S, h, :].unsqueeze(1).broadcast_to([S, S, 128]),
                                ident[0:S, 0:S].unsqueeze(2).broadcast_to([S, S, 128]), ALU.mult).then_inc(kpad_ok, 1)
                if h:
                    v.wait_ge(os_done, h)
                v.tensor_copy(qpad.rearrange("p a b -> p (a b)")[:, 0:S * S:S + 1], qkT[:, h, T:N]).then_inc(kpad_ok, 1)
                v.wait_ge(s0_in[h % 2], 16 * (h // 2 + 1))
                for b in range(S):
                    if b % 4 == 0:
                        v.wait_ge(outer_done, 2 * h + b // 4 + 1)
                    v.scalar_tensor_tensor(out=S0[h % 2][:, b, :], in0=S0[h % 2][:, b, :], scalar=egT[:, h, b:b + 1],
                                           in1=X[0][:, (b % 4) * DV:(b % 4 + 1) * DV], op0=ALU.mult,
                                           op1=ALU.add).then_inc(s0_new, 1)
                if h == 0:
                    branch_b(NT - 1)
            output_stats(NT)
            branch_b(NT)
            v.wait_ge(pj_act, BEFORE_BRANCH)
            for n in range(BEFORE_BRANCH, len(JOBS)):
                blk, _, part = JOBS[n]
                name = BLOCKS[blk]
                c = 4 * int(name[-1]) + part
                ga, gb = (t[:, c, :].rearrange("p (a b) -> p a b", a=2) for t in (gaT, gbT))
                v.wait_ge(pj_done, n + 1)
                half = PJ[:, n % 2, :, 0:HALF]
                if name[:-1] == "bra":
                    v.tensor_tensor(ga, ga, half, ALU.mult).then_inc(pj_dve, 1)
                else:
                    v.wait_ge(pj_dve, n - BEFORE_BRANCH)
                    link(v.tensor_tensor(gb, gb, half, ALU.mult))
                    v.tensor_tensor(ga, ga, gb, ALU.add).then_inc(pj_dve, 1)

            def scaled_add(dst, src):
                p = dst.shape[0]
                chain[0] += 1
                v.scalar_tensor_tensor(out=dst.rearrange("p (a b) -> p a b", a=2),
                                       in0=dst.rearrange("p (a b) -> p a b", a=2), scalar=ALPHA, in1=src[0:p],
                                       op0=ALU.mult, op1=ALU.add).then_inc(dve_chain, 1)
                v.wait_ge(dve_chain, chain[0])
                v.sem_inc(y_read, 1)

            def top16(vals16, inds16, src):
                link(v.max(vals16[:, 0:8], src))
                link(v.max_index(inds16[:, 0:8], vals16[:, 0:8], src))
                link(v.match_replace(src, vals16[:, 0:8], src, NEG))
                link(v.max(vals16[:, 8:16], src))
                link(v.max_index(inds16[:, 8:16], vals16[:, 8:16], src))

            def route(j, h, part):
                p, r = rows(j), ROUTE[j, h]
                if part == 0:
                    v.wait_ge(q_done, r + 1)
                    v.bn_stats(bn[0:p, 0, :], RQ[0:p, 0:128])
                    link(v.bn_stats(bn[0:p, 1, :], RQ[0:p, 128:256]))
                    v.bn_aggr(mv[0:p, 0, :], bn[0:p, 0, :])
                    link(v.bn_aggr(mv[0:p, 1, :], bn[0:p, 1, :]))
                    v.tensor_scalar(mv[0:p, :, 1:2], mv[0:p, :, 1:2], EPS, None, ALU.add).then_inc(var_ok, 1)
                elif part == 1:
                    link(inverse(("route", j, h), p, 2))
                    for i in range(2):
                        last = v.tensor_scalar(qN[0:p, i, :], RQ[0:p, 128 * i:128 * i + 128], mv[0:p, i, 0:1],
                                               rstd[0:p, i:i + 1], ALU.subtract, ALU.mult)
                        last.then_inc(qn_ok, 1)
                elif part == 2:
                    v.wait_ge(s_done, r + 1)
                    v.tensor_copy(scores[0:p], RQ[0:p, 256:512].rearrange("p (a b) -> p a b", a=2)).then_inc(rq_read, 1)
                    v.wait_ge(rq_read, r + 1)
                    top16(vals[0:p, 0, :], inds[0:p, 0, :], scores[0:p, 0, :])
                elif part == 3:
                    top16(vals[0:p, 1, :], inds[0:p, 1, :], scores[0:p, 1, :])
                    v.tensor_copy(indf[0:p], inds[0:p])
                elif part == 4:
                    link(v.tensor_tensor(cand[0:p].rearrange("p (a b) -> p a b", a=TOPK),
                                         vals[0:p, 0, :].unsqueeze(2).broadcast_to([p, TOPK, TOPK]),
                                         vals[0:p, 1, :].unsqueeze(1).broadcast_to([p, TOPK, TOPK]), ALU.add))
                    top16(top[0:p], topi[0:p], cand[0:p])
                    link(v.tensor_scalar(soft[0:p, 0:1], top[0:p, 0:1], -1.0, None, ALU.mult))
                    v.sem_inc(exp_in, 1)
                elif part == 5:
                    v.tensor_scalar(abu[0:p, 0, :], topi[0:p], 4, None, ALU.logical_shift_right)
                    link(v.tensor_scalar(abu[0:p, 1, :], topi[0:p], 15, None, ALU.bitwise_and))
                    link(v.tensor_copy(abf[0:p], abu[0:p]))
                    link(v.tensor_tensor(onehot[0:p], abf[0:p].unsqueeze(3).broadcast_to([p, 2, TOPK, TOPK]),
                                         iota16[0:p].unsqueeze(1).unsqueeze(1).broadcast_to([p, 2, TOPK, TOPK]),
                                         ALU.is_equal))
                    link(v.tensor_tensor(onehot[0:p], onehot[0:p],
                                         indf[0:p].unsqueeze(2).broadcast_to([p, 2, TOPK, TOPK]), ALU.mult))
                    link(v.tensor_reduce(e12[0:p], onehot[0:p], AX.X, ALU.add))
                else:
                    s = slice(h * TOPK, (h + 1) * TOPK)
                    v.wait_ge(exp_ok, r + 1)
                    link(v.reciprocal(soft[0:p, 2:3], soft[0:p, 1:2]))
                    m = (j * PH + h) % AHEAD
                    gate_out, idx_out = (gates[:, m, :], idx[:, m, :]) if j < NT else (gatesS[:, s], idxf[:, s])
                    v.tensor_scalar(gate_out[0:p], ex[0:p, :], soft[0:p, 2:3], None, ALU.mult)
                    link(v.scalar_tensor_tensor(out=idx_out[0:p], in0=e12[0:p, 0, :], scalar=float(NK),
                                                in1=e12[0:p, 1, :], op0=ALU.mult, op1=ALU.add))
                    v.sem_inc(route_ok, 1)

            def dots(n, ks):
                for k in ks:
                    m = u_number(n, k)
                    v.wait_ge(u_in[m % UB], 16 * (m // UB + 1))
                    t = ubuf[m % UB]
                    last = v.tensor_tensor_reduce(out=t, in0=t, in1=x1[:, n // PH, :], scale=1.0, scalar=0.0,
                                                  op0=ALU.mult, op1=ALU.add, accum_out=hraw[:, n % 2, k:k + 1])
                    last.then_inc(u_used, 1)
                if TOPK - 1 in ks:
                    v.wait_ge(u_used, u_number(n, TOPK - 1) + 1)
                    v.sem_inc(h_ok, 1)

            def weights(n):
                if n >= 3:
                    v.wait_ge(diag_ok, (n - 2) * TOPK)
                v.wait_ge(g_ok, n + 1)
                v.tensor_tensor(wgt[:, n % 3, :], hact[:, n % 2, :], gates[:, n % AHEAD, :], ALU.mult).then_inc(
                    w_ok, 1)

            def sample_dot(b):
                m = U_SAMPLE + b
                v.wait_ge(u_in[m % UB], 16 * (m // UB + 1))
                v.wait_ge(xb_done, b + 1)
                t = ubuf[m % UB].rearrange("p (a b) -> p a b", a=2)
                v.tensor_tensor_reduce(out=t, in0=t, in1=X[0][:, :].rearrange("p (a b) -> p a b", a=2), scale=1.0,
                                       scalar=0.0, op0=ALU.mult, op1=ALU.add,
                                       accum_out=hS[:, b:b + 1]).then_inc(u_used, 1)
                if b == S - 1:
                    v.wait_ge(u_used, U_SAMPLE + S)
                    v.sem_inc(hs_ok, 1)

            def sample_weights():
                v.wait_ge(gs_ok, 1)
                v.wait_ge(it_ok, 2)
                v.tensor_tensor(wpad[:, :, :].rearrange("p a b -> p (a b)")[:, 0:S * S:S + 1], aS[:, :], gateT[:, :],
                                ALU.mult).then_inc(wpad_ok, 1)

            def residual_norm(what, j, part):
                p = rows(j)
                t = x1[0:p, j, :]
                g, b, done = (ln1g, ln1b, x1_ok) if what == "x1" else (ln2g, ln2b, x2_ok)
                if part == 0:
                    if what == "x1":
                        v.wait_ge(ln1_in, 32)
                        v.wait_ge(xr_in[j], 16)
                        v.wait_ge(w_done, WIDE["wo", j] + 1)
                        scaled_add(t, W)
                    else:
                        v.wait_ge(ln2_in, 32)
                        if j < NT:
                            v.wait_ge(y_done, j + 1)
                            scaled_add(t, Y)
                        else:
                            v.wait_ge(ys_done, 1)
                            scaled_add(t, W)
                    row_stats(t, p)
                elif part == 1:
                    link(inverse((what, j), p, 1))
                    link(v.tensor_scalar(t, t, mv[0:p, 0, 0:1], rstd[0:p, 0:1], ALU.subtract, ALU.mult))
                elif part == 2:
                    link(v.tensor_tensor(t, t, g[0:p], ALU.mult))
                else:
                    v.tensor_tensor(t, t, b[0:p], ALU.add).then_inc(done, 1)

            for e in PLAN:
                what, args = e[0], e[1:]
                if what in ("x1", "x2"):
                    residual_norm(*e)
                elif what == "route":
                    route(*args)
                elif what == "dots":
                    dots(args[0], range(args[1], args[2]))
                elif what == "weights":
                    weights(args[0])
                elif what == "pe":
                    j = args[0]
                    p = rows(j)
                    v.wait_ge(g_done, X2[j] + 1)
                    v.wait_ge(w_done, WIDE[e[:2]] + 1)
                    s2 = sg[0:p, :].rearrange("p (a b) -> p a b", a=2)
                    link(v.tensor_tensor(s2, s2, W[0:p], ALU.mult))
                    v.tensor_tensor(x1[0:p, j, :], x1[0:p, j, :], sg[0:p, :], ALU.add).then_inc(x3_ok, 1)
                elif what == "samples":
                    v.wait_ge(it_done, 2)
                    v.tensor_copy(idxT[:, :], X[0][:, 0:S]).then_inc(it_ok, 1)
                elif what == "sample dot":
                    sample_dot(*args)
                elif what == "sample sums":
                    sample_weights()

        @block.tensor
        def _(pe):
            mm = nc.tensor.matmul
            pe.wait_ge(const_ok, 6)
            pe.wait_ge(small_in, 48)
            pe.wait_ge(xt_in, 16)

            def project(n):
                blk, kind, part = JOBS[n]
                if n >= 2:
                    if n - 2 < BEFORE_BRANCH:
                        pe.wait_ge(pj_act, n - 1)
                    else:
                        pe.wait_ge(pj_dve, n - 1 - BEFORE_BRANCH)
                if blk is not None:
                    pe.wait_ge(blk_in[blk % RING], 16 * (blk // RING + 1))
                out = PJ[:, n % 2, :, :]
                if kind == "natural":
                    p = rows(part)
                    for c in range(KC):
                        last = mm(out[0:p, 0, :], xT[:, c, cols(part)], ring[blk % RING][:, c, :],
                                  start=c == 0, stop=c == KC - 1)
                elif kind == "decay":
                    pe.wait_ge(pj_act, 1)
                    for s in range(2):
                        last = mm(out[:, s, 0:HALF], wgk[:, part * DK:(part + 1) * DK], gkl[:, s * HALF:(s + 1) * HALF],
                                  start=True, stop=True)
                else:
                    src = {"bra": uaT, "brb": rT}.get(BLOCKS[blk][:-1] if blk is not None else "", xT)
                    for c in range(KC):
                        w = wgkl[:, c, :] if kind == "low" else ring[blk % RING][:, c, part * 128:(part + 1) * 128]
                        for s in range(2):
                            last = mm(out[0:RANK if kind == "low" else 128, s, 0:HALF], w,
                                      src[:, c, s * HALF:(s + 1) * HALF], start=c == 0, stop=c == KC - 1)
                last.then_inc(pj_done, 1)

            for n in range(BEFORE_GATES):
                project(n)

            for j in range(NT + 1):
                p = rows(j)
                pe.wait_ge(vn_ok, j + 1)
                if j >= 2:
                    pe.wait_ge(ya_ok, j - 1)
                z = X[j % 2][:, 0:G * p].rearrange("p (a b) -> p a b", a=G)
                for g in range(G):
                    w = wsT[:, g, :] if j < NT else dg[:, g, :]
                    b = bsrow[:, g * 128:(g + 1) * 128] if j < NT else bs0[:, g, :]
                    mm(z[:, g, :], vaN[0:p, j, g * 128:(g + 1) * 128], w, start=True, stop=False)
                    last = mm(z[:, g, :], ones[0:1, :], b, start=False, stop=True)
                last.then_inc(z_done, 1)

            def turn_output(j):
                p = rows(j)
                pe.wait_ge(on_ok, j + 1)
                pe.wait_ge(pj_act, BEFORE_GATES)
                if j >= 2:
                    pe.wait_ge(yb_ok, j - 1)
                for c in range(KC):
                    last = nc.tensor.transpose(PJ[:, j % 2, c // 4, (c % 4) * 128:(c % 4) * 128 + p],
                                               oN[0:p, c // 2, (c % 2) * 128:(c % 2 + 1) * 128], ident[0:p, 0:p])
                last.then_inc(ot_done, 1)

            pe.wait_ge(ya_ok, NT + 1)
            for j in range(NT):
                pe.wait_ge(qk_ok, j + 1)
                if j:
                    pe.wait_ge(s_ok, j)
                for h in range(H):
                    mm(X[0][:, h * 128:(h + 1) * 128], qkT[:, H + h, cols(j)], qkT[:, h, cols(j)], start=True, stop=True)
                for h in range(H):
                    last = nc.tensor.transpose(X[0][:, 512 + h * 128:640 + h * 128], qkT[:, H + h, cols(j)], ident[:, :])
                last.then_inc(att_done, 1)
                if j:
                    turn_output(j - 1)
                pe.wait_ge(att_ok, j + 1)
                for h in range(H):
                    o_h = X[1][:, h * DV:(h + 1) * DV]
                    last = mm(o_h, attS[:, h, :], vN[:, j, h * DV:(h + 1) * DV], start=True, stop=j == 0)
                    if j:
                        last = mm(o_h, qkT[:, h, cols(j)], Sst[:, h, :], start=False, stop=True)
                last.then_inc(o_done, 1)
                pe.wait_ge(knat_ok, j + 1)
                for h in range(H):
                    last = mm(X[0][:, h * DV:(h + 1) * DV], knat[:, h, :], vN[:, j, h * DV:(h + 1) * DV],
                              start=True, stop=True)
                last.then_inc(kv_done, 1)
            pe.wait_ge(s_ok, NT)
            for h in range(H):
                last = nc.tensor.transpose(X[0][0:S, h * 128:(h + 1) * 128], qkT[:, H + h, T:N], ident[:, :])
            last.then_inc(att_done, 1)
            turn_output(NT - 1)
            pe.wait_ge(knat_ok, NT + 1)
            for h in range(H):
                pe.wait_ge(kpad_ok, 2 * h + 2)
                for b in range(S):
                    if b % 4 == 0 and 8 * h + b:
                        pe.wait_ge(s0_new, 8 * h + b)
                    last = mm(X[0][:, (b % 4) * DV:(b % 4 + 1) * DV], kpad[0:S, b, :], vN[0:S, NT, h * DV:(h + 1) * DV],
                              start=True, stop=True)
                    if b % 4 == 3:
                        last.then_inc(outer_done, 1)
                pe.wait_ge(s0_new, 8 * h + 8)
                for b in range(S):
                    last = mm(X[1][0:S, h * DV:(h + 1) * DV], qpad[:, b, :], S0[h % 2][:, b, :],
                              start=b == 0, stop=b == S - 1)
                last.then_inc(os_done, 1)
            pe.wait_ge(os_done, H)
            pe.sem_inc(o_done, 1)
            turn_output(NT)
            pe.wait_ge(yb_ok, NT + 1)
            for n in range(BEFORE_GATES, len(JOBS)):
                project(n)

            def wide(what, j, part):
                p = rows(j)
                if what == "wo":
                    if part == 0 and X1[j]:
                        pe.wait_ge(y_read, READ["x1", list(X1)[X1[j] - 1]] + 1)
                    lhs = [gaT[:, c, cols(j)] for c in range(KC)]
                    rhs = [[ring[s][:, c, :] for c in range(KC)] for s in range(2)]
                elif what == "pg":
                    if part == 0:
                        pe.wait_ge(y_read, READ["x1", LAST_X1] + 1)
                        if j == NT:
                            pe.wait_ge(y_read, READ["x2", NT] + 1)
                        if X2[j]:
                            pe.wait_ge(x3_ok, X2[j])
                        pe.wait_ge(x1t_ok, TURN["x2", j] + 1)
                        pe.wait_ge(wpg_in, 32)
                    lhs = [x2T[:, c, 0:p] for c in range(KC)]
                    rhs = [[ring[s][:, c, :] for c in range(KC)] for s in range(2)]
                else:
                    pe.wait_ge(g_done, X2[j] + 1)
                    pe.wait_ge(wpe_in, 16)
                    pe.wait_ge(pt_in, 16 * (X2[j] + 1))
                    lhs = [pT[:, c, 0:p] for c in range(2)]
                    rhs = [[wpe[:, c, 512 * s:512 * s + 512] for c in range(2)] for s in range(2)]
                chunks = range(2) if what == "pe" else range(2 * part, 2 * part + 2)
                for c in chunks:
                    for s in range(2):
                        last = mm(W[0:p, s, :], lhs[c], rhs[s][c], start=c == 0, stop=c == len(lhs) - 1)
                if part == 3:
                    last.then_inc(w_done, 1)

            def turn(what, j):
                p = rows(j)
                if what == "x1":
                    pe.wait_ge(x1_ok, X1[j] + 1)
                else:
                    pe.wait_ge(x2_ok, X2[j] + 1)
                if TURN[what, j]:
                    pe.wait_ge(x1t_ok, TURN[what, j])
                if (what, j) == ("x2", NT):
                    pe.wait_ge(u_used, U_SAMPLE + S)
                for c in range(KC):
                    last = nc.tensor.transpose(X[0][:, c * 128:c * 128 + p], x1[0:p, j, c * 128:(c + 1) * 128],
                                               ident[0:p, 0:p])
                last.then_inc(tr_done, 1)

            def queries(j, h):
                p, r = rows(j), ROUTE[j, h]
                pe.wait_ge(x1t_ok, TURN["x1", j] + 1)
                if r:
                    pe.wait_ge(rq_read, r)
                pe.wait_ge(wq_in[h // 2], 16)
                src = x1T if j < NT else x1Ts
                for c in range(KC):
                    last = mm(RQ[0:p, 0:256], src[:, c, 0:p], wq[h // 2][:, c, (h % 2) * 256:(h % 2 + 1) * 256],
                              start=c == 0, stop=c == KC - 1)
                last.then_inc(q_done, 1)

            def route(j, h, part):
                p, r = rows(j), ROUTE[j, h]
                if part == 1:
                    pe.wait_ge(qn_ok, 2 * r + 2)
                    for i in range(2):
                        last = nc.tensor.transpose(RT[:, i * 128:i * 128 + p], qN[0:p, i, :], ident[0:p, 0:p])
                    last.then_inc(qt_done, 1)
                elif part == 2:
                    pe.wait_ge(qt_ok, r + 1)
                    pe.wait_ge(keys_in, 16)
                    for i in range(2):
                        last = mm(RQ[0:p, 256 + i * 128:384 + i * 128], qT[:, i, 0:p], keysT[:, 2 * h + i, :],
                                  start=True, stop=True)
                    last.then_inc(s_done, 1)

            def sums(n, ks):
                for k in ks:
                    m, d = v_number(n, k), n * TOPK + k
                    first, final = d % SLOTS == 0, d % SLOTS == SLOTS - 1
                    if first and n:
                        pe.wait_ge(y_read, READ["x2", n // PH - 1] + 1)
                    pe.wait_ge(v_in[m % VB], 16 * (m // VB + 1))
                    pe.wait_ge(diag_ok, d + 1)
                    for s in range(2):
                        last = mm(Y[:, s, :], diag[d % DB], vbuf[m % VB][:, 512 * s:512 * s + 512], start=first, stop=final)
                    last.then_inc(v_used, 1)
                    if final:
                        pe.wait_ge(v_used, m + 1)
                        pe.sem_inc(y_done, 1)

            def sample_row(b):
                if b == 0:
                    pe.wait_ge(it_ok, 2)
                else:
                    pe.wait_ge(u_used, U_SAMPLE + b)
                for s in range(2):
                    last = mm(X[0][:, 512 * s:512 * s + 512], ident[0:S, b:b + 1].broadcast_to([S, 128]),
                              x1[0:S, NT, 512 * s:512 * s + 512], start=True, stop=True)
                last.then_inc(xb_done, 1)

            def sample_sums():
                pe.wait_ge(wpad_ok, 1)
                pe.wait_ge(x3_ok, NT - 1)
                for b in range(S):
                    m = V_SAMPLE + b
                    pe.wait_ge(v_in[m % VB], 16 * (m // VB + 1))
                    for s in range(2):
                        last = mm(W[0:S, s, :], wpad[:, b, :], vbuf[m % VB][:, 512 * s:512 * s + 512],
                                  start=b == 0, stop=b == S - 1)
                    last.then_inc(v_used, 1)
                pe.wait_ge(v_used, V_SAMPLE + S)
                pe.sem_inc(ys_done, 1)

            pe.wait_ge(pj_dve, len(JOBS) - BEFORE_BRANCH)
            pe.wait_ge(wo_in, 32)
            for e in PLAN:
                what, args = e[0], e[1:]
                if what in ("wo", "pg", "pe"):
                    wide(*e)
                elif what == "turn":
                    turn(*args)
                elif what == "q":
                    queries(*args)
                elif what == "route":
                    route(*args)
                elif what == "sums":
                    sums(args[0], range(args[1], args[2]))
                elif what == "samples":
                    pe.wait_ge(route_ok, ROUTE[NT, PH - 1] + 1)
                    pe.wait_ge(x1t_ok, TURN["x2", NT - 2] + 1)
                    nc.tensor.transpose(X[0][:, 0:S], idxf, ident[0:S, 0:S]).then_inc(it_done, 1)
                    nc.tensor.transpose(X[0][:, 512:512 + S], gatesS, ident[0:S, 0:S]).then_inc(it_done, 1)
                elif what == "sample dot":
                    sample_row(*args)
                elif what == "sample sums":
                    sample_sums()


def kernel(**inputs):
    import numpy as np
    import concourse.bacc as bacc
    from concourse.bass_utils import run_bass_kernel_spmd

    a = {k: np.asarray(t) for k, t in inputs.items()}

    def chunked(w, width):
        r, c = w.shape
        return w.reshape(r // 128, 128, c // width, width).transpose(2, 1, 0, 3)

    w_in = a["w_in"][0]
    starts = {"ua": 0, "va": D, "q": 2 * D, "k": 2 * D + 512, "v": 3 * D, "r": 4 * D,
              "ga": 5 * D + RANK, "gb": 6 * D + RANK}
    blocks = []
    for name in BLOCKS:
        kind, i = name[:-1], int(name[-1])
        if kind == "bra":
            src, c = a["w_br_a"][0], 512 * i
        elif kind == "brb":
            src, c = a["w_br_b"][0], 512 * i
        else:
            src, c = w_in, starts[kind] + 512 * i
        blocks.append(chunked(src[:, c:c + 512], 512)[0])
    x_all = np.concatenate([a["x_prompt"][0], a["x_sample"][:, 0]])
    p_all = np.concatenate([a["p_prompt"][0, 0], a["p_sample"][0, :, 0]])
    ins = {
        "x_all": x_all,
        "x_t": x_all.T.reshape(KC, 128, N).transpose(1, 0, 2),
        "state": a["state_gla"][0].transpose(1, 2, 0, 3),
        "p_t": p_all.T.reshape(2, 128, N).transpose(1, 0, 2),
        "w_blk": np.stack(blocks),
        "w_gkl": chunked(w_in[:, 5 * D:5 * D + RANK], RANK)[0],
        "w_gk": a["w_gk"][0],
        "b_gk": a["b_gk"][0].reshape(H, DK).T,
        "ws_t": a["w_s"][0].transpose(2, 0, 1),
        "ws0": a["w_s"][0][:, 0, 0],
        "b_s": a["b_s"][0].reshape(1, G * 128),
        "lnv_g": a["ln_v_g"][0], "lnv_b": a["ln_v_b"][0],
        "gn_g": a["gla_norm_g"][0].reshape(2, 128).T,
        "w_o": chunked(a["w_o"][0], 512),
        "ln1_g": a["ln1_g"][0], "ln1_b": a["ln1_b"][0],
        "w_q": chunked(a["peer_wq"][0], 512),
        "keys_t": a["peer_keys"][0].reshape(2 * PH, NK, 128).transpose(2, 0, 1),
        "u_tab": a["peer_u"][0], "v_tab": a["peer_v"][0],
        "ln2_g": a["ln2_g"][0], "ln2_b": a["ln2_b"][0],
        "w_pe": a["w_pe"][0].reshape(2, 128, D).transpose(1, 0, 2),
        "w_pg": chunked(a["w_pg"][0], 512),
    }
    outs = {"y_all": (N, D), "st_p": (DK, H, DV), "st_s": (H, DK, S, DV), "cv_p": (128, D), "cv_s": (S, D)}
    nc = bacc.Bacc("TRN2", target_bir_lowering=False, num_devices=1)
    arrays, aps = {}, []
    for name, t in ins.items():
        arrays[f"in_{name}"] = np.ascontiguousarray(t)
        aps.append(nc.dram_tensor(f"in_{name}", t.shape, F32, kind="ExternalInput").ap())
    for name, shape in outs.items():
        aps.append(nc.dram_tensor(f"out_{name}", shape, F32, kind="ExternalOutput").ap())
    decoder_step(nc, *aps)
    r = run_bass_kernel_spmd(nc, [arrays], core_ids=[0]).results[0]
    y = r["out_y_all"]
    return (y[:T].reshape(1, T, D), y[T:].reshape(S, 1, D),
            r["out_st_p"].transpose(1, 0, 2).reshape(1, 1, H, DK, DV),
            r["out_st_s"].transpose(2, 0, 1, 3).reshape(1, S, H, DK, DV),
            r["out_cv_p"].reshape(1, 1, 128, D), r["out_cv_s"].reshape(1, S, 1, D))
```

```python
import math
from contextlib import ExitStack

import concourse.bass as bass
from concourse import mybir

F32 = mybir.dt.float32
F32R = mybir.dt.float32r
U32 = mybir.dt.uint32
ALU = mybir.AluOpType
ACT = mybir.ActivationFunctionType
AX = mybir.AxisListType

D = 1024
T, S = 512, 8
N = T + S
NT = T // 128
HALF = N // 2
KC = D // 128
G = 8
H, DK, DV, RANK = 4, 128, 256, 16
PH, NK, TOPK = 8, 128, 16
SLOTS = PH * TOPK
EPS = 1e-5
ALPHA = 2.0 ** 0.25
TAU = 16.0
NEG = -3.0e38

BC = 256
BLOCKS = [f"{name}{i}" for name, width in (("q", H * DK), ("k", H * DK), ("v", D), ("va", D), ("ua", D), ("r", D),
                                           ("ga", D), ("gb", D), ("bra", D), ("brb", D)) for i in range(width // BC)]
RING = 3
ROUTE_PARTS = 7
LEAD = 2
AHEAD = 4
UB, VB, DB = 5, 5, 6
ITERS = NT * PH
WO_AT = {1: -1, NT: 1, 2: 3, 3: 6}
FIRST_SAMPLE = 5
SAMPLE_DOTS_AT, SAMPLE_SUMS_AT = ITERS - 4, ITERS - 3


def rows(j):
    return 128 if j < NT else S


def cols(j):
    return slice(128 * j, 128 * j + rows(j))


def jobs():
    out = [(None, "low", 0)]
    for i, b in enumerate(BLOCKS):
        if b[:-1] in ("v", "va"):
            out += [(i, "natural", j) for j in range(NT + 1)]
        else:
            out += [(i, "columns", c) for c in range(BC // 128)]
        if b == "q1":
            out += [(None, "decay", h) for h in range(H)]
    return out


JOBS = jobs()


def done_with(name):
    return max(n for n, (b, _, _) in enumerate(JOBS) if b == BLOCKS.index(name)) + 1


BEFORE_GATES = done_with("r3")
BEFORE_BRANCH = done_with("gb3")
EARLY_GATES = done_with("ga2")


def decoder_step(nc, x_all, x_t, state, p_t, w_blk, w_gkl, w_gk, b_gk, ws_t, ws0, b_s, lnv_g, lnv_b, gn_g,
                 w_o, ln1_g, ln1_b, w_q, keys_t, u_tab, v_tab, ln2_g, ln2_b, w_pe, w_pg,
                 y_all, st_p, st_s, cv_p, cv_s):
    with ExitStack() as ctx:
        def sem(name):
            return ctx.enter_context(nc.semaphore(name))

        def tensor(name, shape, dt=F32):
            return ctx.enter_context(nc.sbuf_tensor(name, shape, dt))

        WORDS = 52224
        base = -(-nc.sbuf_base // 32) * 32
        tensor("arena", [128, WORDS])
        assert nc.sbuf_base == base + 4 * WORDS, (nc.sbuf_base, base)
        placed = []

        def at(off, *shape, dtype=F32):
            n = math.prod(shape)
            assert off + n <= WORDS, (off, n)
            placed.append(off)
            t = nc.alloc_sbuf_tensor_at(f"at{off}_{len(placed)}", [128, *shape], dtype, offset=base + 4 * off)
            return t[(slice(None),) * (1 + len(shape))]

        BW, TW = 2 * KC * BC, KC * N
        O_ACT = RING * BW
        O_V = O_ACT + 4 * TW
        O_TMP = O_V + 2 * (NT + 1) * D
        w_hi, w_lo = ([at(BW * i + p * KC * BC, KC, BC, dtype=F32R) for i in range(RING)] for p in range(2))
        w_raw = [at(BW * i + KC * BC, KC, BC) for i in range(RING)]
        uaT, qkT, rT = (at(O_ACT + TW * i, KC, N) for i in range(1, 4))
        x_hi = at(O_ACT, KC, N, dtype=F32R)
        ya_hi, ya_lo = at(O_ACT + 2 * TW, KC, N, dtype=F32R), at(O_ACT + TW, KC, N, dtype=F32R)
        yb_hi, yb_lo = at(O_ACT, KC, N, dtype=F32R), at(O_ACT + 3 * TW, KC, N, dtype=F32R)
        vN = at(O_V, NT + 1, D)
        vaN = at(O_V + (NT + 1) * D, NT + 1, D)
        gaT, gbT = at(O_V, KC, N), at(O_V + TW, KC, N)

        place = [O_TMP]

        def take(*shape):
            v = at(place[0], *shape)
            place[0] += math.prod(shape)
            return v

        logT = take(H, N)
        wsT = take(G, 128)
        S0b, S0a = take(S, DV), take(S, DV)
        S0 = [S0a, S0b]
        x_lo_at = [place[0] - S * DV, O_V + 2 * TW]
        x_lo = [at(o, KC, N, dtype=F32R) for o in x_lo_at]
        x_raw = [at(o, KC, N) for o in x_lo_at]
        lnvg, lnvb = S0[1][:, 0:4, :].rearrange("p a b -> p (a b)"), S0[1][:, 4:8, :].rearrange("p a b -> p (a b)")
        Sst = take(H, DV)
        attS, knat = take(H, 128), take(H, 128)
        kpad = take(S, 128)
        assert place[0] >= x_lo_at[0] + TW
        Ep, Em = take(H, 128), take(H, 128)
        oN = at(place[0] - 2 * H * 128, H, DV)
        mask, ones = take(128), take(128)
        thin = take(N + H * DK)
        gkl, wgk = thin[0:RANK, 0:N], thin[0:RANK, N:N + H * DK]
        bsrow = thin[0:1, 0:G * 128]
        qpad = take(S, S)
        wgkl_at = place[0]
        take(2, KC, RANK)
        gl_hi, gl_lo = (at(wgkl_at + p * KC * RANK, KC, RANK, dtype=F32R) for p in range(2))
        gl_raw = at(wgkl_at + KC * RANK, KC, RANK)
        dg, bs0 = take(G, S)[0:S], take(G, S)[0:1]
        wq = [at(o, KC, 512) for o in (0, BW, O_ACT, O_ACT + 3 * TW)]
        w_wide = [at(O_ACT + TW * i, KC, 512) for i in (1, 2)]
        x1T, x2T = (at(2 * BW + D * i, KC, 128) for i in range(2))
        keysT = at(2 * BW + 2 * D, 2 * PH, NK)
        ln2g, ln2b, wpe = at(O_V, D), at(O_V + D, D), at(O_V + 2 * D, 2, D)
        x1 = at(O_V + TW, NT + 1, D)
        o = O_V + TW + (NT + 1) * D
        qN, qT, pT = at(o, 2, NK), at(o + 256, 2, 128), at(o + 512, 2, 128)
        assert o + 768 <= O_TMP
        ubuf = [at(O_TMP + D * i, D) for i in range(UB)]
        vbuf = [at(O_TMP + D * (UB + i), D) for i in range(VB)]
        place[0] = O_TMP + D * (UB + VB)
        sg = take(D)
        ln1g, ln1b = sg, x2T.rearrange("p a b -> p (a b)")
        x1Ts = at(o + 768, KC, S)
        onehot = take(2, TOPK, TOPK)
        scores = onehot.rearrange("p a b c -> p (a b c)")[:, 0:2 * NK].rearrange("p (a b) -> p a b", a=2)
        cand = take(TOPK * TOPK)
        idxf, gatesS = take(SLOTS)[0:S], take(SLOTS)[0:S]
        diag = [take(128) for _ in range(DB)]

        ident = tensor("ident", [128, 128])
        idx = tensor("idx", [128, AHEAD, TOPK], U32)
        gates = tensor("gates", [128, AHEAD, TOPK])
        vals, e12 = (tensor(n, [128, 2, TOPK]) for n in ("vals", "e12"))
        abf = vals
        inds, abu = (tensor(n, [128, 2, TOPK], U32) for n in ("inds", "abu"))
        indf = tensor("indf", [128, 2, TOPK])
        top, ex, iota16 = (tensor(n, [128, TOPK]) for n in ("top", "ex", "iota16"))
        topi = tensor("topi", [128, TOPK], U32)
        iotau = tensor("iotau", [128, TOPK], U32)
        hraw, hact = (tensor(n, [128, 2, TOPK]) for n in ("hraw", "hact"))
        wgt = tensor("wgt", [128, 3, TOPK])
        bn, mv = tensor("bn", [128, 2, 6]), tensor("mv", [128, 2, 2])
        sd, rstd = tensor("sd", [128, 4]), tensor("rstd", [128, 4])
        soft = tensor("soft", [128, 3])
        ss = tensor("ss", [128, H])
        bgk, gng = tensor("bgk", [128, H]), tensor("gng", [128, 2])
        mid = tensor("mid", [128, NT, 2, H])
        fac = tensor("fac", [128, NT, H])
        egT = tensor("egT", [128, H, S])
        w00 = tensor("w00", [S, G])
        idxT = tensor("idxT", [SLOTS, S], U32)
        gateT, hS, aS = (tensor(n, [SLOTS, S]) for n in ("gateT", "hS", "aS"))
        wpad = tensor("wpad", [SLOTS, S, S])

        PJ = ctx.enter_context(nc.psum_tensor("PJ", [128, 2, 2, 512], F32))
        X = [ctx.enter_context(nc.psum_tensor(f"X{i}", [128, 1024], F32)) for i in range(2)]
        Y = PJ[:, 0, :, :]
        W = PJ[:, 1, :, :]
        sample_x1 = [X[0][:, :].rearrange("p (a b) -> p a b", a=2), W]
        RQ, RT = X[1][:, 0:512], X[1][:, 512:1024]

        small_in, row_in, gl_hi_ok, gl_raw_in, gl_ok, x_ok, x2_raw_in, x2_lo_ok = (sem(n) for n in (
            "small_in", "row_in", "gl_hi_ok", "gl_raw_in", "gl_ok", "x_ok", "x2_raw_in", "x2_lo_ok"))
        x_raw_in = [sem(f"x_raw_in{i}") for i in range(KC // 2)]
        x_hi_ok = sem("x_hi_ok")
        w_hi_in = [sem(f"w_hi_in{i}") for i in range(RING)]
        split_ok, ya_hi_ok, ya_lo_ok, yb_hi_ok, yb_lo_ok = (sem(n) for n in (
            "split_ok", "ya_hi_ok", "ya_lo_ok", "yb_hi_ok", "yb_lo_ok"))
        blk_in = [sem(f"blk_in{i}") for i in range(RING)]
        const_ok, cst_v = sem("const_ok"), sem("cst_v")
        pj_done, pj_act, pj_dve = sem("pj_done"), sem("pj_act"), sem("pj_dve")
        act_chain, dve_chain, pool_chain = sem("act_chain"), sem("dve_chain"), sem("pool_chain")
        soft_part, log_ok, mid_ok, e_ok, qk_ok = (sem(n) for n in ("soft_part", "log_ok", "mid_ok", "e_ok", "qk_ok"))
        var_ok, sd_ok, vn_ok = sem("var_ok"), sem("sd_ok"), sem("vn_ok")
        z_done, ya_ok = sem("z_done"), sem("ya_ok")
        att_done, att_ok, knat_ok, o_done, kv_done, s_ok = (sem(n) for n in (
            "att_done", "att_ok", "knat_ok", "o_done", "kv_done", "s_ok"))
        ss_ok, orms_ok, on_ok, ot_done, yb_ok = (sem(n) for n in ("ss_ok", "orms_ok", "on_ok", "ot_done", "yb_ok"))
        s0_in = [sem("s0_in0"), sem("s0_in1")]
        kpad_ok, outer_done, s0_new, os_done = (sem(n) for n in ("kpad_ok", "outer_done", "s0_new", "os_done"))
        cv_out, stp_out = sem("cv_out"), sem("stp_out")
        s0_out = [sem("s0_out0"), sem("s0_out1")]
        wo_in, ln1_in, keys_in, wpg_in, wpe_in, ln2_in = (sem(n) for n in (
            "wo_in", "ln1_in", "keys_in", "wpg_in", "wpe_in", "ln2_in"))
        xr_in = [sem(f"xr_in{j}") for j in range(NT + 1)]
        wq_in = [sem(f"wq_in{i}") for i in range(4)]
        pt_in = sem("pt_in")
        w_done, x1_ok, tr_done, x1t_ok = (sem(n) for n in ("w_done", "x1_ok", "tr_done", "x1t_ok"))
        q_done, rq_read, qn_ok, qt_done, qt_ok, s_done, route_ok, exp_in, exp_ok = (sem(n) for n in (
            "q_done", "rq_read", "qn_ok", "qt_done", "qt_ok", "s_done", "route_ok", "exp_in", "exp_ok"))
        u_in = [sem(f"u_in{i}") for i in range(UB)]
        v_in = [sem(f"v_in{i}") for i in range(VB)]
        u_used, h_ok, w_ok, diag_ok, v_used, y_done = (sem(n) for n in (
            "u_used", "h_ok", "w_ok", "diag_ok", "v_used", "y_done"))
        y_read, x2_ok, x2t_ok, g_done, g_ok, pe_done, x3_ok = (sem(n) for n in (
            "y_read", "x2_ok", "x2t_ok", "g_done", "g_ok", "pe_done", "x3_ok"))
        it_done, it_ok = sem("it_done"), sem("it_ok")
        xb_done, hs_ok, gs_ok, wpad_ok, ys_done = (sem(n) for n in ("xb_done", "hs_ok", "gs_ok", "wpad_ok", "ys_done"))
        y_out = sem("y_out")

        block = ctx.enter_context(nc.Block())

        def head_at(n):
            return n // PH, n % PH

        def whole(what, j):
            return [(what, j, part) for part in range(4)]

        def step(n):
            j, h = head_at(max(n, 0))
            ahead = head_at(n + LEAD) if n + LEAD < ITERS else None
            following = head_at(n + LEAD + 1) if n + LEAD + 1 < ITERS else None
            samples = (NT, (n - FIRST_SAMPLE) // 3) if n in range(FIRST_SAMPLE, FIRST_SAMPLE + 3 * PH, 3) else None
            out = []
            at_k = {"dots": 0, "sums": 0}

            def upto(what, k):
                m = n + (what == "dots")
                if at_k[what] < k:
                    if m in range(ITERS):
                        out.append((what, m, at_k[what], k))
                    at_k[what] = k

            parts = []
            if ahead:
                parts += [("route", *ahead, part) for part in range(ROUTE_PARTS)]
            if samples:
                parts.insert(4, ("q", *samples))
                parts += [("route", *samples, part) for part in range(ROUTE_PARTS)]
            if following:
                parts.insert(12 if samples else 5, ("q", *following))
            wide = [("wo", tile) for tile, at_step in WO_AT.items() if at_step == n]
            if h == 2 and j:
                wide = [("pg", j - 1)]
            if n == ITERS - 2:
                wide = [("pg", NT)]
            for w in wide:
                for part in range(4):
                    parts.insert(min(len(parts), 4 + 3 * part), (*w, part))
            parts = [("x1", tile, part) for tile, at_step in WO_AT.items() if at_step == n - 1
                     for part in range(4)] + parts
            if h == 3 and j:
                parts.append(("pe", j - 1, 3))
            if n == ITERS - 1:
                parts.append(("pe", NT, 3))
            if h == 1 and j:
                parts.insert(1, ("turn", "x2", j - 1))
            if n == FIRST_SAMPLE - 1:
                parts.insert(4, ("turn", "x1", NT))
            if h == 5 and j + 1 < NT:
                parts.insert(4, ("turn", "x1", j + 1))
            if n == ITERS - 2:
                parts.insert(0, ("turn", "x2", NT))

            if n == SAMPLE_DOTS_AT - 1:
                out.append(("samples",))
            if n == SAMPLE_DOTS_AT:
                out += [("sample dot", b) for b in range(S)]
            if h == 0 and j:
                upto("dots", 1)
                for part in range(4):
                    out.append(("x2", j - 1, part))
                    upto("dots", 2 + part)
                    upto("sums", part)
            if n == SAMPLE_SUMS_AT:
                out.append(("sample sums",))
                parts += whole("x2", NT)
            d0, s0 = at_k["dots"], at_k["sums"]
            for i, part in enumerate(parts):
                out.append(part)
                f = (i + 1) / (len(parts) + 1)
                upto("sums", s0 + int((TOPK - s0) * f))
                upto("dots", min(TOPK, d0 + int((TOPK - d0) * f) + 1))
            upto("sums", TOPK)
            upto("dots", TOPK)
            if n + 1 < ITERS:
                out.append(("weights", n + 1))
            return out

        PLAN = whole("wo", 0) + whole("x1", 0) + [("turn", "x1", 0), ("q", 0, 0)]
        PLAN += [("route", 0, 0, part) for part in range(ROUTE_PARTS)] + [("q", 0, 1)]
        for n in range(-1, ITERS):
            PLAN += step(n)
        PLAN += whole("x2", NT - 1) + [("pe", NT - 1, 3), ("turn", "x2", NT - 1)] + whole("pg", NT - 1)

        def numbers(keys):
            return {k: n for n, k in enumerate(keys)}

        WIDE = numbers(e[:2] for e in PLAN if e[0] in ("wo", "pg", "pe") and e[2] == 3)
        TURN = numbers(e[1:] for e in PLAN if e[0] == "turn")
        ROUTE = numbers(e[1:3] for e in PLAN if e[0] == "q")
        X1 = numbers(e[1] for e in PLAN if e[0] == "x1" and e[2] == 0)
        X2 = numbers(e[1] for e in PLAN if e[0] == "x2" and e[2] == 0)
        SD = numbers([("va", j) for j in range(NT + 1)] + [("o", j) for j in range(NT + 1)]
                     + [e[:2] if e[0] != "route" else e[:3] for e in PLAN
                        if (e[0] in ("x1", "x2") and e[2] == 0) or (e[0] == "route" and e[3] == 0)])
        READ = numbers(e[:2] for e in PLAN if e[0] in ("x1", "x2") and e[2] == 0)
        LAST_X1 = list(X1)[-1]

        def u_number(n, k):
            return n * TOPK + k + (S if n > SAMPLE_DOTS_AT else 0)

        def v_number(n, k):
            return n * TOPK + k + (S if n >= SAMPLE_SUMS_AT else 0)

        U_SAMPLE, V_SAMPLE = (SAMPLE_DOTS_AT + 1) * TOPK, SAMPLE_SUMS_AT * TOPK

        @block.sync
        def _(sp):
            sp.dma_start(gl_raw, w_gkl).then_inc(gl_raw_in, 16)
            for i in range(KC // 2):
                c = slice(2 * i, 2 * i + 2)
                sp.dma_start(x_raw[0][:, c, :], x_t[:, c, :]).then_inc(x_raw_in[i], 16)

            def load_block(i):
                if i >= RING:
                    sp.wait_ge(pj_done, done_with(BLOCKS[i - RING]))
                sp.dma_start(w_raw[i % RING], w_blk[i]).then_inc(blk_in[i % RING], 16)

            load_block(0)
            sp.dma_start(wgk, w_gk).then_inc(small_in, 16)
            sp.dma_start(bgk[:, :], b_gk).then_inc(small_in, 16)
            for i in range(1, RING):
                load_block(i)
            sp.dma_start(wsT, ws_t).then_inc(row_in, 16)
            sp.dma_start(lnvg, lnv_g.partition_broadcast(128)).then_inc(row_in, 16)
            sp.dma_start(lnvb, lnv_b.partition_broadcast(128)).then_inc(row_in, 16)
            sp.dma_start(w00[:, :], ws0.partition_broadcast(S)).then_inc(row_in, 16)
            sp.dma_start(gng[:, :], gn_g).then_inc(row_in, 16)
            for i in range(RING, BLOCKS.index("ga0") + RING):
                load_block(i)
                if i == RING + BLOCKS.index("k0"):
                    sp.dma_start(bsrow, b_s).then_inc(row_in, 16)
            sp.dma_start(S0[0], state[0]).then_inc(s0_in[0], 16)
            sp.wait_ge(vn_ok, NT + 1)
            sp.dma_start(cv_p, vaN[:, NT - 1, :]).then_inc(cv_out, 16)
            sp.dma_start(cv_s, vaN[0:S, NT, :]).then_inc(cv_out, 16)
            sp.dma_start(S0[1], state[1]).then_inc(s0_in[1], 16)
            sp.wait_ge(z_done, NT + 1)
            sp.wait_ge(e_ok, NT + 1)
            sp.wait_ge(cv_out, 32)
            sp.dma_start(x_raw[1], x_t).then_inc(x2_raw_in, 16)
            sp.wait_ge(s_ok, NT)
            sp.dma_start(st_p, Sst).then_inc(stp_out, 16)
            for h in range(H):
                sp.wait_ge(s0_new, 8 * (h + 1))
                sp.wait_ge(os_done, h + 1)
                sp.dma_start(st_s[h], S0[h % 2]).then_inc(s0_out[h % 2], 16)
                if h + 2 < H:
                    sp.wait_ge(s0_out[h % 2], 16)
                    sp.dma_start(S0[h % 2], state[h + 2]).then_inc(s0_in[h % 2], 16)
            for i in range(BLOCKS.index("ga0") + RING, len(BLOCKS)):
                load_block(i)
            sp.wait_ge(yb_ok, NT + 1)
            sp.wait_ge(stp_out, 16)
            for i in range(2):
                sp.wait_ge(s0_out[i], 32)
            sp.dma_start(ln1g, ln1_g.partition_broadcast(128)).then_inc(ln1_in, 16)
            sp.wait_ge(pj_done, done_with("bra3"))
            for i in range(2):
                sp.dma_start(w_wide[i], w_o[i]).then_inc(wo_in, 16)
            for i in range(2):
                sp.wait_ge(pj_done, done_with(BLOCKS[len(BLOCKS) - RING + i]))
                sp.dma_start(wq[i], w_q[i]).then_inc(wq_in[i], 16)
            sp.wait_ge(pj_dve, len(JOBS) - BEFORE_BRANCH)
            sp.dma_start(ln1b, ln1_b.partition_broadcast(128)).then_inc(ln1_in, 16)
            for j in range(NT + 1):
                sp.dma_start(x1[0:rows(j), j, :], x_all[cols(j), :]).then_inc(xr_in[j], 16)
            sp.dma_start(keysT, keys_t).then_inc(keys_in, 16)
            for i in range(2, 4):
                sp.dma_start(wq[i], w_q[i]).then_inc(wq_in[i], 16)
            sp.wait_ge(w_done, WIDE["wo", LAST_X1] + 1)
            sp.dma_start(ln2g, ln2_g.partition_broadcast(128)).then_inc(ln2_in, 16)
            sp.dma_start(ln2b, ln2_b.partition_broadcast(128)).then_inc(ln2_in, 16)
            for i in range(2):
                sp.dma_start(w_wide[i], w_pg[i]).then_inc(wpg_in, 16)
            sp.dma_start(wpe, w_pe).then_inc(wpe_in, 16)
            order = list(X2)
            for i, j in enumerate(order):
                if i:
                    sp.wait_ge(w_done, WIDE["pe", order[i - 1]] + 1)
                sp.dma_start(pT[:, :, 0:rows(j)], p_t[:, :, cols(j)]).then_inc(pt_in, 16)
                sp.wait_ge(x3_ok, i + 1)
                sp.dma_start(y_all[cols(j), :], x1[0:rows(j), j, :]).then_inc(y_out, 16)
            sp.wait_ge(cv_out, 32)
            sp.wait_ge(y_out, 16 * (NT + 1))

        @block.gpsimd
        def _(pool):
            def load_high(i):
                if i >= RING:
                    pool.wait_ge(pj_done, done_with(BLOCKS[i - RING]))
                pool.dma_start(w_hi[i % RING], w_blk[i]).then_inc(w_hi_in[i % RING], 16)

            def low_part(i):
                pool.wait_ge(blk_in[i % RING], 16 * (i // RING + 1))
                pool.wait_ge(w_hi_in[i % RING], 16 * (i // RING + 1))
                pool.tensor_tensor(w_lo[i % RING], w_raw[i % RING], w_hi[i % RING], ALU.subtract).then_inc(split_ok, 1)

            load_high(0)
            low_part(0)
            for i in range(1, RING):
                load_high(i)
            pool.memset(ident[:, :], 0.0).then_inc(pool_chain, 1)
            pool.memset(mask, 1.0).then_inc(pool_chain, 1)
            pool.memset(ones, 1.0).then_inc(const_ok, 1)
            pool.memset(qpad, 0.0).then_inc(const_ok, 1)
            pool.memset(wpad[:, :, :], 0.0).then_inc(const_ok, 1)
            pool.iota(iotau[:, :], pattern=[[1, TOPK]], base=0, channel_multiplier=0).then_inc(pool_chain, 1)
            pool.wait_ge(pool_chain, 3)
            pool.tensor_copy(iota16[:, :], iotau[:, :]).then_inc(const_ok, 1)
            pool.affine_select(out=ident[:, :], in_=ident[:, :], compare_op=ALU.not_equal, fill=1.0, base=0,
                               pattern=[[-1, 128]], channel_multiplier=1).then_inc(const_ok, 1)
            pool.affine_select(out=mask, in_=mask, compare_op=ALU.is_ge, fill=0.0, base=0,
                               pattern=[[1, 128]], channel_multiplier=-1).then_inc(const_ok, 1)
            for i in range(1, RING):
                low_part(i)
            for i in range(RING, len(BLOCKS)):
                load_high(i)
                low_part(i)
                if i == BLOCKS.index("ga2"):
                    pool.wait_ge(x2_raw_in, 16)
                    pool.wait_ge(x_ok, KC // 2)
                    for p in range(2):
                        c = slice(p * KC // 2, (p + 1) * KC // 2)
                        pool.tensor_tensor(x_lo[1][:, c, :], x_raw[1][:, c, :], x_hi[:, c, :], ALU.subtract).then_inc(
                            x2_lo_ok, 1)

            def gather_u(m, rows_of):
                if m >= UB:
                    pool.wait_ge(u_used, m - UB + 1)
                pool.indirect_dma_start(ubuf[m % UB], None, u_tab, bass.IndirectOffsetOnAxis(rows_of, 0)).then_inc(
                    u_in[m % UB], 16)

            def gather_v(m, rows_of):
                if m >= VB:
                    pool.wait_ge(v_used, m - VB + 1)
                pool.indirect_dma_start(vbuf[m % VB], None, v_tab, bass.IndirectOffsetOnAxis(rows_of, 0)).then_inc(
                    v_in[m % VB], 16)

            pool.wait_ge(route_ok, 1)
            for k in range(TOPK):
                gather_u(u_number(0, k), idx[:, 0, k:k + 1])
            for n in range(ITERS):
                if n + 1 < ITERS:
                    pool.wait_ge(route_ok, ROUTE[(n + 1) // PH, (n + 1) % PH] + 1)
                if n == SAMPLE_DOTS_AT:
                    pool.wait_ge(it_ok, 2)
                    for b in range(S):
                        gather_u(U_SAMPLE + b, idxT[:, b:b + 1])
                if n == SAMPLE_SUMS_AT:
                    for b in range(S):
                        gather_v(V_SAMPLE + b, idxT[:, b:b + 1])
                for k in range(TOPK):
                    if n + 1 < ITERS:
                        gather_u(u_number(n + 1, k), idx[:, (n + 1) % AHEAD, k:k + 1])
                    gather_v(v_number(n, k), idx[:, n % AHEAD, k:k + 1])

        @block.scalar
        def _(act):
            chain = [0]

            def link(ins):
                chain[0] += 1
                ins.then_inc(act_chain, 1)
                act.wait_ge(act_chain, chain[0])

            def deviation(key, p, n, src):
                act.wait_ge(var_ok, SD[key] + 1)
                act.activation(sd[0:p, 0:n], src, ACT.Sqrt).then_inc(sd_ok, 1)

            evac = [0]
            dest = {"q": (qkT, 0), "k": (qkT, 4), "ua": (uaT, 0), "r": (rT, 0), "ga": (gaT, 0), "gb": (gbT, 0)}
            func = {"q": ACT.Copy, "k": ACT.Copy, "ua": ACT.Gelu_apprx_tanh, "r": ACT.Silu,
                    "ga": ACT.Sigmoid, "gb": ACT.Sigmoid, "v": ACT.Copy, "va": ACT.Gelu_apprx_tanh}

            def evacuate(n):
                blk, kind, part = JOBS[n]
                act.wait_ge(pj_done, n + 1)
                half = PJ[:, n % 2, :, 0:HALF]
                if kind == "low":
                    act.activation(gkl.rearrange("p (a b) -> p a b", a=2), half[0:RANK], ACT.Copy).then_inc(pj_act, 1)
                elif kind == "decay":
                    act.activation(logT[:, part, :].rearrange("p (a b) -> p a b", a=2), half, ACT.Identity,
                                   bias=bgk[:, part:part + 1]).then_inc(pj_act, 1)
                elif kind == "columns":
                    name = BLOCKS[blk]
                    t, c0 = dest[name[:-1]]
                    c = c0 + BC // 128 * int(name[-1]) + part
                    act.activation(t[:, c, :].rearrange("p (a b) -> p a b", a=2), half, func[name[:-1]],
                                   scale=DK ** -0.5 if name[:-1] == "q" else 1.0).then_inc(pj_act, 1)
                else:
                    name = BLOCKS[blk]
                    t = vN if name[:-1] == "v" else vaN
                    c = BC * int(name[-1])
                    p = rows(part)
                    act.activation(t[0:p, part, c:c + BC], PJ[0:p, n % 2, 0, 0:BC], func[name[:-1]]).then_inc(pj_act, 1)

            def soft_logs():
                act.wait_ge(pj_act, n_log)
                tmp = rT[:, 0:H, :]
                link(act.activation(tmp, logT, ACT.Abs))
                link(act.activation(tmp, tmp, ACT.Exp, scale=-1.0))
                act.activation(tmp, tmp, ACT.Ln, bias=1.0).then_inc(soft_part, 1)

            def decays(j):
                if j < NT:
                    act.wait_ge(mid_ok, j + 1)
                    if j:
                        act.wait_ge(qk_ok, j)
                    for h in range(H):
                        act.activation(Ep[:, h, :], logT[:, h, cols(j)], ACT.Exp, scale=1.0 / TAU,
                                       bias=mid[:, j, 0, h:h + 1])
                        last = act.activation(Em[:, h, :], logT[:, h, cols(j)], ACT.Exp, scale=-1.0 / TAU,
                                              bias=mid[:, j, 1, h:h + 1])
                    last.then_inc(e_ok, 1)
                    return
                act.wait_ge(mid_ok, NT + 1)
                link(act.activation(fac[:, :, :], fac[:, :, :], ACT.Exp, scale=1.0 / TAU))
                act.activation(egT[:, :, :], logT[:, :, T:N], ACT.Exp, scale=1.0 / TAU).then_inc(e_ok, 1)

            n_log = max(n for n, (_, kind, _) in enumerate(JOBS) if kind == "decay") + 1
            n_va = done_with("va3")
            act.wait_ge(gl_raw_in, 16)
            act.activation(gl_hi, gl_raw, ACT.Copy).then_inc(gl_hi_ok, 1)
            for i in range(KC // 2):
                c = slice(2 * i, 2 * i + 2)
                act.wait_ge(x_raw_in[i], 16)
                act.activation(x_hi[:, c, :], x_raw[0][:, c, :], ACT.Copy).then_inc(x_hi_ok, 1)
            for n in range(n_log):
                evacuate(n)
            soft_logs()
            for n in range(n_log, BEFORE_GATES):
                evacuate(n)
                for j in range(NT + 1):
                    if n == done_with("v1") + 3 * j - 1:
                        decays(j)
                    if n == n_va + (3 * j + 1) // 2:
                        deviation(("va", j), rows(j), 1, mv[0:rows(j), 0, 1:2])

            def gla_norm(j):
                p = rows(j)
                act.wait_ge(o_done, j + 1)
                if j:
                    act.wait_ge(ot_done, j)
                for h in range(H):
                    last = act.activation(oN[0:p, h, :], X[1][0:p, h * DV:(h + 1) * DV], ACT.Square,
                                          accum_out=ss[0:p, h:h + 1])
                last.then_inc(ss_ok, 1)
                deviation(("o", j), p, H, rstd[0:p, 0:H])
                act.wait_ge(orms_ok, j + 1)
                for h in range(H):
                    last = act.activation(oN[0:p, h, :], X[1][0:p, h * DV:(h + 1) * DV], ACT.Copy,
                                          scale=rstd[0:p, h:h + 1])
                last.then_inc(on_ok, 1)

            act.wait_ge(qk_ok, NT)
            for j in range(NT):
                act.wait_ge(att_done, j + 1)
                act.activation(knat, X[0][:, 512:1024].rearrange("p (a b) -> p a b", a=H), ACT.Copy).then_inc(knat_ok, 1)
                gla_norm(j)
            act.wait_ge(att_done, NT + 1)
            act.wait_ge(kv_done, NT)
            act.activation(knat[0:S], X[0][0:S, 0:512].rearrange("p (a b) -> p a b", a=H), ACT.Copy).then_inc(knat_ok, 1)
            for n in range(BEFORE_GATES, EARLY_GATES):
                evacuate(n)
            gla_norm(NT)
            act.wait_ge(cv_out, 32)
            for n in range(EARLY_GATES, BEFORE_BRANCH):
                evacuate(n)
                if n == EARLY_GATES + 1:
                    act.wait_ge(yb_ok, NT + 1)
                    act.activation(ya_hi, uaT, ACT.Copy).then_inc(ya_hi_ok, 1)
            act.activation(yb_hi, rT, ACT.Copy).then_inc(yb_hi_ok, 1)

            def route(j, h, part):
                p, r = rows(j), ROUTE[j, h]
                if part == 1:
                    deviation(("route", j, h), p, 2, mv[0:p, :, 1:2].rearrange("p a b -> p (a b)"))
                elif part == 2:
                    act.wait_ge(qt_done, r + 1)
                    act.activation(qT[:, :, 0:p], RT[:, 0:256].rearrange("p (a b) -> p a b", a=2)[:, :, 0:p],
                                   ACT.Copy).then_inc(qt_ok, 1)
                elif part == 5:
                    act.wait_ge(exp_in, r + 1)
                    act.activation(ex[0:p, :], top[0:p, :], ACT.Exp, bias=soft[0:p, 0:1],
                                   accum_out=soft[0:p, 1:2]).then_inc(exp_ok, 1)

            def diagonals(n, ks):
                for k in ks:
                    m = n * TOPK + k
                    if k == 0:
                        act.wait_ge(w_ok, n + 1)
                    if m >= DB:
                        act.wait_ge(v_used, v_number(*divmod(m - DB, TOPK)) + 1)
                    act.activation(diag[m % DB], ident[:, :], ACT.Copy, scale=wgt[:, n % 3, k:k + 1]).then_inc(diag_ok, 1)

            for e in PLAN:
                what, args = e[0], e[1:]
                if what in ("x1", "x2"):
                    if args[1] == 0:
                        deviation(e[:2], rows(args[0]), 1, mv[0:rows(args[0]), 0, 1:2])
                elif what == "turn":
                    name, j = args
                    p = rows(j)
                    act.wait_ge(tr_done, TURN[args] + 1)
                    dst = x1Ts if args == ("x1", NT) else (x1T if name == "x1" else x2T)[:, :, 0:p]
                    act.activation(dst, X[0][:, :].rearrange("p (a b) -> p a b", a=KC)[:, :, 0:p], ACT.Copy).then_inc(
                        x1t_ok, 1)
                elif what == "route":
                    route(*args)
                elif what == "sums":
                    diagonals(args[0], range(args[1], args[2]))
                elif what == "weights":
                    n = args[0]
                    act.wait_ge(h_ok, n + 1)
                    act.activation(hact[:, n % 2, :], hraw[:, n % 2, :], ACT.Gelu_apprx_tanh).then_inc(g_ok, 1)
                elif what == "pg" and args[1] == 3:
                    j = args[0]
                    p = rows(j)
                    act.wait_ge(w_done, WIDE[e[:2]] + 1)
                    if X2[j]:
                        act.wait_ge(x3_ok, X2[j])
                    act.activation(sg[0:p, :].rearrange("p (a b) -> p a b", a=2), W[0:p], ACT.Sigmoid).then_inc(g_done, 1)
                elif what == "samples":
                    act.wait_ge(it_done, 2)
                    act.activation(gateT[:, :], X[0][:, 512:512 + S], ACT.Copy).then_inc(it_ok, 1)
                elif what == "sample dot" and args[0] == S - 1:
                    act.wait_ge(hs_ok, 1)
                    act.activation(aS[:, :], hS[:, :], ACT.Gelu_apprx_tanh).then_inc(gs_ok, 1)

        @block.vector
        def _(v):
            chain = [0]

            def link(ins):
                chain[0] += 1
                ins.then_inc(dve_chain, 1)
                v.wait_ge(dve_chain, chain[0])

            def row_stats(src, p):
                v.bn_stats(bn[0:p, 0, :], src[:, 0:512])
                link(v.bn_stats(bn[0:p, 1, :], src[:, 512:1024]))
                link(v.bn_aggr(mv[0:p, 0, :], bn[0:p].rearrange("p a b -> p (a b)")))
                v.tensor_scalar(mv[0:p, 0, 1:2], mv[0:p, 0, 1:2], EPS, None, ALU.add).then_inc(var_ok, 1)

            def inverse(key, p, n):
                v.wait_ge(sd_ok, SD[key] + 1)
                return v.reciprocal(rstd[0:p, 0:n], sd[0:p, 0:n])

            def layernorm(t, key, g, b, done):
                p = rows(key[1])
                row_stats(t, p)
                link(inverse(key, p, 1))
                link(v.tensor_scalar(t, t, mv[0:p, 0, 0:1], rstd[0:p, 0:1], ALU.subtract, ALU.mult))
                link(v.tensor_tensor(t, t, g[0:p], ALU.mult))
                v.tensor_tensor(t, t, b[0:p], ALU.add).then_inc(done, 1)

            v.wait_ge(gl_hi_ok, 1)
            v.tensor_tensor(gl_lo, gl_raw, gl_hi, ALU.subtract).then_inc(gl_ok, 1)
            for i in range(KC // 2):
                c = slice(2 * i, 2 * i + 2)
                v.wait_ge(x_hi_ok, i + 1)
                v.tensor_tensor(x_lo[0][:, c, :], x_raw[0][:, c, :], x_hi[:, c, :], ALU.subtract).then_inc(x_ok, 1)
            v.wait_ge(const_ok, 6)
            v.wait_ge(soft_part, 1)
            link(v.scalar_tensor_tensor(out=logT, in0=logT, scalar=0.0, in1=rT[:, 0:H, :], op0=ALU.min,
                                        op1=ALU.subtract))
            for j in range(NT):
                for h in range(H):
                    c = logT[:, h, cols(j)]
                    last = v.tensor_tensor_scan(c, ones, c, 0.0, ALU.mult, ALU.add)
                    chain[0] += 1
                    last.then_inc(dve_chain, 1)
            v.wait_ge(dve_chain, chain[0])
            for j in range(NT):
                m = logT[:, :, 128 * j + 63:128 * j + 64].rearrange("p a b -> p (a b)")
                link(v.tensor_scalar(mid[:, j, 0, :], m, -1.0 / TAU, None, ALU.mult))
                v.tensor_scalar(mid[:, j, 1, :], m, 1.0 / TAU, None, ALU.mult).then_inc(mid_ok, 1)
            for j in range(NT):
                m = logT[:, :, 128 * j + 63:128 * j + 64].rearrange("p a b -> p (a b)")
                e = logT[:, :, 128 * j + 127:128 * j + 128].rearrange("p a b -> p (a b)")
                ins = v.tensor_tensor(fac[:, j, :], e, m, ALU.subtract)
                if j + 1 < NT:
                    link(ins)
                    m2 = logT[:, :, 128 * j + 191:128 * j + 192].rearrange("p a b -> p (a b)")
                    link(v.tensor_tensor(fac[:, j, :], fac[:, j, :], m2, ALU.add))
            ins.then_inc(mid_ok, 1)
            v.wait_ge(pj_act, done_with("k1"))
            for j in range(NT):
                v.wait_ge(e_ok, j + 1)
                v.tensor_tensor(qkT[:, 0:H, cols(j)], qkT[:, 0:H, cols(j)], Ep, ALU.mult)
                link(v.tensor_tensor(qkT[:, H:2 * H, cols(j)], qkT[:, H:2 * H, cols(j)], Em, ALU.mult))
                v.sem_inc(qk_ok, 1)
            v.wait_ge(row_in, 16 * 6)
            link(v.tensor_tensor(wsT, wsT, mask.unsqueeze(1).broadcast_to([128, G, 128]), ALU.mult))
            v.tensor_copy(bs0, bsrow.rearrange("p (a b) -> p a b", a=G)[:, :, 0:1].broadcast_to([1, G, S]))
            link(v.tensor_tensor(dg, ident[0:S, 0:S].unsqueeze(1).broadcast_to([S, G, S]),
                                 w00[:, :].unsqueeze(2).broadcast_to([S, G, S]), ALU.mult))
            for j in range(NT + 1):
                n = [i for i, (b, _, part) in enumerate(JOBS)
                     if b is not None and BLOCKS[b] == "va3" and part == j][0]
                v.wait_ge(pj_act, n + 1)
                layernorm(vaN[0:rows(j), j, :], ("va", j), lnvg, lnvb, vn_ok)

            def gate_values(j):
                v.wait_ge(z_done, j + 1)
                if j == 0:
                    v.wait_ge(pj_act, done_with("ua3"))
                p = rows(j)
                z = X[j % 2][:, 0:G * p].rearrange("p (a b) -> p a b", a=G)
                v.tensor_tensor(uaT[:, :, cols(j)], uaT[:, :, cols(j)], z, ALU.mult).then_inc(ya_ok, 1)

            for j in range(NT + 1):
                gate_values(j)

            def output_stats(j):
                p = rows(j)
                v.wait_ge(ss_ok, j + 1)
                v.tensor_scalar(rstd[0:p, 0:H], ss[0:p, 0:H], 1.0 / DV, EPS, ALU.mult, ALU.add).then_inc(var_ok, 1)
                inverse(("o", j), p, H).then_inc(orms_ok, 1)

            def branch_b(j):
                p = rows(j)
                v.wait_ge(ot_done, j + 1)
                v.wait_ge(pj_act, BEFORE_GATES)
                t = PJ[:, j % 2, :, :].rearrange("p a (b c) -> p (a b) c", b=4)
                for q in range(2):
                    dst = rT[:, q::2, cols(j)]
                    last = v.scalar_tensor_tensor(out=dst, in0=t[:, q::2, 0:p], scalar=gng[:, q:q + 1], in1=dst,
                                                  op0=ALU.mult, op1=ALU.mult)
                    chain[0] += 1
                    last.then_inc(dve_chain, 1)
                v.wait_ge(dve_chain, chain[0])
                v.sem_inc(yb_ok, 1)

            for j in range(NT):
                v.wait_ge(att_done, j + 1)
                if j:
                    v.wait_ge(o_done, j)
                v.tensor_tensor(attS, X[0][:, 0:512].rearrange("p (a b) -> p a b", a=H),
                                mask.unsqueeze(1).broadcast_to([128, H, 128]), ALU.mult).then_inc(att_ok, 1)
                v.wait_ge(kv_done, j + 1)
                kv = X[0][:, :].rearrange("p (a b) -> p a b", a=H)
                v.wait_ge(e_ok, NT + 1)
                src = kv
                if j:
                    v.wait_ge(o_done, j + 1)
                    link(v.tensor_tensor(Sst, kv, Sst, ALU.add))
                    src = Sst
                for h in range(H):
                    last = v.tensor_scalar(Sst[:, h, :], src[:, h, :], fac[:, j, h:h + 1], None, ALU.mult)
                    chain[0] += 1
                    last.then_inc(dve_chain, 1)
                v.wait_ge(dve_chain, chain[0])
                v.sem_inc(s_ok, 1)
                output_stats(j)
                if j:
                    branch_b(j - 1)
            v.wait_ge(knat_ok, NT + 1)
            for h in range(H):
                if h:
                    v.wait_ge(outer_done, 4 * h)
                v.tensor_tensor(kpad[0:S], knat[0:S, h, :].unsqueeze(1).broadcast_to([S, S, 128]),
                                ident[0:S, 0:S].unsqueeze(2).broadcast_to([S, S, 128]), ALU.mult).then_inc(kpad_ok, 1)
                if h:
                    v.wait_ge(os_done, h)
                v.tensor_copy(qpad.rearrange("p a b -> p (a b)")[:, 0:S * S:S + 1], qkT[:, h, T:N]).then_inc(kpad_ok, 1)
                v.wait_ge(s0_in[h % 2], 16 * (h // 2 + 1))
                for b in range(S):
                    if b % 2 == 0:
                        v.wait_ge(outer_done, 4 * h + b // 2 + 1)
                    v.scalar_tensor_tensor(out=S0[h % 2][:, b, :], in0=S0[h % 2][:, b, :], scalar=egT[:, h, b:b + 1],
                                           in1=X[0][:, (b % 4) * DV:(b % 4 + 1) * DV], op0=ALU.mult,
                                           op1=ALU.add).then_inc(s0_new, 1)
                if h == 0:
                    branch_b(NT - 1)
            output_stats(NT)
            branch_b(NT)
            v.wait_ge(ya_hi_ok, 1)
            v.tensor_tensor(ya_lo, uaT, ya_hi, ALU.subtract).then_inc(ya_lo_ok, 1)
            v.wait_ge(pj_act, BEFORE_BRANCH)
            for n in range(BEFORE_BRANCH, len(JOBS)):
                blk, _, part = JOBS[n]
                name = BLOCKS[blk]
                c = BC // 128 * int(name[-1]) + part
                ga, gb = (t[:, c, :].rearrange("p (a b) -> p a b", a=2) for t in (gaT, gbT))
                v.wait_ge(pj_done, n + 1)
                half = PJ[:, n % 2, :, 0:HALF]
                if name[:-1] == "bra":
                    v.tensor_tensor(ga, ga, half, ALU.mult).then_inc(pj_dve, 1)
                    if n == BEFORE_BRANCH:
                        v.wait_ge(yb_hi_ok, 1)
                    v.tensor_tensor(yb_lo[:, c, :], rT[:, c, :], yb_hi[:, c, :], ALU.subtract).then_inc(yb_lo_ok, 1)
                else:
                    v.wait_ge(pj_dve, n - BEFORE_BRANCH)
                    link(v.tensor_tensor(gb, gb, half, ALU.mult))
                    v.tensor_tensor(ga, ga, gb, ALU.add).then_inc(pj_dve, 1)

            def scaled_add(dst, src):
                p = dst.shape[0]
                chain[0] += 1
                v.scalar_tensor_tensor(out=dst.rearrange("p (a b) -> p a b", a=2),
                                       in0=dst.rearrange("p (a b) -> p a b", a=2), scalar=ALPHA, in1=src[0:p],
                                       op0=ALU.mult, op1=ALU.add).then_inc(dve_chain, 1)
                v.wait_ge(dve_chain, chain[0])
                v.sem_inc(y_read, 1)

            def top16(vals16, inds16, src):
                link(v.max(vals16[:, 0:8], src))
                link(v.max_index(inds16[:, 0:8], vals16[:, 0:8], src))
                link(v.match_replace(src, vals16[:, 0:8], src, NEG))
                link(v.max(vals16[:, 8:16], src))
                link(v.max_index(inds16[:, 8:16], vals16[:, 8:16], src))

            def route(j, h, part):
                p, r = rows(j), ROUTE[j, h]
                if part == 0:
                    v.wait_ge(q_done, r + 1)
                    v.bn_stats(bn[0:p, 0, :], RQ[0:p, 0:128])
                    link(v.bn_stats(bn[0:p, 1, :], RQ[0:p, 128:256]))
                    v.bn_aggr(mv[0:p, 0, :], bn[0:p, 0, :])
                    link(v.bn_aggr(mv[0:p, 1, :], bn[0:p, 1, :]))
                    v.tensor_scalar(mv[0:p, :, 1:2], mv[0:p, :, 1:2], EPS, None, ALU.add).then_inc(var_ok, 1)
                elif part == 1:
                    link(inverse(("route", j, h), p, 2))
                    for i in range(2):
                        last = v.tensor_scalar(qN[0:p, i, :], RQ[0:p, 128 * i:128 * i + 128], mv[0:p, i, 0:1],
                                               rstd[0:p, i:i + 1], ALU.subtract, ALU.mult)
                        last.then_inc(qn_ok, 1)
                elif part == 2:
                    v.wait_ge(s_done, r + 1)
                    v.tensor_copy(scores[0:p], RQ[0:p, 256:512].rearrange("p (a b) -> p a b", a=2)).then_inc(rq_read, 1)
                    v.wait_ge(rq_read, r + 1)
                    top16(vals[0:p, 0, :], inds[0:p, 0, :], scores[0:p, 0, :])
                elif part == 3:
                    top16(vals[0:p, 1, :], inds[0:p, 1, :], scores[0:p, 1, :])
                    v.tensor_copy(indf[0:p], inds[0:p])
                elif part == 4:
                    link(v.tensor_tensor(cand[0:p].rearrange("p (a b) -> p a b", a=TOPK),
                                         vals[0:p, 0, :].unsqueeze(2).broadcast_to([p, TOPK, TOPK]),
                                         vals[0:p, 1, :].unsqueeze(1).broadcast_to([p, TOPK, TOPK]), ALU.add))
                    top16(top[0:p], topi[0:p], cand[0:p])
                    link(v.tensor_scalar(soft[0:p, 0:1], top[0:p, 0:1], -1.0, None, ALU.mult))
                    v.sem_inc(exp_in, 1)
                elif part == 5:
                    v.tensor_scalar(abu[0:p, 0, :], topi[0:p], 4, None, ALU.logical_shift_right)
                    link(v.tensor_scalar(abu[0:p, 1, :], topi[0:p], 15, None, ALU.bitwise_and))
                    link(v.tensor_copy(abf[0:p], abu[0:p]))
                    link(v.tensor_tensor(onehot[0:p], abf[0:p].unsqueeze(3).broadcast_to([p, 2, TOPK, TOPK]),
                                         iota16[0:p].unsqueeze(1).unsqueeze(1).broadcast_to([p, 2, TOPK, TOPK]),
                                         ALU.is_equal))
                    link(v.tensor_tensor(onehot[0:p], onehot[0:p],
                                         indf[0:p].unsqueeze(2).broadcast_to([p, 2, TOPK, TOPK]), ALU.mult))
                    link(v.tensor_reduce(e12[0:p], onehot[0:p], AX.X, ALU.add))
                else:
                    s = slice(h * TOPK, (h + 1) * TOPK)
                    v.wait_ge(exp_ok, r + 1)
                    link(v.reciprocal(soft[0:p, 2:3], soft[0:p, 1:2]))
                    m = (j * PH + h) % AHEAD
                    gate_out, idx_out = (gates[:, m, :], idx[:, m, :]) if j < NT else (gatesS[:, s], idxf[:, s])
                    v.tensor_scalar(gate_out[0:p], ex[0:p, :], soft[0:p, 2:3], None, ALU.mult)
                    link(v.scalar_tensor_tensor(out=idx_out[0:p], in0=e12[0:p, 0, :], scalar=float(NK),
                                                in1=e12[0:p, 1, :], op0=ALU.mult, op1=ALU.add))
                    v.sem_inc(route_ok, 1)

            def dots(n, ks):
                for k in ks:
                    m = u_number(n, k)
                    v.wait_ge(u_in[m % UB], 16 * (m // UB + 1))
                    t = ubuf[m % UB]
                    last = v.tensor_tensor_reduce(out=t, in0=t, in1=x1[:, n // PH, :], scale=1.0, scalar=0.0,
                                                  op0=ALU.mult, op1=ALU.add, accum_out=hraw[:, n % 2, k:k + 1])
                    last.then_inc(u_used, 1)
                if TOPK - 1 in ks:
                    v.wait_ge(u_used, u_number(n, TOPK - 1) + 1)
                    v.sem_inc(h_ok, 1)

            def weights(n):
                if n >= 3:
                    v.wait_ge(diag_ok, (n - 2) * TOPK)
                v.wait_ge(g_ok, n + 1)
                v.tensor_tensor(wgt[:, n % 3, :], hact[:, n % 2, :], gates[:, n % AHEAD, :], ALU.mult).then_inc(
                    w_ok, 1)

            def sample_dot(b):
                m = U_SAMPLE + b
                v.wait_ge(u_in[m % UB], 16 * (m // UB + 1))
                v.wait_ge(xb_done, b + 1)
                t = ubuf[m % UB].rearrange("p (a b) -> p a b", a=2)
                v.tensor_tensor_reduce(out=t, in0=t, in1=sample_x1[b % 2], scale=1.0, scalar=0.0, op0=ALU.mult, op1=ALU.add,
                                       accum_out=hS[:, b:b + 1]).then_inc(u_used, 1)
                if b == S - 1:
                    v.wait_ge(u_used, U_SAMPLE + S)
                    v.sem_inc(hs_ok, 1)

            def sample_weights():
                v.wait_ge(gs_ok, 1)
                v.wait_ge(it_ok, 2)
                v.tensor_tensor(wpad[:, :, :].rearrange("p a b -> p (a b)")[:, 0:S * S:S + 1], aS[:, :], gateT[:, :],
                                ALU.mult).then_inc(wpad_ok, 1)

            def residual_norm(what, j, part):
                p = rows(j)
                t = x1[0:p, j, :]
                g, b, done = (ln1g, ln1b, x1_ok) if what == "x1" else (ln2g, ln2b, x2_ok)
                if part == 0:
                    if what == "x1":
                        v.wait_ge(ln1_in, 32)
                        v.wait_ge(xr_in[j], 16)
                        v.wait_ge(w_done, WIDE["wo", j] + 1)
                        scaled_add(t, W)
                    else:
                        v.wait_ge(ln2_in, 32)
                        if j < NT:
                            v.wait_ge(y_done, j + 1)
                            scaled_add(t, Y)
                        else:
                            v.wait_ge(ys_done, 1)
                            scaled_add(t, W)
                    row_stats(t, p)
                elif part == 1:
                    link(inverse((what, j), p, 1))
                    link(v.tensor_scalar(t, t, mv[0:p, 0, 0:1], rstd[0:p, 0:1], ALU.subtract, ALU.mult))
                elif part == 2:
                    link(v.tensor_tensor(t, t, g[0:p], ALU.mult))
                else:
                    v.tensor_tensor(t, t, b[0:p], ALU.add).then_inc(done, 1)

            for e in PLAN:
                what, args = e[0], e[1:]
                if what in ("x1", "x2"):
                    residual_norm(*e)
                elif what == "route":
                    route(*args)
                elif what == "dots":
                    dots(args[0], range(args[1], args[2]))
                elif what == "weights":
                    weights(args[0])
                elif what == "pe":
                    j = args[0]
                    p = rows(j)
                    v.wait_ge(g_done, X2[j] + 1)
                    v.wait_ge(w_done, WIDE[e[:2]] + 1)
                    s2 = sg[0:p, :].rearrange("p (a b) -> p a b", a=2)
                    link(v.tensor_tensor(s2, s2, (Y if j == NT - 1 else W)[0:p], ALU.mult))
                    v.tensor_tensor(x1[0:p, j, :], x1[0:p, j, :], sg[0:p, :], ALU.add).then_inc(x3_ok, 1)
                elif what == "samples":
                    v.wait_ge(it_done, 2)
                    v.tensor_copy(idxT[:, :], X[0][:, 0:S]).then_inc(it_ok, 1)
                elif what == "sample dot":
                    sample_dot(*args)
                elif what == "sample sums":
                    sample_weights()

        @block.tensor
        def _(pe):
            mm = nc.tensor.matmul

            def project(n):
                blk, kind, part = JOBS[n]
                if n >= 2:
                    if n - 2 < BEFORE_BRANCH:
                        pe.wait_ge(pj_act, n - 1)
                    else:
                        pe.wait_ge(pj_dve, n - 1 - BEFORE_BRANCH)
                out = PJ[:, n % 2, :, :]
                if kind == "decay":
                    pe.wait_ge(pj_act, 1)
                    pe.wait_ge(small_in, 32)
                    for s in range(2):
                        last = mm(out[:, s, 0:HALF], wgk[:, part * DK:(part + 1) * DK], gkl[:, s * HALF:(s + 1) * HALF],
                                  start=True, stop=True)
                    last.then_inc(pj_done, 1)
                    return
                if kind == "low":
                    pe.wait_ge(gl_ok, 1)
                    wh, wl = gl_hi, gl_lo
                else:
                    pe.wait_ge(split_ok, blk + 1)
                    wh, wl = w_hi[blk % RING], w_lo[blk % RING]
                name = BLOCKS[blk][:-1] if blk is not None else ""
                if name == "bra":
                    pe.wait_ge(ya_lo_ok, 1)
                    xh, xl = ya_hi, ya_lo
                elif name == "brb":
                    pe.wait_ge(yb_lo_ok, KC)
                    xh, xl = yb_hi, yb_lo
                elif name in ("ga", "gb"):
                    pe.wait_ge(x2_lo_ok, 2)
                    xh, xl = x_hi, x_lo[1]
                else:
                    xh, xl = x_hi, x_lo[0]
                for c in range(KC):
                    if kind == "low" and c % 2 == 0:
                        pe.wait_ge(x_ok, 1 + c // 2)
                    for i, (w, x) in enumerate(((wh, xh), (wh, xl), (wl, xh))):
                        start, stop = c == 0 and i == 0, c == KC - 1 and i == 2
                        if kind == "natural":
                            p = rows(part)
                            last = mm(out[0:p, 0, 0:BC], x[:, c, cols(part)], w[:, c, :], start=start, stop=stop)
                            continue
                        m = slice(0, RANK) if kind == "low" else slice(part * 128, (part + 1) * 128)
                        for s in range(2):
                            last = mm(out[0:m.stop - m.start, s, 0:HALF], w[:, c, m], x[:, c, s * HALF:(s + 1) * HALF],
                                      start=start, stop=stop)
                last.then_inc(pj_done, 1)

            for n in range(BEFORE_GATES):
                project(n)

            pe.wait_ge(const_ok, 6)
            for j in range(NT + 1):
                p = rows(j)
                pe.wait_ge(vn_ok, j + 1)
                if j >= 2:
                    pe.wait_ge(ya_ok, j - 1)
                z = X[j % 2][:, 0:G * p].rearrange("p (a b) -> p a b", a=G)
                for g in range(G):
                    w = wsT[:, g, :] if j < NT else dg[:, g, :]
                    b = bsrow[:, g * 128:(g + 1) * 128] if j < NT else bs0[:, g, :]
                    mm(z[:, g, :], vaN[0:p, j, g * 128:(g + 1) * 128], w, start=True, stop=False)
                    last = mm(z[:, g, :], ones[0:1, :], b, start=False, stop=True)
                last.then_inc(z_done, 1)

            def turn_output(j):
                p = rows(j)
                pe.wait_ge(on_ok, j + 1)
                pe.wait_ge(pj_act, BEFORE_GATES)
                if j >= 2:
                    pe.wait_ge(yb_ok, j - 1)
                if j == NT:
                    pe.wait_ge(pj_act, EARLY_GATES)
                for c in range(KC):
                    last = nc.tensor.transpose(PJ[:, j % 2, c // 4, (c % 4) * 128:(c % 4) * 128 + p],
                                               oN[0:p, c // 2, (c % 2) * 128:(c % 2 + 1) * 128], ident[0:p, 0:p])
                last.then_inc(ot_done, 1)

            pe.wait_ge(ya_ok, NT + 1)
            for j in range(NT):
                pe.wait_ge(qk_ok, j + 1)
                if j:
                    pe.wait_ge(s_ok, j)
                for h in range(H):
                    mm(X[0][:, h * 128:(h + 1) * 128], qkT[:, H + h, cols(j)], qkT[:, h, cols(j)], start=True, stop=True)
                for h in range(H):
                    last = nc.tensor.transpose(X[0][:, 512 + h * 128:640 + h * 128], qkT[:, H + h, cols(j)], ident[:, :])
                last.then_inc(att_done, 1)
                if j:
                    turn_output(j - 1)
                pe.wait_ge(att_ok, j + 1)
                for h in range(H):
                    o_h = X[1][:, h * DV:(h + 1) * DV]
                    last = mm(o_h, attS[:, h, :], vN[:, j, h * DV:(h + 1) * DV], start=True, stop=j == 0)
                    if j:
                        last = mm(o_h, qkT[:, h, cols(j)], Sst[:, h, :], start=False, stop=True)
                last.then_inc(o_done, 1)
                pe.wait_ge(knat_ok, j + 1)
                for h in range(H):
                    last = mm(X[0][:, h * DV:(h + 1) * DV], knat[:, h, :], vN[:, j, h * DV:(h + 1) * DV],
                              start=True, stop=True)
                last.then_inc(kv_done, 1)
            pe.wait_ge(s_ok, NT)
            for h in range(H):
                last = nc.tensor.transpose(X[0][0:S, h * 128:(h + 1) * 128], qkT[:, H + h, T:N], ident[:, :])
            last.then_inc(att_done, 1)
            turn_output(NT - 1)
            pe.wait_ge(knat_ok, NT + 1)
            for h in range(H):
                pe.wait_ge(kpad_ok, 2 * h + 2)
                for b in range(S):
                    if b % 2 == 0 and 8 * h + b > 2:
                        pe.wait_ge(s0_new, 8 * h + b - 2)
                    last = mm(X[0][:, (b % 4) * DV:(b % 4 + 1) * DV], kpad[0:S, b, :], vN[0:S, NT, h * DV:(h + 1) * DV],
                              start=True, stop=True)
                    if b % 2 == 1:
                        last.then_inc(outer_done, 1)
                if h == 1:
                    pe.wait_ge(yb_ok, NT)
                if h:
                    project(BEFORE_GATES + 2 * h - 2)
                pe.wait_ge(s0_new, 8 * h + 8)
                for b in range(S):
                    last = mm(X[1][0:S, h * DV:(h + 1) * DV], qpad[:, b, :], S0[h % 2][:, b, :],
                              start=b == 0, stop=b == S - 1)
                last.then_inc(os_done, 1)
                if h:
                    project(BEFORE_GATES + 2 * h - 1)
            pe.wait_ge(os_done, H)
            pe.sem_inc(o_done, 1)
            turn_output(NT)
            pe.wait_ge(yb_ok, NT + 1)
            for n in range(EARLY_GATES, len(JOBS)):
                project(n)

            def wide(what, j, part):
                p = rows(j)
                if what == "wo":
                    if part == 0 and X1[j]:
                        pe.wait_ge(y_read, READ["x1", list(X1)[X1[j] - 1]] + 1)
                    lhs = [gaT[:, c, cols(j)] for c in range(KC)]
                    rhs = [[w_wide[s][:, c, :] for c in range(KC)] for s in range(2)]
                elif what == "pg":
                    if part == 0:
                        pe.wait_ge(y_read, READ["x1", LAST_X1] + 1)
                        if j == NT:
                            pe.wait_ge(y_read, READ["x2", NT] + 1)
                        if X2[j]:
                            pe.wait_ge(x3_ok, X2[j])
                        pe.wait_ge(x1t_ok, TURN["x2", j] + 1)
                        pe.wait_ge(wpg_in, 32)
                    lhs = [x2T[:, c, 0:p] for c in range(KC)]
                    rhs = [[w_wide[s][:, c, :] for c in range(KC)] for s in range(2)]
                else:
                    if j == NT - 1:
                        pe.wait_ge(y_read, READ["x2", j] + 1)
                    else:
                        pe.wait_ge(g_done, X2[j] + 1)
                    pe.wait_ge(wpe_in, 16)
                    pe.wait_ge(pt_in, 16 * (X2[j] + 1))
                    lhs = [pT[:, c, 0:p] for c in range(2)]
                    rhs = [[wpe[:, c, 512 * s:512 * s + 512] for c in range(2)] for s in range(2)]
                chunks = range(2) if what == "pe" else range(2 * part, 2 * part + 2)
                for c in chunks:
                    for s in range(2):
                        last = mm((Y if (what, j) == ("pe", NT - 1) else W)[0:p, s, :], lhs[c], rhs[s][c], start=c == 0, stop=c == len(lhs) - 1)
                if part == 3:
                    last.then_inc(w_done, 1)

            def turn(what, j):
                p = rows(j)
                if what == "x1":
                    pe.wait_ge(x1_ok, X1[j] + 1)
                else:
                    pe.wait_ge(x2_ok, X2[j] + 1)
                if TURN[what, j]:
                    pe.wait_ge(x1t_ok, TURN[what, j])
                if (what, j) == ("x2", NT):
                    pe.wait_ge(u_used, U_SAMPLE + S)
                for c in range(KC):
                    last = nc.tensor.transpose(X[0][:, c * 128:c * 128 + p], x1[0:p, j, c * 128:(c + 1) * 128],
                                               ident[0:p, 0:p])
                last.then_inc(tr_done, 1)

            def queries(j, h):
                p, r = rows(j), ROUTE[j, h]
                pe.wait_ge(x1t_ok, TURN["x1", j] + 1)
                if r:
                    pe.wait_ge(rq_read, r)
                pe.wait_ge(wq_in[h // 2], 16)
                src = x1T if j < NT else x1Ts
                for c in range(KC):
                    last = mm(RQ[0:p, 0:256], src[:, c, 0:p], wq[h // 2][:, c, (h % 2) * 256:(h % 2 + 1) * 256],
                              start=c == 0, stop=c == KC - 1)
                last.then_inc(q_done, 1)

            def route(j, h, part):
                p, r = rows(j), ROUTE[j, h]
                if part == 1:
                    pe.wait_ge(qn_ok, 2 * r + 2)
                    for i in range(2):
                        last = nc.tensor.transpose(RT[:, i * 128:i * 128 + p], qN[0:p, i, :], ident[0:p, 0:p])
                    last.then_inc(qt_done, 1)
                elif part == 2:
                    pe.wait_ge(qt_ok, r + 1)
                    pe.wait_ge(keys_in, 16)
                    for i in range(2):
                        last = mm(RQ[0:p, 256 + i * 128:384 + i * 128], qT[:, i, 0:p], keysT[:, 2 * h + i, :],
                                  start=True, stop=True)
                    last.then_inc(s_done, 1)

            def sums(n, ks):
                for k in ks:
                    m, d = v_number(n, k), n * TOPK + k
                    first, final = d % SLOTS == 0, d % SLOTS == SLOTS - 1
                    if first and n:
                        pe.wait_ge(y_read, READ["x2", n // PH - 1] + 1)
                    pe.wait_ge(v_in[m % VB], 16 * (m // VB + 1))
                    pe.wait_ge(diag_ok, d + 1)
                    for s in range(2):
                        last = mm(Y[:, s, :], diag[d % DB], vbuf[m % VB][:, 512 * s:512 * s + 512], start=first, stop=final)
                    last.then_inc(v_used, 1)
                    if final:
                        pe.wait_ge(v_used, m + 1)
                        pe.sem_inc(y_done, 1)

            def sample_row(b):
                if b == 0:
                    pe.wait_ge(it_ok, 2)
                elif b == 1:
                    pe.wait_ge(x3_ok, NT - 1)
                else:
                    pe.wait_ge(u_used, U_SAMPLE + b - 1)
                for s in range(2):
                    last = mm(sample_x1[b % 2][:, s, :], ident[0:S, b:b + 1].broadcast_to([S, 128]),
                              x1[0:S, NT, 512 * s:512 * s + 512], start=True, stop=True)
                last.then_inc(xb_done, 1)

            def sample_sums():
                pe.wait_ge(wpad_ok, 1)
                pe.wait_ge(x3_ok, NT - 1)
                for b in range(S):
                    m = V_SAMPLE + b
                    pe.wait_ge(v_in[m % VB], 16 * (m // VB + 1))
                    for s in range(2):
                        last = mm(W[0:S, s, :], wpad[:, b, :], vbuf[m % VB][:, 512 * s:512 * s + 512],
                                  start=b == 0, stop=b == S - 1)
                    last.then_inc(v_used, 1)
                pe.wait_ge(v_used, V_SAMPLE + S)
                pe.sem_inc(ys_done, 1)

            pe.wait_ge(pj_dve, len(JOBS) - BEFORE_BRANCH)
            pe.wait_ge(wo_in, 32)
            for e in PLAN:
                what, args = e[0], e[1:]
                if what in ("wo", "pg", "pe"):
                    wide(*e)
                elif what == "turn":
                    turn(*args)
                elif what == "q":
                    queries(*args)
                elif what == "route":
                    route(*args)
                elif what == "sums":
                    sums(args[0], range(args[1], args[2]))
                elif what == "samples":
                    pe.wait_ge(route_ok, ROUTE[NT, PH - 1] + 1)
                    pe.wait_ge(x1t_ok, TURN["x2", NT - 2] + 1)
                    nc.tensor.transpose(X[0][:, 0:S], idxf, ident[0:S, 0:S]).then_inc(it_done, 1)
                    nc.tensor.transpose(X[0][:, 512:512 + S], gatesS, ident[0:S, 0:S]).then_inc(it_done, 1)
                elif what == "sample dot":
                    sample_row(*args)
                elif what == "sample sums":
                    sample_sums()


def kernel(**inputs):
    import numpy as np
    import concourse.bacc as bacc
    from concourse.bass_utils import run_bass_kernel_spmd

    a = {k: np.asarray(t) for k, t in inputs.items()}

    def chunked(w, width):
        r, c = w.shape
        return w.reshape(r // 128, 128, c // width, width).transpose(2, 1, 0, 3)

    w_in = a["w_in"][0]
    starts = {"ua": 0, "va": D, "q": 2 * D, "k": 2 * D + 512, "v": 3 * D, "r": 4 * D,
              "ga": 5 * D + RANK, "gb": 6 * D + RANK}
    blocks = []
    for name in BLOCKS:
        kind, i = name[:-1], int(name[-1])
        if kind == "bra":
            src, c = a["w_br_a"][0], BC * i
        elif kind == "brb":
            src, c = a["w_br_b"][0], BC * i
        else:
            src, c = w_in, starts[kind] + BC * i
        blocks.append(chunked(src[:, c:c + BC], BC)[0])
    x_all = np.concatenate([a["x_prompt"][0], a["x_sample"][:, 0]])
    p_all = np.concatenate([a["p_prompt"][0, 0], a["p_sample"][0, :, 0]])
    ins = {
        "x_all": x_all,
        "x_t": x_all.T.reshape(KC, 128, N).transpose(1, 0, 2),
        "state": a["state_gla"][0].transpose(1, 2, 0, 3),
        "p_t": p_all.T.reshape(2, 128, N).transpose(1, 0, 2),
        "w_blk": np.stack(blocks),
        "w_gkl": chunked(w_in[:, 5 * D:5 * D + RANK], RANK)[0],
        "w_gk": a["w_gk"][0],
        "b_gk": a["b_gk"][0].reshape(H, DK).T,
        "ws_t": a["w_s"][0].transpose(2, 0, 1),
        "ws0": a["w_s"][0][:, 0, 0],
        "b_s": a["b_s"][0].reshape(1, G * 128),
        "lnv_g": a["ln_v_g"][0], "lnv_b": a["ln_v_b"][0],
        "gn_g": a["gla_norm_g"][0].reshape(2, 128).T,
        "w_o": chunked(a["w_o"][0], 512),
        "ln1_g": a["ln1_g"][0], "ln1_b": a["ln1_b"][0],
        "w_q": chunked(a["peer_wq"][0], 512),
        "keys_t": a["peer_keys"][0].reshape(2 * PH, NK, 128).transpose(2, 0, 1),
        "u_tab": a["peer_u"][0], "v_tab": a["peer_v"][0],
        "ln2_g": a["ln2_g"][0], "ln2_b": a["ln2_b"][0],
        "w_pe": a["w_pe"][0].reshape(2, 128, D).transpose(1, 0, 2),
        "w_pg": chunked(a["w_pg"][0], 512),
    }
    outs = {"y_all": (N, D), "st_p": (DK, H, DV), "st_s": (H, DK, S, DV), "cv_p": (128, D), "cv_s": (S, D)}
    nc = bacc.Bacc("TRN2", target_bir_lowering=False, num_devices=1)
    arrays, aps = {}, []
    for name, t in ins.items():
        arrays[f"in_{name}"] = np.ascontiguousarray(t)
        aps.append(nc.dram_tensor(f"in_{name}", t.shape, F32, kind="ExternalInput").ap())
    for name, shape in outs.items():
        aps.append(nc.dram_tensor(f"out_{name}", shape, F32, kind="ExternalOutput").ap())
    decoder_step(nc, *aps)
    r = run_bass_kernel_spmd(nc, [arrays], core_ids=[0]).results[0]
    y = r["out_y_all"]
    return (y[:T].reshape(1, T, D), y[T:].reshape(S, 1, D),
            r["out_st_p"].transpose(1, 0, 2).reshape(1, 1, H, DK, DV),
            r["out_st_s"].transpose(2, 0, 1, 3).reshape(1, S, H, DK, DV),
            r["out_cv_p"].reshape(1, 1, 128, D), r["out_cv_s"].reshape(1, S, 1, D))
```
